# Optimizing a Trainium2 kernel written in Bass

```python
import math
import jax, jax.numpy as jnp
from jax import lax
import numpy as np

D_MODEL = 1024
BATCH = 1
SEQ = 256
DEPTH = 2

PLE_DIM = 256
HEAD_DIM = 64
DIFF_HEADS = 4
DSA_HEADS = 8
IDX_HEADS = 8
IDX_DIM = 64
TOPK_MAX = 256
N_GROUPS = 4
EXPERTS_PER_GROUP = 8
TOP_K_IN_GROUP = 2
D_EXPERT = 256
ROPE_THETA = 500000.0
ROT_DIM = HEAD_DIM // 4
Q_BLOCK = 128
LN_EPS = 1e-5
NEG_INF = -1e30
ALPHA = (2 * DEPTH) ** 0.25
BETA = (8 * DEPTH) ** -0.25
DIFF_WIDTH = DIFF_HEADS * 2 * HEAD_DIM
DSA_WIDTH = DSA_HEADS * HEAD_DIM
SPLIT_SIZES = (DIFF_WIDTH, DIFF_WIDTH, DIFF_WIDTH, DSA_WIDTH, DSA_WIDTH, DSA_WIDTH,
               IDX_HEADS * IDX_DIM, IDX_DIM, IDX_HEADS, D_MODEL, D_MODEL)
W_IN_COLS = sum(SPLIT_SIZES)


def layer_norm(x, g, b):
    xf = x.astype(jnp.float32)
    mu = jnp.mean(xf, axis=-1, keepdims=True)
    var = jnp.mean(jnp.square(xf - mu), axis=-1, keepdims=True)
    y = (xf - mu) * lax.rsqrt(var + LN_EPS)
    return (y * g.astype(jnp.float32) + b.astype(jnp.float32)).astype(x.dtype)

def rms_norm(x, g):
    xf = x.astype(jnp.float32)
    y = xf * lax.rsqrt(jnp.mean(jnp.square(xf), axis=-1, keepdims=True) + LN_EPS)
    return (y * g.astype(jnp.float32)).astype(x.dtype)

def rope_tables(positions):
    inv_freq = 1.0 / (ROPE_THETA ** (jnp.arange(0, ROT_DIM, 2, dtype=jnp.float32) / ROT_DIM))
    ang = positions.astype(jnp.float32)[..., None] * inv_freq
    return jnp.cos(ang), jnp.sin(ang)

def partial_rope(t, cos, sin):
    half = ROT_DIM // 2
    shp = cos.shape[:2] + (1,) * (t.ndim - 3) + (half,)
    c = cos.reshape(shp).astype(t.dtype)
    s = sin.reshape(shp).astype(t.dtype)
    x1 = t[..., :half]
    x2 = t[..., half:ROT_DIM]
    return jnp.concatenate([x1 * c - x2 * s, x2 * c + x1 * s, t[..., ROT_DIM:]], axis=-1)

def diff_attention(q, k, v, lam):
    B, S, H, _, dk = q.shape
    nb = S // Q_BLOCK
    scale = dk ** -0.5
    qb = q.reshape(B, nb, Q_BLOCK, H, 2, dk).swapaxes(0, 1)
    key_pos = jnp.arange(S)

    def one_block(args):
        q_i, b_i = args
        q_pos = b_i * Q_BLOCK + jnp.arange(Q_BLOCK)
        s = jnp.einsum('bqhcd,bkhcd->bhcqk', q_i, k).astype(jnp.float32) * scale
        s = jnp.where(key_pos[None, :] <= q_pos[:, None], s, NEG_INF)
        pr = jax.nn.softmax(s, axis=-1)
        a = pr[:, :, 0] - lam * pr[:, :, 1]
        return jnp.einsum('bhqk,bkhe->bqhe', a.astype(v.dtype), v)

    o = lax.map(one_block, (qb, jnp.arange(nb)))
    return o.swapaxes(0, 1).reshape(B, S, H, v.shape[-1])

def dsa_attention(q, k, v, q_idx, k_idx, w_idx, topk):
    B, S, H, dh = q.shape
    nb = S // Q_BLOCK
    scale = dh ** -0.5
    to_blocks = lambda t: t.reshape((B, nb, Q_BLOCK) + t.shape[2:]).swapaxes(0, 1)
    key_pos = jnp.arange(S)

    def one_block(args):
        q_b, qi_b, wi_b, b_i = args
        q_pos = b_i * Q_BLOCK + jnp.arange(Q_BLOCK)
        dots = jnp.einsum('bqhd,bsd->bqhs', qi_b, k_idx).astype(jnp.float32) * (IDX_DIM ** -0.5)
        score = jnp.einsum('bqhs,bqh->bqs', jax.nn.relu(dots), wi_b.astype(jnp.float32))
        score = jnp.where(key_pos[None, None, :] <= q_pos[None, :, None], score, NEG_INF)
        _, sel = lax.top_k(score, topk)
        valid = sel <= q_pos[None, :, None]
        kg = jax.vmap(lambda kb, ib: kb[ib])(k, sel)
        vg = jax.vmap(lambda vb, ib: vb[ib])(v, sel)
        s = jnp.einsum('bqhd,bqkhd->bhqk', q_b, kg).astype(jnp.float32) * scale
        s = jnp.where(valid[:, None], s, NEG_INF)
        pr = jax.nn.softmax(s, axis=-1)
        return jnp.einsum('bhqk,bqkhd->bqhd', pr.astype(v.dtype), vg)

    o = lax.map(one_block, (to_blocks(q), to_blocks(q_idx), to_blocks(w_idx), jnp.arange(nb)))
    return o.swapaxes(0, 1).reshape(B, S, H * dh)

def token_mixers(x, cos, sin, w_in, lam_params, subln_g, w_bd, w_bs, w_o, lam_init):
    B, S, _ = x.shape
    h = x @ w_in
    points = [int(c) for c in np.cumsum(SPLIT_SIZES)[:-1]]
    dq, dkk, dv, sq, sk, sv, iq, ik, iw, ga, gb = jnp.split(h, points, axis=-1)

    dq = partial_rope(dq.reshape(B, S, DIFF_HEADS, 2, HEAD_DIM), cos, sin)
    dkk = partial_rope(dkk.reshape(B, S, DIFF_HEADS, 2, HEAD_DIM), cos, sin)
    dv = dv.reshape(B, S, DIFF_HEADS, 2 * HEAD_DIM)
    lp = lam_params.astype(jnp.float32)
    lam = jnp.exp(jnp.sum(lp[0] * lp[1])) - jnp.exp(jnp.sum(lp[2] * lp[3])) + lam_init
    ya = diff_attention(dq, dkk, dv, lam)
    ya = (rms_norm(ya, subln_g) * (1.0 - lam_init)).reshape(B, S, DIFF_WIDTH)

    sq = partial_rope(sq.reshape(B, S, DSA_HEADS, HEAD_DIM), cos, sin)
    sk = partial_rope(sk.reshape(B, S, DSA_HEADS, HEAD_DIM), cos, sin)
    sv = sv.reshape(B, S, DSA_HEADS, HEAD_DIM)
    iq = partial_rope(iq.reshape(B, S, IDX_HEADS, IDX_DIM), cos, sin)
    ik = partial_rope(ik, cos, sin)
    iw = iw * (IDX_HEADS ** -0.5)
    topk = min(TOPK_MAX, S // 4)
    yb = dsa_attention(sq, sk, sv, iq, ik, iw, topk)

    merged = jax.nn.sigmoid(ga) * (ya @ w_bd) + jax.nn.sigmoid(gb) * (yb @ w_bs)
    return merged @ w_o

def hierarchical_moe(x, w_rg, b_rg, w_re, b_re, w_g, w_u, w_d):
    B, S, D = x.shape
    xt = x.reshape(-1, D)
    n = xt.shape[0]
    g_prob = jax.nn.softmax((xt @ w_rg).astype(jnp.float32) + b_rg.astype(jnp.float32), axis=-1)
    g_val, g_idx = lax.top_k(g_prob, 1)
    e_logit = ((xt @ w_re).astype(jnp.float32) + b_re.astype(jnp.float32)).reshape(n, N_GROUPS, EXPERTS_PER_GROUP)
    e_logit = jnp.take_along_axis(e_logit, g_idx[:, :, None], axis=1)[:, 0]
    e_prob = jax.nn.softmax(e_logit, axis=-1)
    e_val, e_idx = lax.top_k(e_prob, TOP_K_IN_GROUP)
    e_val = e_val / jnp.sum(e_val, axis=-1, keepdims=True)
    within = jnp.sum(jax.nn.one_hot(e_idx, EXPERTS_PER_GROUP, dtype=jnp.float32) * e_val[..., None], axis=1)
    comb = jax.nn.one_hot(g_idx[:, 0], N_GROUPS, dtype=jnp.float32)[:, :, None] * (g_val * within)[:, None, :]
    y = jnp.zeros_like(xt)
    for g in range(N_GROUPS):
        hg = jax.nn.silu(jnp.einsum('nd,edf->nef', xt, w_g[g])) * jnp.einsum('nd,edf->nef', xt, w_u[g])
        y = y + jnp.einsum('nef,efd->nd', hg * comb[:, g, :, None].astype(hg.dtype), w_d[g])
    return y.reshape(B, S, D)

def first_inputs(seed: int = 0) -> dict:
    key = jax.random.key(seed)
    ks = jax.random.split(key, 24)
    L, D = DEPTH, D_MODEL
    G, E, F = N_GROUPS, EXPERTS_PER_GROUP, D_EXPERT
    nrm = lambda k, shape, scale: jax.random.normal(k, shape, jnp.float32) * scale
    return {
        'x': nrm(ks[0], (BATCH, SEQ, D), 1.0),
        'p': nrm(ks[1], (L, BATCH, SEQ, PLE_DIM), 1.0),
        'positions': jnp.broadcast_to(jnp.arange(SEQ, dtype=jnp.int32), (BATCH, SEQ)),
        'w_in': nrm(ks[2], (L, D, W_IN_COLS), D ** -0.5),
        'diff_lambda': nrm(ks[3], (L, 4, HEAD_DIM), 0.1),
        'diff_subln_g': 1.0 + nrm(ks[4], (L, 2 * HEAD_DIM), 0.01),
        'w_branch_diff': nrm(ks[5], (L, DIFF_WIDTH, D), DIFF_WIDTH ** -0.5),
        'w_branch_dsa': nrm(ks[6], (L, DSA_WIDTH, D), DSA_WIDTH ** -0.5),
        'w_out': nrm(ks[7], (L, D, D), BETA * D ** -0.5),
        'ln1_g': 1.0 + nrm(ks[8], (L, D), 0.01),
        'ln1_b': nrm(ks[9], (L, D), 0.01),
        'w_route_group': nrm(ks[10], (L, D, G), D ** -0.5),
        'b_route_group': nrm(ks[11], (L, G), 0.01),
        'w_route_expert': nrm(ks[12], (L, D, G * E), D ** -0.5),
        'b_route_expert': nrm(ks[13], (L, G * E), 0.01),
        'w_exp_gate': nrm(ks[14], (L, G, E, D, F), D ** -0.5),
        'w_exp_up': nrm(ks[15], (L, G, E, D, F), D ** -0.5),
        'w_exp_down': nrm(ks[16], (L, G, E, F, D), BETA * F ** -0.5),
        'w_ple': nrm(ks[17], (L, PLE_DIM, D), BETA * PLE_DIM ** -0.5),
        'w_ple_gate': nrm(ks[18], (L, D, D), D ** -0.5),
        'ln2_g': 1.0 + nrm(ks[19], (L, D), 0.01),
        'ln2_b': nrm(ks[20], (L, D), 0.01),
    }

def first_block(x, p, positions, w_in, diff_lambda, diff_subln_g, w_branch_diff, w_branch_dsa,
              w_out, ln1_g, ln1_b, w_route_group, b_route_group, w_route_expert, b_route_expert,
              w_exp_gate, w_exp_up, w_exp_down, w_ple, w_ple_gate, ln2_g, ln2_b):
    cos, sin = rope_tables(positions)
    for i in range(DEPTH):
        lam_init = 0.8 - 0.6 * math.exp(-0.3 * i)
        mix = token_mixers(x, cos, sin, w_in[i], diff_lambda[i], diff_subln_g[i],
                           w_branch_diff[i], w_branch_dsa[i], w_out[i], lam_init)
        x = layer_norm(ALPHA * x + mix, ln1_g[i], ln1_b[i])
        ffn = hierarchical_moe(x, w_route_group[i], b_route_group[i], w_route_expert[i],
                               b_route_expert[i], w_exp_gate[i], w_exp_up[i], w_exp_down[i])
        ple = jax.nn.sigmoid(x @ w_ple_gate[i]) * (p[i] @ w_ple[i])
        x = layer_norm(ALPHA * x + ffn + ple, ln2_g[i], ln2_b[i])
    return x


MLA_HEADS = 8
MLA_Q_RANK = 256
MLA_KV_RANK = 128
MLA_NOPE = 64
MLA_ROPE = 32
MLA_V = 64
MOBA_HEADS = 8
MOBA_HEAD_DIM = 64
MOBA_BLOCK = 256
MOBA_TOPK = 3
MOBA_Q_CHUNK = 32
RET_HEADS = 4
RET_QK_DIM = 64
RET_V_DIM = 128
RET_CHUNK = 128
RET_THETA = 10000.0
PARTIAL_ROPE_DIV = 4
ATTN_Q_BLOCK = 128
D_FF = 4 * D_MODEL
NORM_EPS = 1e-6
GN_EPS = 1e-5
NEG_INF_2 = -1e30

MOBA_W = MOBA_HEADS * MOBA_HEAD_DIM
RET_QK_W = RET_HEADS * RET_QK_DIM
RET_V_W = RET_HEADS * RET_V_DIM
MLA_OUT_W = MLA_HEADS * MLA_V
IN_SPLIT_SIZES = (MLA_Q_RANK, MLA_KV_RANK, MLA_ROPE,
                  MOBA_W, MOBA_W, MOBA_W,
                  RET_QK_W, RET_QK_W, RET_V_W, RET_V_W,
                  D_MODEL, D_MODEL, D_MODEL)
IN_COLS = sum(IN_SPLIT_SIZES)
IN_SPLIT_IDX = tuple(int(i) for i in np.cumsum(IN_SPLIT_SIZES)[:-1])


def rms_norm_2(x, g, eps=NORM_EPS):
    xf = x.astype(jnp.float32)
    y = xf * lax.rsqrt(jnp.mean(xf * xf, axis=-1, keepdims=True) + eps)
    return (y * g.astype(jnp.float32)).astype(x.dtype)

def rope_tables_2(seq, dim, theta):
    inv = 1.0 / (theta ** (jnp.arange(0, dim, 2, dtype=jnp.float32) / dim))
    ang = jnp.arange(seq, dtype=jnp.float32)[:, None] * inv[None, :]
    return jnp.cos(ang), jnp.sin(ang)

def apply_rope(x, cos, sin):
    half = x.shape[-1] // 2
    x1, x2 = x[..., :half], x[..., half:]
    c, s = cos.astype(x.dtype), sin.astype(x.dtype)
    return jnp.concatenate([x1 * c - x2 * s, x1 * s + x2 * c], axis=-1)

def causal_attention(q, k, v, scale):
    B, H, S, _ = q.shape
    kpos = jnp.arange(S)

    def block(i):
        start = i * ATTN_Q_BLOCK
        qb = lax.dynamic_slice_in_dim(q, start, ATTN_Q_BLOCK, axis=2)
        s = jnp.einsum('bhqd,bhkd->bhqk', qb, k).astype(jnp.float32) * scale
        qpos = start + jnp.arange(ATTN_Q_BLOCK)
        s = jnp.where(kpos[None, :] <= qpos[:, None], s, NEG_INF_2)
        p = jax.nn.softmax(s, axis=-1).astype(v.dtype)
        return jnp.einsum('bhqk,bhkd->bhqd', p, v)

    o = lax.map(block, jnp.arange(S // ATTN_Q_BLOCK))
    return o.transpose(1, 2, 0, 3, 4).reshape(B, H, S, v.shape[-1])

def mla_branch(cq, ckv, k_rope, q_norm_g, kv_norm_g, w_q_up, w_kv_up, cos, sin):
    B, S, _ = cq.shape
    cq = rms_norm_2(cq, q_norm_g)
    ckv = rms_norm_2(ckv, kv_norm_g)
    q = (cq @ w_q_up).reshape(B, S, MLA_HEADS, MLA_NOPE + MLA_ROPE).transpose(0, 2, 1, 3)
    q = jnp.concatenate([q[..., :MLA_NOPE], apply_rope(q[..., MLA_NOPE:], cos, sin)], axis=-1)
    kv = (ckv @ w_kv_up).reshape(B, S, MLA_HEADS, MLA_NOPE + MLA_V).transpose(0, 2, 1, 3)
    k_pe = apply_rope(k_rope, cos, sin)[:, None]
    k = jnp.concatenate([kv[..., :MLA_NOPE],
                         jnp.broadcast_to(k_pe, (B, MLA_HEADS, S, MLA_ROPE))], axis=-1)
    v = kv[..., MLA_NOPE:]
    o = causal_attention(q, k, v, (MLA_NOPE + MLA_ROPE) ** -0.5)
    return o.transpose(0, 2, 1, 3).reshape(B, S, MLA_OUT_W)

def moba_branch(q, k, v, cos, sin):
    B, S, _ = q.shape
    H, Dh, BS, QC = MOBA_HEADS, MOBA_HEAD_DIM, MOBA_BLOCK, MOBA_Q_CHUNK
    rd = Dh // PARTIAL_ROPE_DIV

    def heads(t):
        return t.reshape(B, S, H, Dh).transpose(0, 2, 1, 3)

    def partial_rope(t):
        return jnp.concatenate([apply_rope(t[..., :rd], cos, sin), t[..., rd:]], axis=-1)

    q, k, v = partial_rope(heads(q)), partial_rope(heads(k)), heads(v)
    nb = -(-S // BS)
    pad = nb * BS - S
    padw = ((0, 0), (0, 0), (0, pad), (0, 0))
    q, k, v = jnp.pad(q, padw), jnp.pad(k, padw), jnp.pad(v, padw)
    kb = k.reshape(B, H, nb, BS, Dh)
    vb = v.reshape(B, H, nb, BS, Dh)
    k_mean = jnp.mean(kb.astype(jnp.float32), axis=3)
    topk = min(MOBA_TOPK, nb)
    scale = Dh ** -0.5
    bi = jnp.arange(B)[:, None, None, None]
    hi = jnp.arange(H)[None, :, None, None]

    def chunk(c):
        start = c * QC
        blk = start // BS
        qc = lax.dynamic_slice_in_dim(q, start, QC, axis=2)
        gate = jnp.einsum('bhqd,bhnd->bhqn', qc.astype(jnp.float32), k_mean)
        gate = jnp.where(jnp.arange(nb) < blk, gate, NEG_INF_2)
        _, idx = lax.top_k(gate, topk)
        sel_valid = jnp.arange(topk) < blk
        k_sel = kb[bi, hi, idx]
        v_sel = vb[bi, hi, idx]
        s_sel = jnp.einsum('bhqd,bhqnkd->bhqnk', qc, k_sel).astype(jnp.float32) * scale
        s_sel = jnp.where(sel_valid[:, None], s_sel, NEG_INF_2).reshape(B, H, QC, topk * BS)
        k_own = lax.dynamic_index_in_dim(kb, blk, axis=2, keepdims=False)
        v_own = lax.dynamic_index_in_dim(vb, blk, axis=2, keepdims=False)
        s_own = jnp.einsum('bhqd,bhkd->bhqk', qc, k_own).astype(jnp.float32) * scale
        qpos = start + jnp.arange(QC)
        kpos = blk * BS + jnp.arange(BS)
        s_own = jnp.where(kpos[None, :] <= qpos[:, None], s_own, NEG_INF_2)
        p = jax.nn.softmax(jnp.concatenate([s_sel, s_own], axis=-1), axis=-1).astype(v.dtype)
        o_sel = jnp.einsum('bhqn,bhqnd->bhqd', p[..., :topk * BS],
                           v_sel.reshape(B, H, QC, topk * BS, Dh))
        o_own = jnp.einsum('bhqk,bhkd->bhqd', p[..., topk * BS:], v_own)
        return o_sel + o_own

    o = lax.map(chunk, jnp.arange(nb * BS // QC))
    o = o.transpose(1, 2, 0, 3, 4).reshape(B, H, nb * BS, Dh)[:, :, :S]
    return o.transpose(0, 2, 1, 3).reshape(B, S, MOBA_W)

def retention_branch(q, k, v, g, gn_w, gn_b, cos, sin):
    B, S, _ = q.shape
    H, Dk, Dv, C = RET_HEADS, RET_QK_DIM, RET_V_DIM, RET_CHUNK
    nc = S // C
    f32 = jnp.float32
    q = apply_rope(q.astype(f32).reshape(B, S, H, Dk).transpose(0, 2, 1, 3), cos, sin)
    k = apply_rope(k.astype(f32).reshape(B, S, H, Dk).transpose(0, 2, 1, 3), cos, sin) * (Dk ** -0.5)
    v = v.astype(f32).reshape(B, S, H, Dv).transpose(0, 2, 1, 3)
    log_gamma = jnp.log(1.0 - 2.0 ** (-5.0 - jnp.arange(H, dtype=f32)))
    pos = jnp.arange(C, dtype=f32)
    diff = pos[:, None] - pos[None, :]
    decay_in = jnp.where(diff >= 0, jnp.exp(log_gamma[:, None, None] * diff), 0.0)
    xi = jnp.exp(log_gamma[:, None] * (pos + 1.0))
    zeta = jnp.exp(log_gamma[:, None] * (C - 1.0 - pos))
    gamma_c = jnp.exp(log_gamma * C)[None, :, None, None]
    qc = q.reshape(B, H, nc, C, Dk)
    kc = k.reshape(B, H, nc, C, Dk)
    vc = v.reshape(B, H, nc, C, Dv)
    scores = jnp.einsum('bhnid,bhnjd->bhnij', qc, kc) * decay_in[:, None]
    inner = jnp.einsum('bhnij,bhnje->bhnie', scores, vc)
    kv_chunk = jnp.einsum('bhnjd,bhnje->bhnde', kc * zeta[:, None, :, None], vc)

    def step(R, kv):
        return gamma_c * R + kv, R

    _, R_prev = lax.scan(step, jnp.zeros((B, H, Dk, Dv), f32), kv_chunk.transpose(2, 0, 1, 3, 4))
    R_prev = R_prev.transpose(1, 2, 0, 3, 4)
    cross = jnp.einsum('bhnid,bhnde->bhnie', qc * xi[:, None, :, None], R_prev)
    o = (inner + cross).reshape(B, H, S, Dv)
    mu = jnp.mean(o, axis=-1, keepdims=True)
    var = jnp.mean(jnp.square(o - mu), axis=-1, keepdims=True)
    o = (o - mu) * lax.rsqrt(var + GN_EPS)
    o = o.transpose(0, 2, 1, 3).reshape(B, S, RET_V_W) * gn_w.astype(f32) + gn_b.astype(f32)
    return jax.nn.silu(g) * o.astype(g.dtype)

def hybrid_mixer(h, w_in, mla_q_norm, mla_kv_norm, mla_w_q_up, mla_w_kv_up, ret_gn_w, ret_gn_b,
                 w_branch_mla, w_branch_moba, w_branch_ret, w_out, ropes):
    (cos_mla, sin_mla), (cos_moba, sin_moba), (cos_ret, sin_ret) = ropes
    p = h @ w_in
    (cq, ckv, k_rope, mq, mk, mv, rq, rk, rv, rg, g_mla, g_moba, g_ret) = jnp.split(p, IN_SPLIT_IDX, axis=-1)
    o_mla = mla_branch(cq, ckv, k_rope, mla_q_norm, mla_kv_norm, mla_w_q_up, mla_w_kv_up, cos_mla, sin_mla)
    o_moba = moba_branch(mq, mk, mv, cos_moba, sin_moba)
    o_ret = retention_branch(rq, rk, rv, rg, ret_gn_w, ret_gn_b, cos_ret, sin_ret)
    merged = (jax.nn.sigmoid(g_mla) * (o_mla @ w_branch_mla)
              + jax.nn.sigmoid(g_moba) * (o_moba @ w_branch_moba)
              + jax.nn.sigmoid(g_ret) * (o_ret @ w_branch_ret))
    return merged @ w_out

def squared_relu_mlp(h, w_up, w_down):
    return jnp.square(jax.nn.relu(h @ w_up)) @ w_down

def second_inputs(seed: int = 0) -> dict:
    key = jax.random.key(seed)
    ks = jax.random.split(key, 18)

    def dense(k, shape):
        return jax.random.normal(k, shape, jnp.float32) * (shape[-2] ** -0.5)

    def gain(k, shape):
        return 1.0 + 0.02 * jax.random.normal(k, shape, jnp.float32)

    L = DEPTH
    return {
        "x": jax.random.normal(ks[0], (BATCH, SEQ, D_MODEL), jnp.float32),
        "attn_norm": gain(ks[1], (L, D_MODEL)),
        "w_in": dense(ks[2], (L, D_MODEL, IN_COLS)),
        "mla_q_norm": gain(ks[3], (L, MLA_Q_RANK)),
        "mla_kv_norm": gain(ks[4], (L, MLA_KV_RANK)),
        "mla_w_q_up": dense(ks[5], (L, MLA_Q_RANK, MLA_HEADS * (MLA_NOPE + MLA_ROPE))),
        "mla_w_kv_up": dense(ks[6], (L, MLA_KV_RANK, MLA_HEADS * (MLA_NOPE + MLA_V))),
        "ret_gn_w": gain(ks[7], (L, RET_V_W)),
        "ret_gn_b": 0.02 * jax.random.normal(ks[8], (L, RET_V_W), jnp.float32),
        "w_branch_mla": dense(ks[9], (L, MLA_OUT_W, D_MODEL)),
        "w_branch_moba": dense(ks[10], (L, MOBA_W, D_MODEL)),
        "w_branch_ret": dense(ks[11], (L, RET_V_W, D_MODEL)),
        "w_out": dense(ks[12], (L, D_MODEL, D_MODEL)),
        "mlp_norm": gain(ks[13], (L, D_MODEL)),
        "w_mlp_up": dense(ks[14], (L, D_MODEL, D_FF)),
        "w_mlp_down": dense(ks[15], (L, D_FF, D_MODEL)),
        "final_norm": gain(ks[16], (D_MODEL,)),
    }

def second_block(x, attn_norm, w_in, mla_q_norm, mla_kv_norm, mla_w_q_up, mla_w_kv_up, ret_gn_w, ret_gn_b,
              w_branch_mla, w_branch_moba, w_branch_ret, w_out, mlp_norm, w_mlp_up, w_mlp_down, final_norm):
    S = x.shape[1]
    ropes = (rope_tables_2(S, MLA_ROPE, ROPE_THETA),
             rope_tables_2(S, MOBA_HEAD_DIM // PARTIAL_ROPE_DIV, ROPE_THETA),
             rope_tables_2(S, RET_QK_DIM, RET_THETA))
    for l in range(DEPTH):
        h = rms_norm_2(x, attn_norm[l])
        x = x + hybrid_mixer(h, w_in[l], mla_q_norm[l], mla_kv_norm[l], mla_w_q_up[l], mla_w_kv_up[l],
                             ret_gn_w[l], ret_gn_b[l], w_branch_mla[l], w_branch_moba[l], w_branch_ret[l],
                             w_out[l], ropes)
        h = rms_norm_2(x, mlp_norm[l])
        x = x + squared_relu_mlp(h, w_mlp_up[l], w_mlp_down[l])
    return rms_norm_2(x, final_norm)


def setup_inputs(seed=0):
    out = dict(first_inputs(seed))
    for name, value in second_inputs(seed + 1).items():
        if name != "x":
            out[name + "_2"] = value
    return out


def reference(
    x, p, positions, w_in, diff_lambda, diff_subln_g, w_branch_diff, w_branch_dsa, w_out, ln1_g,
    ln1_b, w_route_group, b_route_group, w_route_expert, b_route_expert, w_exp_gate, w_exp_up,
    w_exp_down, w_ple, w_ple_gate, ln2_g, ln2_b, attn_norm_2, w_in_2, mla_q_norm_2,
    mla_kv_norm_2, mla_w_q_up_2, mla_w_kv_up_2, ret_gn_w_2, ret_gn_b_2, w_branch_mla_2,
    w_branch_moba_2, w_branch_ret_2, w_out_2, mlp_norm_2, w_mlp_up_2, w_mlp_down_2,
    final_norm_2,
):
    x = first_block(
        x, p, positions, w_in, diff_lambda, diff_subln_g, w_branch_diff, w_branch_dsa, w_out,
        ln1_g, ln1_b, w_route_group, b_route_group, w_route_expert, b_route_expert, w_exp_gate,
        w_exp_up, w_exp_down, w_ple, w_ple_gate, ln2_g, ln2_b,
    )
    return second_block(
        x, attn_norm_2, w_in_2, mla_q_norm_2, mla_kv_norm_2, mla_w_q_up_2, mla_w_kv_up_2,
        ret_gn_w_2, ret_gn_b_2, w_branch_mla_2, w_branch_moba_2, w_branch_ret_2, w_out_2,
        mlp_norm_2, w_mlp_up_2, w_mlp_down_2, final_norm_2,
    )


_drawn_inputs = setup_inputs


def setup_inputs(seed=0):
    import zlib

    import numpy as np

    out = dict(_drawn_inputs(seed))
    spreads = {}
    factors = {'diff_subln_g': 6.784,
     'b_route_group': 3.896,
     'b_route_expert': 4.376,
     'attn_norm_2': 2.962,
     'mla_q_norm_2': 8.0,
     'mla_kv_norm_2': 8.0,
     'ret_gn_w_2': 6.491,
     'ret_gn_b_2': 6.42,
     'final_norm_2': 7.451,
     'mlp_norm_2': 5.239}
    for name, (base, spread) in spreads.items():
        noise = np.random.default_rng([zlib.crc32(name.encode()), seed]).standard_normal(out[name].shape)
        drawn = base * np.exp(spread * noise) if base else spread * noise
        out[name] = __import__('jax').numpy.asarray(drawn.astype(out[name].dtype))
    for name, factor in factors.items():
        out[name] = (out[name] * factor).astype(out[name].dtype)
    return out
```

```python
import math
from contextlib import ExitStack

import numpy as np
import concourse.bass as bass
from concourse import mybir

F32 = mybir.dt.float32
I32 = mybir.dt.int32
U32 = mybir.dt.uint32
ALU = mybir.AluOpType
ACT = mybir.ActivationFunctionType
AX = mybir.AxisListType

P = 128
S = 256
T = S // P
D = 1024
KD = D // P
DEPTH = 2
NG, EPG, NE, DE = 4, 8, 32, 256
TOPK = 64
ALPHA = (2 * DEPTH) ** 0.25
LN_EPS = 1e-5
NORM_EPS = 1e-6
GN_EPS = 1e-5
NEG = -1e30
GONE = -3e38
MAGIC = 12582912.0
BLK = 2048
RING = 4
DFF = 4096

W1 = dict(zip(("dq", "dk", "dv", "sq", "sk", "sv", "iq", "ik", "iw", "ga", "gb"),
              np.cumsum([0, 512, 512, 512, 512, 512, 512, 512, 64, 8, 1024]).tolist()))
W2 = dict(zip(("cq", "ckv", "kr", "mq", "mk", "mv", "rq", "rk", "rv", "rg", "g0", "g1", "g2"),
              np.cumsum([0, 256, 128, 32, 512, 512, 512, 256, 256, 512, 512, 1024, 1024]).tolist()))

P1 = [("ln1_g", D), ("ln1_b", D), ("ln2_g", D), ("ln2_b", D), ("diff_subln_g", 128),
      ("b_route_group", NG), ("b_route_expert", NE), ("diff_lambda", 256)]
P2 = [("attn_norm_2", D), ("mlp_norm_2", D), ("mla_q_norm_2", 256), ("mla_kv_norm_2", 128),
      ("ret_gn_w_2", 512), ("ret_gn_b_2", 512), ("final_norm_2", D)]


def offsets(table):
    at, out = 0, {}
    for name, n in table:
        out[name] = (at, n)
        at += n
    return out, at


P1_AT, P1_N = offsets(P1)
P2_AT, P2_N = offsets(P2)

C_TABLE = [("ident", 128), ("caus", 128), ("decay", 4 * 384), ("invf", 8),
           ("c16", 2 * 16), ("s16", 2 * 16), ("c32", 2 * 32), ("s32", 2 * 32),
           ("c64", 2 * 64), ("s64", 2 * 64), ("iota8", 8), ("nhalf", 8)]
C_AT, C_N = offsets(C_TABLE)


def blocks(layer, first):
    out = []

    def cols(name, idx, kt, c0, c1, step):
        for c in range(c0, c1, step):
            out.append([(name, idx, 0, kt, c, min(c + step, c1))])

    if first:
        w = ("w_in", (layer,), KD)
        cols(*w, W1["iq"], W1["ik"], 256)
        cols(*w, W1["ik"], W1["ga"], 72)
        for n in ("sq", "sk", "sv", "dq", "dk", "dv"):
            cols(*w, W1[n], W1[n] + 512, 256)
        cols(*w, W1["ga"], W1["ga"] + 2 * D, 256)
        cols("w_branch_diff", (layer,), 4, 0, D, 512)
        cols("w_branch_dsa", (layer,), 4, 0, D, 512)
        cols("w_out", (layer,), KD, 0, D, 256)
        out.append([("w_route_group", (layer,), 0, KD, 0, NG), ("w_route_expert", (layer,), 0, KD, 0, NE)])
        cols("w_ple_gate", (layer,), KD, 0, D, 256)
        cols("w_ple", (layer,), 2, 0, D, 1024)
        for e in range(NE):
            idx = (layer, e // EPG, e % EPG)
            cols("w_exp_gate", idx, KD, 0, DE, DE)
            cols("w_exp_up", idx, KD, 0, DE, DE)
            cols("w_exp_down", idx, 2, 0, D, D)
    else:
        w = ("w_in_2", (layer,), KD)
        cols(*w, W2["cq"], W2["ckv"], 256)
        cols(*w, W2["ckv"], W2["mq"], 160)
        cols("mla_w_q_up_2", (layer,), 2, 0, 768, 768)
        cols("mla_w_kv_up_2", (layer,), 1, 0, 1024, 1024)
        for n, m in (("mq", 512), ("mk", 512), ("mv", 512), ("rq", 256), ("rk", 256), ("rv", 512), ("rg", 512)):
            cols(*w, W2[n], W2[n] + m, 256)
        cols(*w, W2["g0"], W2["g0"] + 3 * D, 256)
        for n in ("w_branch_mla_2", "w_branch_moba_2", "w_branch_ret_2"):
            cols(n, (layer,), 4, 0, D, 512)
        cols("w_out_2", (layer,), KD, 0, D, 256)
        cols("w_mlp_up_2", (layer,), KD, 0, DFF, 256)
        for k in range(0, DFF // P, 2):
            out.append([("w_mlp_down_2", (layer,), k, 2, 0, D)])
    return out


STREAM = [b for first in (True, False) for layer in range(DEPTH) for b in blocks(layer, first)]


def width(block):
    return sum(kt * (c1 - c0) for _, _, _, kt, c0, c1 in block)


AT = np.cumsum([0] + [P * width(b) for b in STREAM]).tolist()


class Token:

    def __init__(self, sem):
        self.sem, self.value, self.marked = sem, None, False


class Queue:

    def __init__(self, eng, sem):
        self.eng, self.sem, self.items = eng, sem, []

    def do(self, fn, *waits):
        token = Token(self.sem)
        flat = []
        for w in waits:
            flat += w if isinstance(w, list) else [w] if w is not None else []
        for w in flat:
            w.marked = True
        self.items.append((fn, flat, token))
        return token

    def number(self):
        n = 0
        for _, _, token in self.items:
            if isinstance(token, Token) and token.value is None and token.marked:
                n += 1
                token.value = n

    def emit(self):
        seen = {}
        for fn, waits, token in self.items:
            for w in waits:
                if seen.get(id(w.sem), 0) < w.value:
                    self.eng.wait_ge(w.sem, w.value)
                    seen[id(w.sem)] = w.value
            ins = fn()
            if token.marked and token.sem is self.sem:
                ins.then_inc(self.sem, 1)


class DmaDone:

    def __init__(self, sem, value):
        self.sem, self.value, self.marked = sem, value, True


def build(nc, wts, par1, par2, consts, pos, x0, x0T, pT, out):
    ctx = ExitStack()
    with ctx:
        def sb(name, *shape, dt=F32):
            return ctx.enter_context(nc.sbuf_tensor(name, [P, *shape], dt))

        def sem(name):
            return ctx.enter_context(nc.semaphore(name))

        pe = Queue(nc.tensor, sem("pe"))
        dve = Queue(nc.vector, sem("dve"))
        act = Queue(nc.scalar, sem("act"))
        pool = Queue(nc.gpsimd, sem("pool"))
        sp = Queue(nc.sync, sem("sp"))

        ring = [sb(f"ring{i}", BLK) for i in range(RING)]
        ring_sem = [sem(f"ring_sem{i}") for i in range(RING)]
        X = sb("X", T, D)
        XT = sb("XT", KD, S)
        A = sb("A", 36 * 256)
        STA = A[:, 0:2048]
        STB = A[:, 2048:5120]
        QKT = A[:, 5120:9216]
        V = sb("V", T, 2048)
        GT = sb("GT", 3, KD, S)
        SC = sb("SC", 8, S)
        PT = sb("PT", 8, 2, P)
        O = sb("O", T, 512)
        OT = sb("OT", 3, 4, S)
        H = sb("H", T, D)
        TMP = sb("TMP", 1024)
        TMP2 = sb("TMP2", 1792)
        PAR = sb("PAR", max(P1_N, P2_N))
        CST = sb("CST", C_N)
        sm = sb("sm", 512)
        bias = TMP[:, 512:1024].rearrange("p (t s) -> p t s", t=T)
        work = TMP2[:, 1024:1536].rearrange("p (t s) -> p t s", t=T)
        comb = sb("comb", T, NE)
        posi = sb("posi", T, dt=I32)
        idx8 = sb("idx8", 8, dt=U32)
        ropeb = sb("ropeb", 2, T, 16)

        def const(name):
            a, n = C_AT[name]
            return CST[:, a:a + n]

        def par1_(name):
            a, n = P1_AT[name]
            return PAR[:, a:a + n]

        def par2_(name):
            a, n = P2_AT[name]
            return PAR[:, a:a + n]

        ident = const("ident")

        scp = ctx.enter_context(nc.psum_tensor("scp", [P, 8, S], F32))
        bank = [ctx.enter_context(nc.psum_tensor(f"bank{i}", [P, 512], F32)) for i in range(4)]

        dma_n = {}

        def load(q, dst, src, name, *waits):
            if name not in dma_n:
                dma_n[name] = [sem(name), 0]
            s = dma_n[name]
            s[1] += 16
            q.items.append((lambda: q.eng.dma_start(dst, src).then_inc(s[0], 16),
                            [w for v in waits for w in (v if isinstance(v, list) else [v])], DmaDone(s[0], s[1])))
            for w in q.items[-1][1]:
                w.marked = True
            return DmaDone(s[0], s[1])

        sent, taken = [0], [0]
        freed = []

        def send_block():
            i = sent[0]
            n = width(STREAM[i])
            src = wts[AT[i]:AT[i + 1]].rearrange("(p n) -> p n", p=P)
            slot, turn = i % RING, i // RING + 1
            waits = [freed[i - RING]] if i >= RING else []
            for w in waits:
                w.marked = True
            sp.items.append((lambda: nc.sync.dma_start(ring[slot][:, 0:n], src).then_inc(ring_sem[slot], 16),
                             waits, DmaDone(ring_sem[slot], 16 * turn)))
            sent[0] += 1

        def take(*names):
            i = taken[0]
            taken[0] += 1
            assert tuple(b[0] for b in STREAM[i]) == names, (names, STREAM[i])
            at, views = 0, []
            for _, _, _, kt, c0, c1 in STREAM[i]:
                n = kt * (c1 - c0)
                views.append(ring[i % RING][:, at:at + n].rearrange("p (k n) -> p k n", k=kt))
                at += n
            return views, DmaDone(ring_sem[i % RING], 16 * (i // RING + 1))

        def release(token):
            freed.append(token)
            assert len(freed) == taken[0]
            if sent[0] < len(STREAM):
                send_block()

        c_in = [load(sp, CST[:, :], consts.rearrange("(p n) -> p n", p=P), "l_cst"),
                load(sp, posi[:, :], pos, "l_pos")]
        xt_in = load(sp, XT[:, :, :], x0T, "l_xt")
        x_in = load(sp, X[:, :, :], x0, "l_x")
        for _ in range(RING):
            send_block()

        bank_free = [None] * 4
        bank_at = [0]

        def next_bank():
            b = bank_at[0] % 4
            bank_at[0] += 1
            return b

        turn = [0]

        def copy(q, dst, src, *waits):
            if q is act:
                return act.do(lambda: nc.scalar.copy(dst, src), *waits)
            return dve.do(lambda: nc.vector.tensor_copy(dst, src), *waits)

        def either():
            turn[0] += 1
            return act if turn[0] % 2 else dve

        def mm(dst, lhsT, rhs, start, stop, *waits):
            return pe.do(lambda: nc.tensor.matmul(dst, lhsT, rhs, start=start, stop=stop), *waits)

        def tr(dst, src, *waits):
            return pe.do(lambda: nc.tensor.transpose(dst, src, ident), *waits)

        def tokens_major(name, src, src_ready, kt=KD):
            (w,), loaded = take(name)
            n = w.shape[2]
            b = next_bank()
            v = bank[b][:, 0:T * n].rearrange("p (t n) -> p t n", t=T)
            waits = [loaded, src_ready, bank_free[b]]
            for t in range(T):
                for k in range(kt):
                    last = mm(v[:, t, :], src[:, k, t * P:(t + 1) * P], w[:, k, :], k == 0, k == kt - 1, *waits)
                    waits = []
            release(last)
            return b, v, last

        def features_major(w, m0, src, waits, kt=KD):
            b = next_bank()
            v = bank[b][:, :].rearrange("p (m s) -> p m s", m=2)
            waits = [*waits, bank_free[b]]
            for m in range(2):
                for k in range(kt):
                    c = (m0 + m) * P
                    last = mm(v[:, m, :], w[:, k, c:c + P], src[:, k, :], k == 0, k == kt - 1, *waits)
                    waits = []
            return b, v, last

        def transposes(dst, pieces, ready, free):
            done = []
            for i0 in range(0, len(pieces), 4):
                part = pieces[i0:i0 + 4]
                b = next_bank()
                waits = [ready, bank_free[b]]
                waits = [w for v in waits if v is not None for w in (v if isinstance(v, list) else [v])]
                c = part[0].shape[1]
                for j, src in enumerate(part):
                    last = tr(bank[b][0:c, j * P:(j + 1) * P], src, *waits)
                    waits = []
                q = either()
                bank_free[b] = copy(q, dst(i0, len(part)), bank[b][0:c, 0:len(part) * P], last, free)
                done.append(bank_free[b])
            return done

        def rope(st, heads, lo, hw, cc, ss, ready):
            n = T * heads * 2 * hw
            a = TMP[:, 0:n].rearrange("p (t h d) -> p t h d", t=T, h=heads)
            b = TMP2[:, 0:n].rearrange("p (t h d) -> p t h d", t=T, h=heads)

            def table(v, d0, d1):
                return v[:, :, d0:d1].unsqueeze(2).broadcast_to([P, T, heads, d1 - d0])

            toks = []
            for t in range(T):
                def tab(v, d0, d1, t=t):
                    return v[:, t, d0:d1].unsqueeze(1).broadcast_to([P, heads, d1 - d0])
                x = st[:, t, :, lo:lo + 2 * hw]
                x1 = st[:, t, :, lo:lo + hw]
                x2 = st[:, t, :, lo + hw:lo + 2 * hw]
                o1 = dve.do(lambda t=t, x=x: nc.vector.tensor_tensor(a[:, t], x, tab(cc, 0, 2 * hw, t), ALU.mult),
                            ready, rope_done[-1:])
                dve.do(lambda t=t, x2=x2: nc.vector.tensor_tensor(b[:, t, :, 0:hw], x2, tab(ss, 0, hw, t), ALU.mult))
                o3 = dve.do(lambda t=t, x1=x1: nc.vector.tensor_tensor(b[:, t, :, hw:2 * hw], x1, tab(ss, hw, 2 * hw, t), ALU.mult))
                toks.append((x, o1, o3))
            for t, (x, o1, o3) in enumerate(toks):
                last = dve.do(lambda t=t, x=x: nc.vector.tensor_tensor(x, a[:, t], b[:, t], ALU.add), o1, o3)
            rope_done.append(last)
            return last

        rope_done = []

        def pos_of(i):
            return ((i % 2) + 2 * (i // 4)) * 2 + (i // 2) % 2

        sc_free = [None]
        p_free = [None]
        pt_free = [None]
        o_free = [None]

        def scores(t, heads, q_of, k_of, ready):
            kl = P * (t + 1)
            waits = [ready, sc_free[0]]
            for i in range(heads):
                last = mm(scp[:, pos_of(i), 0:kl], q_of(i)[:, t * P:(t + 1) * P], k_of(i)[:, 0:kl],
                          True, True, *waits)
                waits = []
            return last

        def softmax_parts(t, heads, scale, done, extra=None):
            kl = P * (t + 1)
            if extra is None:
                v = scp[:, 0:heads, t * P:kl]
                m = const("caus").unsqueeze(1).broadcast_to([P, heads, P])
                a = dve.do(lambda: nc.vector.tensor_tensor(v, v, m, ALU.add), done)
            else:
                v = scp[:, 0:heads, 0:kl]
                m = bias[:, t, 0:kl].unsqueeze(1).broadcast_to([P, heads, kl])
                a = dve.do(lambda: nc.vector.tensor_tensor(v, v, m, ALU.add), done, extra)
            mx = sm[:, 0:8]
            nb = sm[:, 8 + 8 * t:16 + 8 * t]
            z = sm[:, 24 + 8 * t:32 + 8 * t]
            rz = sm[:, 40 + 8 * t:48 + 8 * t]
            b = dve.do(lambda: nc.vector.tensor_reduce(mx[:, 0:heads], scp[:, 0:heads, 0:kl], AX.X, ALU.max), a)
            c = dve.do(lambda: nc.vector.tensor_scalar(nb, mx, -scale, None, ALU.mult), b)
            for i in range(heads):
                e = act.do(lambda i=i: nc.scalar.activation(SC[:, i, 0:kl], scp[:, i, 0:kl], ACT.Exp,
                                                            bias=nb[:, i:i + 1], scale=scale,
                                                            accum_out=z[:, i:i + 1]), c, p_free[0])
            sc_free[0] = e
            r = dve.do(lambda: nc.vector.reciprocal(rz, z), e)
            return e, r, rz

        def weighted(t, heads, p_of, v_of, vw, p_ready):
            nk = t + 1
            done = []
            pieces = [p_of(i)[:, k * P:(k + 1) * P] for i in range(heads) for k in range(nk)]
            flat = PT[:, :, :, :].rearrange("p h k q -> p (h k q)")
            done = transposes(lambda i0, n: flat[:, i0 * P:(i0 + n) * P], pieces, p_ready, pt_free[0])
            p_free[0] = pe_last()
            b = next_bank()
            waits = [*done, bank_free[b]]
            for i in range(heads):
                for k in range(nk):
                    j = i * nk + k
                    last = mm(bank[b][:, i * vw:(i + 1) * vw], flat[:, j * P:(j + 1) * P], v_of(i, k),
                              k == 0, k == nk - 1, *waits)
                    waits = []
            pt_free[0] = last
            return b, last

        def pe_last():
            return pe.items[-1][2]

        def norm_stats(src, groups, n, base, eps, rms, ready):
            chunk = min(n, 512)
            st = sm[:, 128:128 + 12 * max(1, groups)]
            last = None
            nch = n // chunk
            for g in range(groups):
                for c in range(nch):
                    o = st[:, (g * nch + c) * 6:(g * nch + c) * 6 + 6]
                    s_ = src[:, g, c * chunk:(c + 1) * chunk]
                    last = dve.do(lambda o=o, s_=s_: nc.vector.bn_stats(o, s_), ready if last is None else None,
                                  stat_free[0] if last is None else None)
            mv = sm[:, base:base + 2 * groups]
            for g in range(groups):
                i_ = st[:, g * nch * 6:(g + 1) * nch * 6]
                last2 = dve.do(lambda g=g, i_=i_: nc.vector.bn_aggr(mv[:, 2 * g:2 * g + 2], i_), last)
            stat_free[0] = last2
            mean = mv.rearrange("p (g c) -> p g c", c=2)[:, :, 0]
            var = mv.rearrange("p (g c) -> p g c", c=2)[:, :, 1]
            if rms:
                sq = sm[:, 120:120 + groups]
                a = dve.do(lambda: nc.vector.tensor_tensor(sq, mean, mean, ALU.mult), last2)
                last2 = dve.do(lambda: nc.vector.tensor_tensor(var, var, sq, ALU.add), a)
            e_ = dve.do(lambda: nc.vector.tensor_scalar(var, var, eps, None, ALU.add), last2)
            return mean, var, pool.do(lambda: nc.gpsimd.tensor_tensor(var, var, const("nhalf")[:, 0:groups], ALU.pow), e_)

        stat_free = [None]

        def rms_norm(dst, src, g, eps, n, ready, base=64):
            last = []
            for t in range(T):
                mean, var, ok = norm_stats(src[:, t:t + 1, :], 1, n, base + 2 * t, eps, True, ready)
                last.append(dve.do(lambda t=t, var=var: nc.vector.scalar_tensor_tensor(
                    dst[:, t, :], src[:, t, :], var, g, ALU.mult, ALU.mult), ok))
            return last

        def layer_norm(x, g, b, ready):
            last = []
            for t in range(T):
                mean, var, ok = norm_stats(x[:, t:t + 1, :], 1, D, 64 + 2 * t, LN_EPS, False, ready)
                a = dve.do(lambda t=t, mean=mean, var=var: nc.vector.tensor_scalar(
                    x[:, t, :], x[:, t, :], mean, var, ALU.subtract, ALU.mult), ok)
                a = dve.do(lambda t=t: nc.vector.tensor_tensor(x[:, t, :], x[:, t, :], g, ALU.mult), a)
                last.append(dve.do(lambda t=t: nc.vector.tensor_tensor(x[:, t, :], x[:, t, :], b, ALU.add), a))
            return last

        def turn_x(src, ready):
            done = []
            for c in range(0, KD, 2):
                pieces = [src[:, t, (c + j) * P:(c + j + 1) * P] for j in range(2) for t in range(T)]
                dst = XT[:, c:c + 2, :].rearrange("p k s -> p (k s)")
                done += transposes(lambda i0, n, dst=dst: dst, pieces, ready, None)
            return done

        fill_n = [0, 0]
        fill_src = [None]
        fill_name = [None]
        gate_done = []

        def start_fill(name, n, src_ready):
            fill_n[:] = [0, n]
            fill_src[0] = src_ready
            fill_name[0] = name
            gate_done.clear()

        def fill(n=1):
            for _ in range(n):
                if fill_n[0] == fill_n[1]:
                    return
                j = fill_n[0]
                fill_n[0] += 1
                (w,), loaded = take(fill_name[0])
                b, v, last = features_major(w, 0, XT, [loaded, fill_src[0]])
                release(last)
                dst = GT[:, j // 4, 2 * (j % 4):2 * (j % 4) + 2, :]
                bank_free[b] = act.do(lambda dst=dst, v=v: nc.scalar.activation(dst, v, ACT.Tanh, scale=0.5),
                                      last, merged_read[0])
                gate_done.append(bank_free[b])

        merged_read = [None]

        def projection(name, dsts, src_ready, *free, kt=KD, src=None):
            b, v, last = tokens_major(name, XT if src is None else src, src_ready, kt=kt)
            done = []
            q = act
            for dst, c0, c1 in dsts:
                tok = copy(q, dst, v[:, :, c0:c1], last, *free)
                done.append(tok)
            bank_free[b] = done[-1]
            return done

        MG = H[:, :, :].rearrange("p t d -> p (t d)").rearrange("p (k s) -> p k s", k=KD)

        def branches(names, ready):
            done = [None] * 4
            for n, name in enumerate(names):
                for half in range(2):
                    (w,), loaded = take(name)
                    for m in range(2):
                        b, v, last = features_major(w, 2 * m, OT[:, n], [loaded, ready[n]], kt=4)
                        c = 4 * half + 2 * m
                        g = GT[:, n, c:c + 2, :]
                        dst = g if n else MG[:, c:c + 2, :]
                        a = dve.do(lambda g=g, v=v, dst=dst: nc.vector.scalar_tensor_tensor(
                            dst, g, 1.0, v, ALU.add, ALU.mult), last, list(gate_done), h_free[0])
                        bank_free[b] = a
                        if n:
                            M = MG[:, c:c + 2, :]
                            a = dve.do(lambda M=M, g=g: nc.vector.tensor_tensor(M, M, g, ALU.add), a, done[2 * half + m])
                        done[2 * half + m] = a
                    release(last)
            merged_read[0] = done[-1]
            return done

        h_free = [None]

        def mix_out(name, scale, ready):
            done = []
            for c in range(4):
                b, v, last = tokens_major(name, MG, ready)
                xs = X[:, :, c * 256:(c + 1) * 256]
                if scale != 1.0:
                    a = dve.do(lambda xs=xs: nc.vector.tensor_scalar(xs, xs, scale, None, ALU.mult), last)
                else:
                    a = last
                bank_free[b] = dve.do(lambda xs=xs, v=v: nc.vector.scalar_tensor_tensor(
                    xs, v, 0.5, xs, ALU.mult, ALU.add), a, last)
                done.append(bank_free[b])
            return done

        def cs(n):
            return (const(f"c{n}").rearrange("p (t d) -> p t d", t=T), const(f"s{n}").rearrange("p (t d) -> p t d", t=T))

        posf = sm[:, 100:102]
        ang = TMP[:, 0:16].rearrange("p (t d) -> p t d", t=T)
        kk = TMP[:, 16:32].rearrange("p (t d) -> p t d", t=T)
        r = TMP[:, 32:48].rearrange("p (t d) -> p t d", t=T)
        ab = TMP[:, 48:64].rearrange("p (t d) -> p t d", t=T)
        a = dve.do(lambda: nc.vector.tensor_copy(posf, posi[:, :]), c_in)
        for t in range(T):
            a2 = dve.do(lambda t=t: nc.vector.tensor_scalar(ang[:, t, :], const("invf"), posf[:, t:t + 1], None, ALU.mult), a)
        a = dve.do(lambda: nc.vector.tensor_scalar(kk, ang, 1.0 / (2 * math.pi), MAGIC, ALU.mult, ALU.add), a2)
        a = dve.do(lambda: nc.vector.tensor_scalar(kk, kk, -MAGIC, None, ALU.add), a)
        parts, rest = [], 2 * math.pi
        for bits in (4, 12, 20):
            c = math.floor(rest * 2 ** bits) / 2 ** bits
            parts.append(c)
            rest -= c
        parts.append(rest)
        src_ = ang
        for c in parts:
            a = dve.do(lambda c=c, src_=src_: nc.vector.scalar_tensor_tensor(r, kk, -c, src_, ALU.mult, ALU.add), a)
            src_ = r
        a = dve.do(lambda: nc.vector.tensor_scalar(r, r, -3.1415925, 3.1415925, ALU.max, ALU.min), a)
        b_ = dve.do(lambda: nc.vector.tensor_scalar(ab, r, -1.0, None, ALU.mult), a)
        b_ = dve.do(lambda: nc.vector.tensor_tensor(ab, ab, r, ALU.max), b_)
        b_ = dve.do(lambda: nc.vector.tensor_scalar(ab, ab, -1.0, math.pi / 2, ALU.mult, ALU.add), b_)
        RC, RS = ropeb[:, 0], ropeb[:, 1]
        e1 = act.do(lambda: nc.scalar.activation(RS[:, :, 8:16], r, ACT.Sin), a)
        e2 = act.do(lambda: nc.scalar.activation(RC[:, :, 0:8], ab, ACT.Sin), b_)
        dve.do(lambda: nc.vector.tensor_scalar(RS[:, :, 0:8], RS[:, :, 8:16], -1.0, None, ALU.mult), e1)
        rope_ready = dve.do(lambda: nc.vector.tensor_copy(RC[:, :, 8:16], RC[:, :, 0:8]), e2)
        rope_done.append(rope_ready)

        x_ready = [xt_in]
        par_free = []
        x_ok = [x_in]

        def causal_heads(t, heads, q_of, k_of, v_of, vw, scale, ready, extra=None):
            d = scores(t, heads, q_of, k_of, ready)
            fill()
            e, rdy, rz = softmax_parts(t, heads, scale, d, extra)
            b, last = weighted(t, heads, lambda i: SC[:, pos_of(i), :], v_of, vw, [e])
            fill()
            o = O[:, t, :]
            for i in range(heads):
                p_ = pos_of(i)
                tok = dve.do(lambda i=i, p_=p_: nc.vector.tensor_scalar(
                    o[:, i * vw:(i + 1) * vw], bank[b][:, i * vw:(i + 1) * vw], rz[:, p_:p_ + 1], None, ALU.mult),
                    last, rdy, o_free[0])
            bank_free[b] = tok
            return tok

        def turn_o(n, ready):
            flat = OT[:, n].rearrange("p k s -> p (k s)")
            pieces = [O[:, t, k * P:(k + 1) * P] for k in range(4) for t in range(T)]
            done = transposes(lambda i0, m: flat[:, i0 * P:(i0 + m) * P], pieces, ready, ot_free[0])
            o_free[0] = pe_last()
            return done

        ot_free = [None]

        def turn_heads(dst, st, nblk, w, ready, free):
            pieces = [st[:, t, k * w:(k + 1) * w] for k in range(nblk) for t in range(T)]
            flat = dst.rearrange("p k s -> p (k s)")
            return transposes(lambda i0, m: flat[:, i0 * P:(i0 + m) * P], pieces, ready, free)

        def first_layer(l):
            lam_init = 0.8 - 0.6 * math.exp(-0.3 * l)
            src = par1[l * P1_N:(l + 1) * P1_N].partition_broadcast(P)
            par = load(pool, PAR[:, 0:P1_N], src, "l_par", par_free)
            xr = x_ready
            IST = STB[:, 0:T * 640].rearrange("p (t c) -> p t c", t=T)
            IW = sm[:, 104:104 + 16].rearrange("p (t h) -> p t h", t=T)
            done = []
            for c in range(2):
                done += projection("w_in", [(IST[:, :, c * 256:(c + 1) * 256], 0, 256)], xr, a_free[0])
            done += projection("w_in", [(IST[:, :, 512:576], 0, 64), (IST[:, :, 576:640], 0, 64), (IW, 64, 72)],
                               xr, a_free[0])
            iw = dve.do(lambda: nc.vector.tensor_scalar(IW, IW, 8 ** -0.5, None, ALU.mult), done)
            rot = rope(IST.rearrange("p t (h d) -> p t h d", d=64), 10, 0, 8, RC, RS, [*done, rope_ready])
            SST = STA.rearrange("p (t c) -> p t c", t=T)
            done = []
            for c in range(4):
                done += projection("w_in", [(SST[:, :, c * 256:(c + 1) * 256], 0, 256)], xr, a_free[0])
            IT = QKT[:, 0:5 * S].rearrange("p (k s) -> p k s", k=5)
            it = turn_heads(IT, IST, 5, P, rot, a_free[0])
            ist_free = pe_last()
            rot = rope(SST.rearrange("p t (h d) -> p t h d", d=64), 16, 0, 8, RC, RS, done)
            sel = []
            for t in range(T):
                kl = P * (t + 1)
                d = scores(t, 8, lambda i: IT[64 * (i % 2):64 * (i % 2) + 64, i // 2, :],
                           lambda i: IT[64 * (i % 2):64 * (i % 2) + 64, 4, :], it)
                if t == 0:
                    for c in range(2):
                        vt = projection("w_in", [(V[:, :, c * 256:(c + 1) * 256], 0, 256)], xr, v_free[0])
                else:
                    fillq = vt
                e = act.do(lambda t=t, kl=kl: nc.scalar.activation(SC[:, :, 0:kl], scp[:, :, 0:kl], ACT.Relu, scale=0.125),
                           d, p_free[0])
                sc_free[0] = e
                wk = work[:, t, 0:kl]
                a = e
                for i in range(8):
                    p_ = pos_of(i)
                    if i == 0:
                        a = dve.do(lambda wk=wk, p_=p_, t=t, kl=kl, i=i: nc.vector.tensor_scalar(
                            wk, SC[:, p_, 0:kl], IW[:, t, i:i + 1], None, ALU.mult), a, iw)
                    else:
                        a = dve.do(lambda wk=wk, p_=p_, t=t, kl=kl, i=i: nc.vector.scalar_tensor_tensor(
                            wk, SC[:, p_, 0:kl], IW[:, t, i:i + 1], wk, ALU.mult, ALU.add), a)
                p_free[0] = a
                dg = work[:, t, t * P:kl]
                a = dve.do(lambda dg=dg: nc.vector.tensor_tensor(dg, dg, const("caus"), ALU.add), a)
                m8 = sm[:, 80 + 8 * t:88 + 8 * t]
                for _ in range(TOPK // 8):
                    a = dve.do(lambda m8=m8, wk=wk: nc.vector.max(m8, wk), a)
                    a = dve.do(lambda m8=m8, wk=wk: nc.vector.match_replace(wk, m8, wk, GONE), a)
                bs = bias[:, t, 0:kl]
                a = dve.do(lambda bs=bs, wk=wk: nc.vector.tensor_scalar(bs, wk, -2e38, NEG, ALU.is_gt, ALU.mult), a)
                dg = bias[:, t, t * P:kl]
                sel.append(dve.do(lambda dg=dg: nc.vector.tensor_tensor(dg, dg, const("caus"), ALU.add), a))
            it_free = pe_last()
            DST = STB.rearrange("p (t c) -> p t c", t=T)[:, :, 0:1024]
            done = []
            for c in range(4):
                done += projection("w_in", [(STB[:, 0:2048].rearrange("p (t c) -> p t c", t=T)[:, :, c * 256:(c + 1) * 256], 0, 256)],
                                   xr, ist_free)
            DST = STB[:, 0:2048].rearrange("p (t c) -> p t c", t=T)
            dt_ = []
            for c in range(2):
                dt_ += projection("w_in", [(V[:, :, 512 + c * 256:512 + (c + 1) * 256], 0, 256)], xr, v_free[0])
            drot = rope(DST.rearrange("p t (h d) -> p t h d", d=64), 16, 0, 8, RC, RS, done)
            start_fill("w_in", 8, xr)
            ST = QKT[:, 0:8 * S].rearrange("p (k s) -> p k s", k=8)
            DT = QKT[:, 8 * S:16 * S].rearrange("p (k s) -> p k s", k=8)
            dtr = turn_heads(DT, DST, 8, P, drot, None)
            str_ = turn_heads(ST, SST, 8, P, rot, it_free)
            lp = par1_("diff_lambda").rearrange("p (a b d) -> p a b d", a=2, b=2)
            pr = sm[:, 256:384].rearrange("p (a d) -> p a d", a=2)
            sums, lam = sm[:, 116:118], sm[:, 118:119]
            a = dve.do(lambda: nc.vector.tensor_tensor(pr, lp[:, :, 0], lp[:, :, 1], ALU.mult), par)
            a = dve.do(lambda: nc.vector.tensor_reduce(sums, pr, AX.X, ALU.add), a)
            a = act.do(lambda: nc.scalar.activation(sums, sums, ACT.Exp), a)
            a = dve.do(lambda: nc.vector.tensor_tensor(lam, sums[:, 1:2], sums[:, 0:1], ALU.subtract), a)
            nlam = dve.do(lambda: nc.vector.tensor_scalar(lam, lam, -lam_init, None, ALU.add), a)
            for t in range(T):
                kl = P * (t + 1)
                d = scores(t, 8, lambda i: DT[64 * (i % 2):64 * (i % 2) + 64, i // 2, :],
                           lambda i: DT[64 * (i % 2):64 * (i % 2) + 64, 4 + i // 2, :], dtr)
                fill()
                e, rdy, rz = softmax_parts(t, 8, 0.125, d)
                w1 = sm[:, 56:64]
                a = dve.do(lambda rz=rz: nc.vector.tensor_scalar(w1, rz, lam, None, ALU.mult), rdy, nlam)
                for h in range(4):
                    p0, p1 = pos_of(2 * h), pos_of(2 * h + 1)
                    x1 = SC[:, p1, 0:kl]
                    x0_ = SC[:, p0, 0:kl]
                    b = dve.do(lambda x1=x1, p1=p1: nc.vector.tensor_scalar(x1, x1, w1[:, p1:p1 + 1], None, ALU.mult), a, e)
                    pr_ = dve.do(lambda x0_=x0_, x1=x1, p0=p0, rz=rz: nc.vector.scalar_tensor_tensor(
                        x0_, x0_, rz[:, p0:p0 + 1], x1, ALU.mult, ALU.add), b)
                b, last = weighted(t, 4, lambda i: SC[:, pos_of(2 * i), :],
                                   lambda i, k: V[:, k, 512 + i * P:512 + (i + 1) * P], P, [pr_])
                fill()
                ob = O[:, t, :].rearrange("p (h d) -> p h d", h=4)
                o = dve.do(lambda ob=ob, b=b: nc.vector.tensor_copy(ob, bank[b][:, :].rearrange("p (h d) -> p h d", h=4)),
                           last, o_free[0])
                bank_free[b] = o
                mean, var, ok = norm_stats(ob, 4, P, 64, LN_EPS, True, o)
                g = par1_("diff_subln_g")
                for h in range(4):
                    oh = ob[:, h, :]
                    a = dve.do(lambda oh=oh, var=var, h=h: nc.vector.tensor_scalar(
                        oh, oh, var[:, h:h + 1], 1.0 - lam_init, ALU.mult, ALU.mult), ok)
                o = dve.do(lambda ob=ob, g=g: nc.vector.tensor_tensor(
                    ob, ob, g.unsqueeze(1).broadcast_to([P, 4, P]), ALU.mult), a)
            ota = turn_o(0, o)
            for t in range(T):
                o = causal_heads(t, 8, lambda i: ST[64 * (i % 2):64 * (i % 2) + 64, i // 2, :],
                                 lambda i: ST[64 * (i % 2):64 * (i % 2) + 64, 4 + i // 2, :],
                                 lambda i, k: V[:, k, i * 64:(i + 1) * 64], 64, 0.125, str_, sel[t])
            v_free[0] = pe_last()
            fill(8)
            otb = turn_o(1, o)
            m = branches(("w_branch_diff", "w_branch_dsa"), (ota, otb))
            ot_free[0] = pe_last()
            x = mix_out("w_out", ALPHA, [*m, *x_ok])
            h_free[0] = pe_last()
            x = layer_norm(X, par1_("ln1_g"), par1_("ln1_b"), [*x, par])
            xt = turn_x(X, x)
            (wg, we), loaded = take("w_route_group", "w_route_expert")
            b = next_bank()
            lg = sm[:, 384:384 + T * 36].rearrange("p (t c) -> p t c", t=T)
            waits = [loaded, *xt, bank_free[b]]
            for t in range(T):
                for c0, w in ((0, wg), (4, we)):
                    n = w.shape[2]
                    for k in range(KD):
                        last = mm(bank[b][:, t * 64 + c0:t * 64 + c0 + n], XT[:, k, t * P:(t + 1) * P], w[:, k, :],
                                  k == 0, k == KD - 1, *waits)
                        waits = []
            release(last)
            rb = PAR[:, P1_AT["b_route_group"][0]:P1_AT["b_route_group"][0] + 36]
            for t in range(T):
                a = dve.do(lambda t=t, b=b: nc.vector.tensor_tensor(lg[:, t, :], bank[b][:, t * 64:t * 64 + 36], rb, ALU.add),
                           last)
            bank_free[b] = a
            for t in range(T):
                route(lg[:, t, :], comb[:, t, :], a)
            cm = dve.items[-1][2]
            pt_in = load(pool, TMP2[:, 0:512].rearrange("p (k s) -> p k s", k=2), pT[l], "l_pt", rope_done[-1:])
            PG = TMP
            aa = []
            GP = A[:, 0:2048].rearrange("p (t d) -> p t d", t=T)
            for c in range(4):
                b, v, last = tokens_major("w_ple_gate", XT, xt)
                g = GP[:, :, c * 256:(c + 1) * 256]
                bank_free[b] = act.do(lambda g=g, v=v: nc.scalar.activation(g, v, ACT.Tanh, scale=0.5), last)
                aa.append(bank_free[b])
            (w,), loaded = take("w_ple")
            PTT = TMP2[:, 0:512].rearrange("p (k s) -> p k s", k=2)
            for c in range(4):
                b = next_bank()
                v = bank[b][:, :].rearrange("p (t n) -> p t n", t=T)
                waits = [loaded, pt_in, bank_free[b]]
                for t in range(T):
                    for k in range(2):
                        last = mm(v[:, t, :], PTT[:, k, t * P:(t + 1) * P], w[:, k, c * 256:(c + 1) * 256],
                                  k == 0, k == 1, *waits)
                        waits = []
                g = GP[:, :, c * 256:(c + 1) * 256]
                xs = X[:, :, c * 256:(c + 1) * 256]
                a = dve.do(lambda g=g, v=v: nc.vector.scalar_tensor_tensor(g, g, 1.0, v, ALU.add, ALU.mult), last, aa)
                bank_free[b] = a
                dve.do(lambda xs=xs: nc.vector.tensor_scalar(xs, xs, ALPHA, None, ALU.mult), xt)
                a = dve.items[-1][2]
                xl = dve.do(lambda xs=xs, g=g: nc.vector.scalar_tensor_tensor(xs, g, 0.5, xs, ALU.mult, ALU.add), a,
                            bank_free[b])
            release(last)
            ple = xl
            yv = scp[:, :, :].rearrange("p a s -> p (a s)").rearrange("p (t n) -> p t n", t=T)
            HG = [A[:, 2048 + i * 1024:2048 + i * 1024 + 512].rearrange("p (m s) -> p m s", m=2) for i in range(2)]
            CB = [A[:, 2048 + i * 1024 + 512:2048 + i * 1024 + 768] for i in range(2)]
            SG = [A[:, 4096 + i * 512:4096 + (i + 1) * 512].rearrange("p (m s) -> p m s", m=2) for i in range(2)]
            hg_free = [None, None]
            pending = None

            def down(e, ready):
                (w,), loaded = take("w_exp_down")
                waits = [loaded, ready, sc_free[0]]
                for k in range(2):
                    for t in range(T):
                        for n in range(2):
                            last = pe.do(lambda k=k, t=t, n=n, e=e: nc.tensor.matmul(
                                yv[:, t, n * 512:(n + 1) * 512], HG[e % 2][:, k, t * P:(t + 1) * P],
                                w[:, k, n * 512:(n + 1) * 512], start=(e == 0 and k == 0), stop=(e == NE - 1 and k == 1)),
                                *waits)
                            waits = []
                release(last)
                hg_free[e % 2] = last

            for e in range(NE):
                (w,), loaded = take("w_exp_gate")
                b1, g, l1 = features_major(w, 0, XT, [loaded, *xt])
                release(l1)
                (w,), loaded = take("w_exp_up")
                b2, u, l2 = features_major(w, 0, XT, [loaded])
                release(l2)
                b3 = next_bank()
                waits = [cm, bank_free[b3]]
                for t in range(T):
                    l3 = mm(bank[b3][:, t * P:(t + 1) * P], comb[:, t, e:e + 1].broadcast_to([P, P]), ident, True, True, *waits)
                    waits = []
                i = e % 2
                a = act.do(lambda g=g, i=i: nc.scalar.activation(SG[i], g, ACT.Tanh, scale=0.5), l1, hg_free[i])
                cb = act.do(lambda i=i, b3=b3: nc.scalar.copy(CB[i], bank[b3][:, 0:S]), l3, hg_free[i])
                bank_free[b3] = cb
                a = dve.do(lambda g=g, i=i: nc.vector.scalar_tensor_tensor(SG[i], SG[i], 1.0, g, ALU.add, ALU.mult), a)
                bank_free[b1] = a
                a = dve.do(lambda u=u, i=i: nc.vector.scalar_tensor_tensor(SG[i], SG[i], 0.5, u, ALU.mult, ALU.mult), a, l2)
                bank_free[b2] = a
                a = dve.do(lambda i=i: nc.vector.tensor_tensor(
                    HG[i], SG[i], CB[i].unsqueeze(1).broadcast_to([P, 2, S]), ALU.mult), a, cb, hg_free[i])
                down(e, a)
            last = pe_last()
            for t in range(T):
                a = dve.do(lambda t=t: nc.vector.tensor_tensor(X[:, t, :], X[:, t, :], yv[:, t, :], ALU.add), last, ple)
            sc_free[0] = a
            a_free[0] = last
            x = layer_norm(X, par1_("ln2_g"), par1_("ln2_b"), a)
            par_free[:] = x
            x_ok[:] = x
            if l < DEPTH - 1:
                x_ready[:] = turn_x(X, x)

        a_free = [None]
        v_free = [None]

        def one_hots(src, prob, which, out_, base, ready):
            m8 = sm[:, base:base + 8]
            fi = sm[:, base + 8:base + 16]
            a = dve.do(lambda: nc.vector.max(m8, src), ready)
            a = dve.do(lambda: nc.vector.max_index(idx8[:, :], m8, src), a)
            a = dve.do(lambda: nc.vector.tensor_copy(fi, idx8[:, :]), a)
            for i in range(which):
                last = dve.do(lambda i=i: nc.vector.tensor_scalar(out_[i], const("iota8"), fi[:, i:i + 1], None, ALU.is_equal), a)
            return m8, last

        def route(lg, cb, ready):
            b0 = 160
            gp = sm[:, b0:b0 + 8]
            gmx, gz, gv = (sm[:, b0 + 8 + i:b0 + 9 + i] for i in range(3))
            emx, es, ev = (sm[:, b0 + 12 + i:b0 + 13 + i] for i in range(3))
            oh = sm[:, b0 + 16:b0 + 24]
            e8 = sm[:, b0 + 24:b0 + 32]
            h1, h2 = sm[:, b0 + 32:b0 + 40], sm[:, b0 + 40:b0 + 48]
            sel = sm[:, 256:288].rearrange("p (g e) -> p g e", g=NG)
            d = [ready]

            def step(fn, *w):
                d[0] = dve.do(fn, d[0], *w)

            def astep(fn):
                d[0] = act.do(fn, d[0])

            step(lambda: nc.vector.memset(gp, -1.0))
            step(lambda: nc.vector.tensor_reduce(gmx, lg[:, 0:NG], AX.X, ALU.max))
            step(lambda: nc.vector.tensor_scalar(gmx, gmx, -1.0, None, ALU.mult))
            astep(lambda: nc.scalar.activation(gp[:, 0:NG], lg[:, 0:NG], ACT.Exp, bias=gmx, accum_out=gz))
            _, d[0] = one_hots(gp, None, 1, [oh], b0 + 48, d[0])
            m8 = sm[:, b0 + 48:b0 + 56]
            step(lambda: nc.vector.reciprocal(gz, gz))
            step(lambda: nc.vector.tensor_tensor(gv, m8[:, 0:1], gz, ALU.mult))
            le = lg[:, NG:NG + NE].rearrange("p (g e) -> p g e", g=NG)
            step(lambda: nc.vector.tensor_tensor(sel, le, oh[:, 0:NG].unsqueeze(2).broadcast_to([P, NG, EPG]), ALU.mult))
            step(lambda: nc.vector.tensor_reduce(e8, sel.rearrange("p g e -> p e g"), AX.X, ALU.add))
            step(lambda: nc.vector.tensor_reduce(emx, e8, AX.X, ALU.max))
            step(lambda: nc.vector.tensor_scalar(emx, emx, -1.0, None, ALU.mult))
            astep(lambda: nc.scalar.activation(e8, e8, ACT.Exp, bias=emx, accum_out=es))
            step(lambda: nc.vector.reciprocal(es, es))
            step(lambda: nc.vector.tensor_scalar(e8, e8, es, None, ALU.mult))
            _, d[0] = one_hots(e8, None, 2, [h1, h2], b0 + 48, d[0])
            step(lambda: nc.vector.tensor_tensor(es, m8[:, 0:1], m8[:, 1:2], ALU.add))
            step(lambda: nc.vector.reciprocal(es, es))
            step(lambda: nc.vector.tensor_tensor(es, es, gv, ALU.mult))
            step(lambda: nc.vector.tensor_scalar(h1, h1, m8[:, 0:1], None, ALU.mult))
            step(lambda: nc.vector.scalar_tensor_tensor(h1, h2, m8[:, 1:2], h1, ALU.mult, ALU.add))
            step(lambda: nc.vector.tensor_scalar(h1, h1, es, None, ALU.mult))
            for g in range(NG):
                step(lambda g=g: nc.vector.tensor_scalar(cb[:, g * EPG:(g + 1) * EPG], h1, oh[:, g:g + 1], None, ALU.mult))

        def second_layer(l):
            src = par2[l * P2_N:(l + 1) * P2_N].partition_broadcast(P)
            par = load(pool, PAR[:, 0:P2_N], src, "l_par", par_free)
            h = rms_norm(H, X, par2_("attn_norm_2"), NORM_EPS, D, [*x_ok, par, *([h_free[0]] if h_free[0] else [])])
            xr = turn_x(H, h)
            h_free[0] = pe_last()
            CST_ = STA[:, 0:T * 416].rearrange("p (t c) -> p t c", t=T)
            done = projection("w_in_2", [(CST_[:, :, 0:256], 0, 256)], xr, a_free[0])
            done += projection("w_in_2", [(CST_[:, :, 256:416], 0, 160)], xr, a_free[0])
            a1 = rms_norm(CST_[:, :, 0:256], CST_[:, :, 0:256], par2_("mla_q_norm_2"), NORM_EPS, 256, done)
            a2 = rms_norm(CST_[:, :, 256:384], CST_[:, :, 256:384], par2_("mla_kv_norm_2"), NORM_EPS, 128, done)
            kr = rope(CST_[:, :, 384:416].unsqueeze(2), 1, 0, 16, *cs(32), done)
            CT = TMP2[:, 1024:1792].rearrange("p (k s) -> p k s", k=3)
            ct = turn_heads(CT, CST_[:, :, 0:384], 3, P, [*a1, *a2], None)
            QS = STB[:, 0:1536].rearrange("p (t c) -> p t c", t=T)
            KS = STB[:, 1536:3072].rearrange("p (t c) -> p t c", t=T)
            KS4 = KS.rearrange("p t (h d) -> p t h d", h=8)
            (w,), loaded = take("mla_w_q_up_2")
            qd = []
            for c in range(3):
                b = next_bank()
                v = bank[b][:, :].rearrange("p (t n) -> p t n", t=T)
                waits = [loaded, *ct, bank_free[b]]
                for t in range(T):
                    for k in range(2):
                        last = mm(v[:, t, :], CT[:, k, t * P:(t + 1) * P], w[:, k, c * 256:(c + 1) * 256], k == 0, k == 1, *waits)
                        waits = []
                bank_free[b] = copy(act, QS[:, :, c * 256:(c + 1) * 256], v, last, a_free[0])
                qd.append(bank_free[b])
            release(last)
            (w,), loaded = take("mla_w_kv_up_2")
            kd = []
            for c in range(4):
                b = next_bank()
                v = bank[b][:, :].rearrange("p (t n) -> p t n", t=T)
                waits = [loaded, bank_free[b]]
                for t in range(T):
                    last = mm(v[:, t, :], CT[:, 2, t * P:(t + 1) * P], w[:, 0, c * 256:(c + 1) * 256], True, True, *waits)
                    waits = []
                v4 = v.rearrange("p t (h d) -> p t h d", h=2)
                for t in range(T):
                    vd = V[:, t, c * P:(c + 1) * P].rearrange("p (h d) -> p h d", h=2)
                    copy(act, KS4[:, t, 2 * c:2 * c + 2, 0:64], v4[:, t, :, 0:64], last, a_free[0])
                    bank_free[b] = copy(act, vd, v4[:, t, :, 64:128], last, v_free[0])
                kd.append(bank_free[b])
            release(last)
            for t in range(T):
                kp = dve.do(lambda t=t: nc.vector.tensor_copy(
                    KS4[:, t, :, 64:96], CST_[:, t, 384:416].unsqueeze(1).broadcast_to([P, 8, 32])), kr, a_free[0])
            qr = rope(QS.rearrange("p t (h d) -> p t h d", h=8), 8, 64, 16, *cs(32), qd)
            MST = STA.rearrange("p (t c) -> p t c", t=T)
            mdone = []
            cst_free = kp
            for c in range(4):
                mdone += projection("w_in_2", [(MST[:, :, c * 256:(c + 1) * 256], 0, 256)], xr, cst_free, *ct)
            for c in range(2):
                mv = projection("w_in_2", [(V[:, :, 512 + c * 256:512 + (c + 1) * 256], 0, 256)], xr, v_free[0])
            QT = QKT[0:96, 0:8 * S].rearrange("p (k s) -> p k s", k=8)
            KT = QKT[0:96, 8 * S:16 * S].rearrange("p (k s) -> p k s", k=8)
            qt = turn_heads(QT, QS, 8, 96, qr, a_free[0])
            kt = turn_heads(KT, KS, 8, 96, [*kd, kp], a_free[0])
            stb_free = pe_last()
            mr = rope(MST.rearrange("p t (h d) -> p t h d", d=64), 16, 0, 8, *cs(16), mdone)
            RST = STB[:, 0:1024].rearrange("p (t c) -> p t c", t=T)
            rdone = []
            for c in range(2):
                rdone += projection("w_in_2", [(RST[:, :, c * 256:(c + 1) * 256], 0, 256)], xr, stb_free)
            rr = rope(RST.rearrange("p t (h d) -> p t h d", d=64), 8, 0, 32, *cs(64), rdone)
            rs = dve.do(lambda: nc.vector.tensor_scalar(RST[:, :, 256:512], RST[:, :, 256:512], 0.125, None, ALU.mult), rr)
            for c in range(4):
                rv = projection("w_in_2", [(V[:, :, 1024 + c * 256:1024 + (c + 1) * 256], 0, 256)], xr, v_free[0])
            start_fill("w_in_2", 12, xr)
            for t in range(T):
                o = causal_heads(t, 8, lambda i: QT[:, i, :], lambda i: KT[:, i, :],
                                 lambda i, k: V[:, k, i * 64:(i + 1) * 64], 64, 96 ** -0.5, [*qt, *kt])
            qk_free = pe_last()
            o0 = turn_o(0, o)
            MT = QKT[:, 0:8 * S].rearrange("p (k s) -> p k s", k=8)
            RT = QKT[:, 8 * S:12 * S].rearrange("p (k s) -> p k s", k=4)
            mt = turn_heads(MT, MST, 8, P, mr, qk_free)
            rt = turn_heads(RT, RST, 4, P, rs, qk_free)
            for t in range(T):
                o = causal_heads(t, 8, lambda i: MT[64 * (i % 2):64 * (i % 2) + 64, i // 2, :],
                                 lambda i: MT[64 * (i % 2):64 * (i % 2) + 64, 4 + i // 2, :],
                                 lambda i, k: V[:, k, 512 + i * 64:512 + (i + 1) * 64], 64, 0.125, mt)
            o1 = turn_o(1, o)
            dec = const("decay").rearrange("p (h k) -> p h k", h=4)
            for t in range(T):
                kl = P * (t + 1)
                d = scores(t, 4, lambda i: RT[64 * (i % 2):64 * (i % 2) + 64, i // 2, :],
                           lambda i: RT[64 * (i % 2):64 * (i % 2) + 64, 2 + i // 2, :], rt)
                fill()
                for i in range(4):
                    p_ = pos_of(i)
                    a = dve.do(lambda i=i, p_=p_, t=t, kl=kl: nc.vector.tensor_tensor(
                        SC[:, p_, 0:kl], scp[:, p_, 0:kl], dec[:, i, t * P:t * P + kl], ALU.mult), d, p_free[0])
                sc_free[0] = a
                b, last = weighted(t, 4, lambda i: SC[:, pos_of(i), :],
                                   lambda i, k: V[:, k, 1024 + i * P:1024 + (i + 1) * P], P, [a])
                fill()
                ob = O[:, t, :].rearrange("p (h d) -> p h d", h=4)
                o = dve.do(lambda ob=ob, b=b: nc.vector.tensor_copy(ob, bank[b][:, :].rearrange("p (h d) -> p h d", h=4)),
                           last, o_free[0])
                bank_free[b] = o
                mean, var, ok = norm_stats(ob, 4, P, 64, GN_EPS, False, o)
                for h in range(4):
                    oh = ob[:, h, :]
                    a = dve.do(lambda oh=oh, var=var, mean=mean, h=h: nc.vector.tensor_scalar(
                        oh, oh, mean[:, h:h + 1], var[:, h:h + 1], ALU.subtract, ALU.mult), ok)
                ot = O[:, t, :]
                a = dve.do(lambda ot=ot: nc.vector.tensor_tensor(ot, ot, par2_("ret_gn_w_2"), ALU.mult), a)
                a = dve.do(lambda ot=ot: nc.vector.tensor_tensor(ot, ot, par2_("ret_gn_b_2"), ALU.add), a)
                rg = V[:, t, 1536:2048]
                th = TMP2[:, 0:512]
                s_ = act.do(lambda rg=rg: nc.scalar.activation(th, rg, ACT.Tanh, scale=0.5), rv, rope_done[-1:], a)
                s_ = dve.do(lambda rg=rg: nc.vector.scalar_tensor_tensor(th, th, 1.0, rg, ALU.add, ALU.mult), s_)
                o = dve.do(lambda ot=ot: nc.vector.scalar_tensor_tensor(ot, th, 0.5, ot, ALU.mult, ALU.mult), s_, a)
            v_free[0] = pe_last()
            v_free2 = o
            fill(12)
            o2 = turn_o(2, o)
            m = branches(("w_branch_mla_2", "w_branch_moba_2", "w_branch_ret_2"), (o0, o1, o2))
            ot_free[0] = pe_last()
            x = mix_out("w_out_2", 1.0, [*m, *x_ok])
            h_free[0] = pe_last()
            h = rms_norm(H, X, par2_("mlp_norm_2"), NORM_EPS, D, [*x, h_free[0]])
            xt = turn_x(H, h)
            h_free[0] = pe_last()
            UT = A[:, 0:32 * S].rearrange("p (k s) -> p k s", k=32)
            ud = []
            for j in range(16):
                (w,), loaded = take("w_mlp_up_2")
                b, v, last = features_major(w, 0, XT, [loaded, *xt])
                release(last)
                u = UT[:, 2 * j:2 * j + 2, :]
                bank_free[b] = act.do(lambda u=u, v=v: nc.scalar.activation(u, v, ACT.Relu), last)
                ud.append(dve.do(lambda u=u: nc.vector.tensor_tensor(u, u, u, ALU.mult), bank_free[b]))
            yv = scp[:, :, :].rearrange("p a s -> p (a s)").rearrange("p (t n) -> p t n", t=T)
            for j in range(16):
                (w,), loaded = take("w_mlp_down_2")
                waits = [loaded, ud[j], sc_free[0]]
                for k in range(2):
                    for t in range(T):
                        for n in range(2):
                            last = mm(yv[:, t, n * 512:(n + 1) * 512], UT[:, 2 * j + k, t * P:(t + 1) * P],
                                      w[:, k, n * 512:(n + 1) * 512], j == 0 and k == 0, j == 15 and k == 1, *waits)
                            waits = []
                release(last)
            x = []
            for t in range(T):
                x.append(dve.do(lambda t=t: nc.vector.tensor_tensor(X[:, t, :], X[:, t, :], yv[:, t, :], ALU.add), last))
            sc_free[0] = x[-1]
            a_free[0] = last
            x_ok[:] = x
            par_free[:] = [*h, x[-1]]
            if l == DEPTH - 1:
                y = rms_norm(H, X, par2_("final_norm_2"), NORM_EPS, D, [*x, h_free[0]])
                for t in range(T):
                    o = load(sp, out[t], H[:, t, :], "l_out", y)
                sp.items.append((lambda: nc.sync.nop(), [o], Token(None)))

        for l in range(DEPTH):
            first_layer(l)
        for l in range(DEPTH):
            second_layer(l)
        assert taken[0] == len(STREAM)
        for q in (pe, dve, act, pool, sp):
            q.number()
        block = ctx.enter_context(nc.Block())

        @block.sync
        def _(e):
            sp.emit()

        @block.tensor
        def _(e):
            pe.emit()

        @block.vector
        def _(e):
            dve.emit()

        @block.scalar
        def _(e):
            act.emit()

        @block.gpsimd
        def _(e):
            pool.emit()


def constants():
    c = {}
    c["ident"] = np.eye(P)
    q = np.arange(P)
    c["caus"] = np.where(q[None, :] <= q[:, None], 0.0, NEG)
    lg = np.log(np.float32(1.0) - np.float32(2.0) ** (-5.0 - np.arange(4, dtype=np.float32))).astype(np.float64)
    s = np.arange(S)
    diff = s[:, None] - s[None, :]
    dec = np.where(diff[None] >= 0, np.exp(lg[:, None, None] * np.maximum(diff, 0)[None]), 0.0)
    dec = dec.reshape(4, T, P, S)
    c["decay"] = np.concatenate([dec[:, 0, :, 0:P], dec[:, 1]], 2).transpose(1, 0, 2).reshape(P, -1)

    def inv(dim, theta):
        return (np.float32(1.0) / (np.float32(theta) ** (np.arange(0, dim, 2, dtype=np.float32) / np.float32(dim)))).astype(np.float32)

    c["invf"] = np.broadcast_to(inv(16, 500000.0), (P, 8))
    for dim, theta in ((16, 500000.0), (32, 500000.0), (64, 10000.0)):
        ang = (np.arange(S, dtype=np.float32)[:, None] * inv(dim, theta)[None, :]).astype(np.float32).astype(np.float64)
        co, si = np.cos(ang), np.sin(ang)
        c[f"c{dim}"] = np.concatenate([co, co], 1).reshape(T, P, dim).transpose(1, 0, 2).reshape(P, -1)
        c[f"s{dim}"] = np.concatenate([-si, si], 1).reshape(T, P, dim).transpose(1, 0, 2).reshape(P, -1)
    c["iota8"] = np.broadcast_to(np.arange(8), (P, 8))
    c["nhalf"] = np.full((P, 8), -0.5)
    return np.ascontiguousarray(np.concatenate([np.asarray(c[n], np.float32).reshape(P, m) for n, m in C_TABLE], 1))


def kernel(**inputs):
    import numpy as _np
    import concourse.bacc as _bacc
    from concourse import mybir as _mybir
    from concourse.bass_utils import run_bass_kernel_spmd as _run

    a = {k: _np.asarray(v) for k, v in inputs.items()}
    arrays = {}
    stream = _np.empty(AT[-1], _np.float32)
    for i, block in enumerate(STREAM):
        at = 0
        dst = stream[AT[i]:AT[i + 1]].reshape(P, -1)
        for name, idx, k0, kt, c0, c1 in block:
            w = a[name][idx].reshape(-1, P, a[name].shape[-1])[k0:k0 + kt, :, c0:c1]
            n = kt * (c1 - c0)
            dst[:, at:at + n].reshape(P, kt, c1 - c0)[:] = w.transpose(1, 0, 2)
            at += n
    arrays["wts"] = stream
    flat = lambda name, l: a[name].reshape(-1) if name == "final_norm_2" else a[name][l].reshape(-1)
    arrays["par1"] = _np.concatenate([flat(n, l) for l in range(DEPTH) for n, _ in P1])
    arrays["par2"] = _np.concatenate([flat(n, l) for l in range(DEPTH) for n, _ in P2])
    arrays["consts"] = constants().reshape(-1)
    arrays["pos"] = _np.ascontiguousarray(a["positions"].reshape(T, P).T)
    x = a["x"].reshape(S, D)
    arrays["x0"] = _np.ascontiguousarray(x.reshape(T, P, D).transpose(1, 0, 2))
    arrays["x0T"] = _np.ascontiguousarray(x.T.reshape(KD, P, S).transpose(1, 0, 2))
    p = a["p"].reshape(DEPTH, S, 256)
    arrays["pT"] = _np.ascontiguousarray(p.transpose(0, 2, 1).reshape(DEPTH, 2, P, S).transpose(0, 2, 1, 3))

    nc = _bacc.Bacc("TRN2", target_bir_lowering=False, num_devices=1)
    args = {n: nc.dram_tensor(n, v.shape, _mybir.dt.from_np(v.dtype), kind="ExternalInput").ap() for n, v in arrays.items()}
    out = nc.dram_tensor("out", (T, P, D), _mybir.dt.float32, kind="ExternalOutput").ap()
    build(nc, out=out, **args)
    r = _run(nc, [arrays], core_ids=[0])
    return r.results[0]["out"].reshape(1, S, D)
```

```python
import math
from contextlib import ExitStack

import numpy as np
import concourse.bass as bass
from concourse import mybir

F32 = mybir.dt.float32
I32 = mybir.dt.int32
U32 = mybir.dt.uint32
ALU = mybir.AluOpType
ACT = mybir.ActivationFunctionType
AX = mybir.AxisListType

P = 128
S = 256
T = S // P
D = 1024
KD = D // P
DEPTH = 2
NG, EPG, NE, DE = 4, 8, 32, 256
TOPK = 64
ALPHA = (2 * DEPTH) ** 0.25
LN_EPS = 1e-5
NORM_EPS = 1e-6
GN_EPS = 1e-5
NEG = -1e30
GONE = -3e38
MAGIC = 12582912.0
BLK = 2048
RING = 4
DFF = 4096

W1 = dict(zip(("dq", "dk", "dv", "sq", "sk", "sv", "iq", "ik", "iw", "ga", "gb"),
              np.cumsum([0, 512, 512, 512, 512, 512, 512, 512, 64, 8, 1024]).tolist()))
W2 = dict(zip(("cq", "ckv", "kr", "mq", "mk", "mv", "rq", "rk", "rv", "rg", "g0", "g1", "g2"),
              np.cumsum([0, 256, 128, 32, 512, 512, 512, 256, 256, 512, 512, 1024, 1024]).tolist()))

P1 = [("ln1_g", D), ("ln1_b", D), ("ln2_g", D), ("ln2_b", D), ("diff_subln_g", 128),
      ("b_route_group", NG), ("b_route_expert", NE), ("diff_lambda", 256)]
P2 = [("attn_norm_2", D), ("mlp_norm_2", D), ("mla_q_norm_2", 256), ("mla_kv_norm_2", 128),
      ("ret_gn_w_2", 512), ("ret_gn_b_2", 512), ("final_norm_2", D)]


def offsets(table):
    at, out = 0, {}
    for name, n in table:
        out[name] = (at, n)
        at += n
    return out, at


P1_AT, P1_N = offsets(P1)
P2_AT, P2_N = offsets(P2)

CAP = 64
SLOTS = 2 * S
C_TABLE = [("ident", 128), ("caus", 128), ("invf", 8), ("iota8", 8), ("nhalf", 8)]
C1_TABLE = [("before", 128), ("iota", SLOTS), ("one", 1)]
C2_TABLE = [("decay", 4 * 384), ("c16", 2 * 16), ("s16", 2 * 16), ("c32", 2 * 32), ("s32", 2 * 32),
            ("c64", 2 * 64), ("s64", 2 * 64)]
C_AT, C_N = offsets(C_TABLE)
C1_AT, C1_N = offsets(C1_TABLE)
C2_AT, C2_N = offsets(C2_TABLE)
CX_AT = {n: (C_N + a, m) for at in (C1_AT, C2_AT) for n, (a, m) in at.items()} | C_AT


def blocks(layer, first):
    out = []

    def cols(name, idx, kt, c0, c1, step):
        for c in range(c0, c1, step):
            out.append([(name, idx, 0, kt, c, min(c + step, c1))])

    if first:
        w = ("w_in", (layer,), KD)
        cols(*w, W1["iq"], W1["ik"], 256)
        cols(*w, W1["ik"], W1["ga"], 72)
        for n in ("sq", "sk", "sv", "dq", "dk", "dv"):
            cols(*w, W1[n], W1[n] + 512, 256)
        cols(*w, W1["ga"], W1["ga"] + 2 * D, 256)
        cols("w_branch_diff", (layer,), 4, 0, D, 512)
        cols("w_branch_dsa", (layer,), 4, 0, D, 512)
        cols("w_out", (layer,), KD, 0, D, 256)
        out.append([("w_route_group", (layer,), 0, KD, 0, NG), ("w_route_expert", (layer,), 0, KD, 0, NE)])
        cols("w_ple_gate", (layer,), KD, 0, D, 256)
        cols("w_ple", (layer,), 2, 0, D, 1024)
        for e in range(NE + 1):
            if e < NE:
                idx = (layer, e // EPG, e % EPG)
                cols("w_exp_gate", idx, KD, 0, DE, DE)
                cols("w_exp_up", idx, KD, 0, DE, DE)
            if e:
                cols("w_exp_down", (layer, (e - 1) // EPG, (e - 1) % EPG), 2, 0, D, D)
    else:
        w = ("w_in_2", (layer,), KD)
        cols(*w, W2["cq"], W2["ckv"], 256)
        cols(*w, W2["ckv"], W2["mq"], 160)
        cols("mla_w_q_up_2", (layer,), 2, 0, 768, 768)
        cols("mla_w_kv_up_2", (layer,), 1, 0, 1024, 1024)
        for n, m in (("mq", 512), ("mk", 512), ("mv", 512), ("rq", 256), ("rk", 256), ("rv", 512), ("rg", 512)):
            cols(*w, W2[n], W2[n] + m, 256)
        cols(*w, W2["g0"], W2["g0"] + 3 * D, 256)
        for n in ("w_branch_mla_2", "w_branch_moba_2", "w_branch_ret_2"):
            cols(n, (layer,), 4, 0, D, 512)
        cols("w_out_2", (layer,), KD, 0, D, 256)
        cols("w_mlp_up_2", (layer,), KD, 0, DFF, 256)
        for k in range(0, DFF // P, 2):
            out.append([("w_mlp_down_2", (layer,), k, 2, 0, D)])
    return out


STREAM = [b for first in (True, False) for layer in range(DEPTH) for b in blocks(layer, first)]


def width(block):
    return sum(kt * (c1 - c0) for _, _, _, kt, c0, c1 in block)


AT = np.cumsum([0] + [P * width(b) for b in STREAM]).tolist()
WHERE = {b[0][:2]: i for i, b in enumerate(STREAM) if b[0][0].startswith("w_exp_")}


class Token:

    def __init__(self, sem):
        self.sem, self.value, self.marked = sem, None, False


class Queue:

    def __init__(self, eng, sem):
        self.eng, self.sem, self.items = eng, sem, []

    def do(self, fn, *waits):
        token = Token(self.sem)
        flat = []
        for w in waits:
            flat += w if isinstance(w, list) else [w] if w is not None else []
        for w in flat:
            w.marked = True
        self.items.append((fn, flat, token))
        return token

    def number(self):
        n = 0
        for _, _, token in self.items:
            if isinstance(token, Token) and token.value is None and token.marked:
                n += 1
                token.value = n

    def branch(self, flag, other, *waits):
        self.do(None, *waits)
        fn, flat, token = self.items.pop()
        self.items.append(((flag, other), flat, token))

    def emit(self, seen=None):
        seen = dict(seen or {})
        for fn, waits, token in self.items:
            for w in waits:
                if seen.get(id(w.sem), 0) < w.value:
                    self.eng.wait_ge(w.sem, w.value)
                    seen[id(w.sem)] = w.value
            if isinstance(fn, tuple):
                flag = self.eng.value_load(fn[0], min_val=0, max_val=1)
                with self.eng.If(flag > 0):
                    fn[1].emit(seen)
                continue
            ins = fn()
            if token.marked and token.sem is self.sem:
                ins.then_inc(self.sem, 1)


class DmaDone:

    def __init__(self, sem, value):
        self.sem, self.value, self.marked = sem, value, True


def build(nc, wts, par1, par2, consts, pos, x0, x0T, pT, out):
    ctx = ExitStack()
    with ctx:
        def sb(name, *shape, dt=F32):
            return ctx.enter_context(nc.sbuf_tensor(name, [P, *shape], dt))

        def sem(name):
            return ctx.enter_context(nc.semaphore(name))

        pe = Queue(nc.tensor, sem("pe"))
        dve = Queue(nc.vector, sem("dve"))
        act = Queue(nc.scalar, sem("act"))
        pool = Queue(nc.gpsimd, sem("pool"))
        sp = Queue(nc.sync, sem("sp"))

        ring = [sb(f"ring{i}", BLK) for i in range(RING)]
        ring_sem = [sem(f"ring_sem{i}") for i in range(RING)]
        X = sb("X", T, D)
        XT = sb("XT", KD, S)
        A = sb("A", 36 * 256)
        STA = A[:, 0:2048]
        STB = A[:, 2048:5120]
        QKT = A[:, 5120:9216]
        V = sb("V", T, 2048)
        GT = sb("GT", 3, KD, S)
        SC = sb("SC", 8, S)
        PT = sb("PT", 8, 2, P)
        O = sb("O", T, 512)
        OT = sb("OT", 3, 4, S)
        H = sb("H", T, D)
        TMP = sb("TMP", 1024)
        TMP2 = sb("TMP2", 1792)
        PAR = sb("PAR", max(P1_N, P2_N))
        CST = sb("CST", C_N + max(C1_N, C2_N))
        sm = sb("sm", 512)
        bias = TMP[:, 512:1024].rearrange("p (t s) -> p t s", t=T)
        work = TMP2[:, 1024:1536].rearrange("p (t s) -> p t s", t=T)
        comb = sb("comb", T, NE)
        OH = sb("OH", 2, T, NE)
        MK = sb("MK", T, NE)
        PS = sb("PS", T, NE)
        OFF = sb("OFF", NE)
        offi = sb("offi", NE, dt=I32)
        flag = sb("flag", 1, dt=I32)
        rt = sb("rt", 32)
        posi = sb("posi", T, dt=I32)
        idx8 = sb("idx8", 8, dt=U32)
        ropeb = sb("ropeb", 2, T, 16)

        def const(name):
            a, n = CX_AT[name]
            return CST[:, a:a + n]

        def par1_(name):
            a, n = P1_AT[name]
            return PAR[:, a:a + n]

        def par2_(name):
            a, n = P2_AT[name]
            return PAR[:, a:a + n]

        ident = const("ident")

        scp = ctx.enter_context(nc.psum_tensor("scp", [P, 8, S], F32))
        bank = [ctx.enter_context(nc.psum_tensor(f"bank{i}", [P, 512], F32)) for i in range(4)]

        dma_n = {}

        def load(q, dst, src, name, *waits):
            if name not in dma_n:
                dma_n[name] = [sem(name), 0]
            s = dma_n[name]
            s[1] += 16
            q.items.append((lambda: q.eng.dma_start(dst, src).then_inc(s[0], 16),
                            [w for v in waits for w in (v if isinstance(v, list) else [v])], DmaDone(s[0], s[1])))
            for w in q.items[-1][1]:
                w.marked = True
            return DmaDone(s[0], s[1])

        sent, taken = [0], [0]
        freed = []

        def send_block():
            i = sent[0]
            n = width(STREAM[i])
            src = wts[AT[i]:AT[i + 1]].rearrange("(p n) -> p n", p=P)
            slot, turn = i % RING, i // RING + 1
            waits = [freed[i - RING]] if i >= RING else []
            for w in waits:
                w.marked = True
            sp.items.append((lambda: nc.sync.dma_start(ring[slot][:, 0:n], src).then_inc(ring_sem[slot], 16),
                             waits, DmaDone(ring_sem[slot], 16 * turn)))
            sent[0] += 1

        def take(*names):
            i = taken[0]
            taken[0] += 1
            assert tuple(b[0] for b in STREAM[i]) == names, (names, STREAM[i])
            at, views = 0, []
            for _, _, _, kt, c0, c1 in STREAM[i]:
                n = kt * (c1 - c0)
                views.append(ring[i % RING][:, at:at + n].rearrange("p (k n) -> p k n", k=kt))
                at += n
            return views, DmaDone(ring_sem[i % RING], 16 * (i // RING + 1))

        def release(token):
            freed.append(token)
            assert len(freed) == taken[0]
            if sent[0] < len(STREAM):
                send_block()

        c_in = [load(sp, CST[:, 0:C_N], consts[0:P * C_N].rearrange("(p n) -> p n", p=P), "l_cst"),
                load(sp, CST[:, C_N:C_N + C1_N], consts[P * C_N:P * (C_N + C1_N)].rearrange("(p n) -> p n", p=P), "l_cst1"),
                load(sp, posi[:, :], pos, "l_pos")]
        xt_in = load(sp, XT[:, :, :], x0T, "l_xt")
        x_in = load(sp, X[:, :, :], x0, "l_x")
        for _ in range(RING):
            send_block()

        bank_free = [None] * 4
        bank_at = [0]

        def next_bank():
            b = bank_at[0] % 4
            bank_at[0] += 1
            return b

        turn = [0]

        def copy(q, dst, src, *waits):
            if q is act:
                return act.do(lambda: nc.scalar.copy(dst, src), *waits)
            return dve.do(lambda: nc.vector.tensor_copy(dst, src), *waits)

        def either():
            turn[0] += 1
            return act if turn[0] % 2 else dve

        def mm(dst, lhsT, rhs, start, stop, *waits):
            return pe.do(lambda: nc.tensor.matmul(dst, lhsT, rhs, start=start, stop=stop), *waits)

        def tr(dst, src, *waits):
            return pe.do(lambda: nc.tensor.transpose(dst, src, ident), *waits)

        def tokens_major(name, src, src_ready, kt=KD):
            (w,), loaded = take(name)
            n = w.shape[2]
            b = next_bank()
            v = bank[b][:, 0:T * n].rearrange("p (t n) -> p t n", t=T)
            waits = [loaded, src_ready, bank_free[b]]
            for t in range(T):
                for k in range(kt):
                    last = mm(v[:, t, :], src[:, k, t * P:(t + 1) * P], w[:, k, :], k == 0, k == kt - 1, *waits)
                    waits = []
            release(last)
            return b, v, last

        def features_major(w, m0, src, waits, kt=KD):
            b = next_bank()
            v = bank[b][:, :].rearrange("p (m s) -> p m s", m=2)
            waits = [*waits, bank_free[b]]
            for m in range(2):
                for k in range(kt):
                    c = (m0 + m) * P
                    last = mm(v[:, m, :], w[:, k, c:c + P], src[:, k, :], k == 0, k == kt - 1, *waits)
                    waits = []
            return b, v, last

        def transposes(dst, pieces, ready, free):
            done = []
            for i0 in range(0, len(pieces), 4):
                part = pieces[i0:i0 + 4]
                b = next_bank()
                waits = [ready, bank_free[b]]
                waits = [w for v in waits if v is not None for w in (v if isinstance(v, list) else [v])]
                c = part[0].shape[1]
                for j, src in enumerate(part):
                    last = tr(bank[b][0:c, j * P:(j + 1) * P], src, *waits)
                    waits = []
                q = either()
                bank_free[b] = copy(q, dst(i0, len(part)), bank[b][0:c, 0:len(part) * P], last, free)
                done.append(bank_free[b])
            return done

        def rope(st, heads, lo, hw, cc, ss, ready):
            n = T * heads * 2 * hw
            a = TMP[:, 0:n].rearrange("p (t h d) -> p t h d", t=T, h=heads)
            b = TMP2[:, 0:n].rearrange("p (t h d) -> p t h d", t=T, h=heads)

            def table(v, d0, d1):
                return v[:, :, d0:d1].unsqueeze(2).broadcast_to([P, T, heads, d1 - d0])

            toks = []
            for t in range(T):
                def tab(v, d0, d1, t=t):
                    return v[:, t, d0:d1].unsqueeze(1).broadcast_to([P, heads, d1 - d0])
                x = st[:, t, :, lo:lo + 2 * hw]
                x1 = st[:, t, :, lo:lo + hw]
                x2 = st[:, t, :, lo + hw:lo + 2 * hw]
                o1 = dve.do(lambda t=t, x=x: nc.vector.tensor_tensor(a[:, t], x, tab(cc, 0, 2 * hw, t), ALU.mult),
                            ready, rope_done[-1:])
                dve.do(lambda t=t, x2=x2: nc.vector.tensor_tensor(b[:, t, :, 0:hw], x2, tab(ss, 0, hw, t), ALU.mult))
                o3 = dve.do(lambda t=t, x1=x1: nc.vector.tensor_tensor(b[:, t, :, hw:2 * hw], x1, tab(ss, hw, 2 * hw, t), ALU.mult))
                toks.append((x, o1, o3))
            for t, (x, o1, o3) in enumerate(toks):
                last = dve.do(lambda t=t, x=x: nc.vector.tensor_tensor(x, a[:, t], b[:, t], ALU.add), o1, o3)
            rope_done.append(last)
            return last

        rope_done = []

        def pos_of(i):
            return ((i % 2) + 2 * (i // 4)) * 2 + (i // 2) % 2

        sc_free = [None]
        p_free = [None]
        pt_free = [None]
        o_free = [None]

        def scores(t, heads, q_of, k_of, ready):
            kl = P * (t + 1)
            waits = [ready, sc_free[0]]
            for i in range(heads):
                last = mm(scp[:, pos_of(i), 0:kl], q_of(i)[:, t * P:(t + 1) * P], k_of(i)[:, 0:kl],
                          True, True, *waits)
                waits = []
            return last

        def softmax_parts(t, heads, scale, done, extra=None):
            kl = P * (t + 1)
            if extra is None:
                v = scp[:, 0:heads, t * P:kl]
                m = const("caus").unsqueeze(1).broadcast_to([P, heads, P])
                a = dve.do(lambda: nc.vector.tensor_tensor(v, v, m, ALU.add), done)
            else:
                v = scp[:, 0:heads, 0:kl]
                m = bias[:, t, 0:kl].unsqueeze(1).broadcast_to([P, heads, kl])
                a = dve.do(lambda: nc.vector.tensor_tensor(v, v, m, ALU.add), done, extra)
            mx = sm[:, 0:8]
            nb = sm[:, 8 + 8 * t:16 + 8 * t]
            z = sm[:, 24 + 8 * t:32 + 8 * t]
            rz = sm[:, 40 + 8 * t:48 + 8 * t]
            b = dve.do(lambda: nc.vector.tensor_reduce(mx[:, 0:heads], scp[:, 0:heads, 0:kl], AX.X, ALU.max), a)
            c = dve.do(lambda: nc.vector.tensor_scalar(nb, mx, -scale, None, ALU.mult), b)
            for i in range(heads):
                e = act.do(lambda i=i: nc.scalar.activation(SC[:, i, 0:kl], scp[:, i, 0:kl], ACT.Exp,
                                                            bias=nb[:, i:i + 1], scale=scale,
                                                            accum_out=z[:, i:i + 1]), c, p_free[0])
            sc_free[0] = e
            r = dve.do(lambda: nc.vector.reciprocal(rz, z), e)
            return e, r, rz

        def weighted(t, heads, p_of, v_of, vw, p_ready):
            nk = t + 1
            done = []
            pieces = [p_of(i)[:, k * P:(k + 1) * P] for i in range(heads) for k in range(nk)]
            flat = PT[:, :, :, :].rearrange("p h k q -> p (h k q)")
            done = transposes(lambda i0, n: flat[:, i0 * P:(i0 + n) * P], pieces, p_ready, pt_free[0])
            p_free[0] = pe_last()
            b = next_bank()
            waits = [*done, bank_free[b]]
            for i in range(heads):
                for k in range(nk):
                    j = i * nk + k
                    last = mm(bank[b][:, i * vw:(i + 1) * vw], flat[:, j * P:(j + 1) * P], v_of(i, k),
                              k == 0, k == nk - 1, *waits)
                    waits = []
            pt_free[0] = last
            return b, last

        def pe_last():
            return pe.items[-1][2]

        def norm_stats(src, groups, n, base, eps, rms, ready):
            chunk = min(n, 512)
            st = sm[:, 128:128 + 12 * max(1, groups)]
            last = None
            nch = n // chunk
            for g in range(groups):
                for c in range(nch):
                    o = st[:, (g * nch + c) * 6:(g * nch + c) * 6 + 6]
                    s_ = src[:, g, c * chunk:(c + 1) * chunk]
                    last = dve.do(lambda o=o, s_=s_: nc.vector.bn_stats(o, s_), ready if last is None else None,
                                  stat_free[0] if last is None else None)
            mv = sm[:, base:base + 2 * groups]
            for g in range(groups):
                i_ = st[:, g * nch * 6:(g + 1) * nch * 6]
                last2 = dve.do(lambda g=g, i_=i_: nc.vector.bn_aggr(mv[:, 2 * g:2 * g + 2], i_), last)
            stat_free[0] = last2
            mean = mv.rearrange("p (g c) -> p g c", c=2)[:, :, 0]
            var = mv.rearrange("p (g c) -> p g c", c=2)[:, :, 1]
            if rms:
                sq = sm[:, 120:120 + groups]
                a = dve.do(lambda: nc.vector.tensor_tensor(sq, mean, mean, ALU.mult), last2)
                last2 = dve.do(lambda: nc.vector.tensor_tensor(var, var, sq, ALU.add), a)
            e_ = dve.do(lambda: nc.vector.tensor_scalar(var, var, eps, None, ALU.add), last2)
            return mean, var, pool.do(lambda: nc.gpsimd.tensor_tensor(var, var, const("nhalf")[:, 0:groups], ALU.pow), e_)

        stat_free = [None]

        def rms_norm(dst, src, g, eps, n, ready, base=64):
            last = []
            for t in range(T):
                mean, var, ok = norm_stats(src[:, t:t + 1, :], 1, n, base + 2 * t, eps, True, ready)
                last.append(dve.do(lambda t=t, var=var: nc.vector.scalar_tensor_tensor(
                    dst[:, t, :], src[:, t, :], var, g, ALU.mult, ALU.mult), ok))
            return last

        def layer_norm(x, g, b, ready):
            last = []
            for t in range(T):
                mean, var, ok = norm_stats(x[:, t:t + 1, :], 1, D, 64 + 2 * t, LN_EPS, False, ready)
                a = dve.do(lambda t=t, mean=mean, var=var: nc.vector.tensor_scalar(
                    x[:, t, :], x[:, t, :], mean, var, ALU.subtract, ALU.mult), ok)
                a = dve.do(lambda t=t: nc.vector.tensor_tensor(x[:, t, :], x[:, t, :], g, ALU.mult), a)
                last.append(dve.do(lambda t=t: nc.vector.tensor_tensor(x[:, t, :], x[:, t, :], b, ALU.add), a))
            return last

        def turn_x(src, ready):
            done = []
            for c in range(0, KD, 2):
                pieces = [src[:, t, (c + j) * P:(c + j + 1) * P] for j in range(2) for t in range(T)]
                dst = XT[:, c:c + 2, :].rearrange("p k s -> p (k s)")
                done += transposes(lambda i0, n, dst=dst: dst, pieces, ready, None)
            return done

        fill_n = [0, 0]
        fill_src = [None]
        fill_name = [None]
        gate_done = []

        def start_fill(name, n, src_ready):
            fill_n[:] = [0, n]
            fill_src[0] = src_ready
            fill_name[0] = name
            gate_done.clear()

        def fill(n=1):
            for _ in range(n):
                if fill_n[0] == fill_n[1]:
                    return
                j = fill_n[0]
                fill_n[0] += 1
                (w,), loaded = take(fill_name[0])
                b, v, last = features_major(w, 0, XT, [loaded, fill_src[0]])
                release(last)
                dst = GT[:, j // 4, 2 * (j % 4):2 * (j % 4) + 2, :]
                bank_free[b] = act.do(lambda dst=dst, v=v: nc.scalar.activation(dst, v, ACT.Tanh, scale=0.5),
                                      last, merged_read[0])
                gate_done.append(bank_free[b])

        merged_read = [None]

        def projection(name, dsts, src_ready, *free, kt=KD, src=None):
            b, v, last = tokens_major(name, XT if src is None else src, src_ready, kt=kt)
            done = []
            q = act
            for dst, c0, c1 in dsts:
                tok = copy(q, dst, v[:, :, c0:c1], last, *free)
                done.append(tok)
            bank_free[b] = done[-1]
            return done

        MG = H[:, :, :].rearrange("p t d -> p (t d)").rearrange("p (k s) -> p k s", k=KD)

        def branches(names, ready):
            done = [None] * 4
            for n, name in enumerate(names):
                for half in range(2):
                    (w,), loaded = take(name)
                    for m in range(2):
                        b, v, last = features_major(w, 2 * m, OT[:, n], [loaded, ready[n]], kt=4)
                        c = 4 * half + 2 * m
                        g = GT[:, n, c:c + 2, :]
                        dst = g if n else MG[:, c:c + 2, :]
                        a = dve.do(lambda g=g, v=v, dst=dst: nc.vector.scalar_tensor_tensor(
                            dst, g, 1.0, v, ALU.add, ALU.mult), last, list(gate_done), h_free[0])
                        bank_free[b] = a
                        if n:
                            M = MG[:, c:c + 2, :]
                            a = dve.do(lambda M=M, g=g: nc.vector.tensor_tensor(M, M, g, ALU.add), a, done[2 * half + m])
                        done[2 * half + m] = a
                    release(last)
            merged_read[0] = done[-1]
            return done

        h_free = [None]

        def mix_out(name, scale, ready):
            done = []
            for c in range(4):
                b, v, last = tokens_major(name, MG, ready)
                xs = X[:, :, c * 256:(c + 1) * 256]
                if scale != 1.0:
                    a = dve.do(lambda xs=xs: nc.vector.tensor_scalar(xs, xs, scale, None, ALU.mult), last)
                else:
                    a = last
                bank_free[b] = dve.do(lambda xs=xs, v=v: nc.vector.scalar_tensor_tensor(
                    xs, v, 0.5, xs, ALU.mult, ALU.add), a, last)
                done.append(bank_free[b])
            return done

        def cs(n):
            return (const(f"c{n}").rearrange("p (t d) -> p t d", t=T), const(f"s{n}").rearrange("p (t d) -> p t d", t=T))

        posf = sm[:, 100:102]
        ang = TMP[:, 0:16].rearrange("p (t d) -> p t d", t=T)
        kk = TMP[:, 16:32].rearrange("p (t d) -> p t d", t=T)
        r = TMP[:, 32:48].rearrange("p (t d) -> p t d", t=T)
        ab = TMP[:, 48:64].rearrange("p (t d) -> p t d", t=T)
        a = dve.do(lambda: nc.vector.tensor_copy(posf, posi[:, :]), c_in)
        for t in range(T):
            a2 = dve.do(lambda t=t: nc.vector.tensor_scalar(ang[:, t, :], const("invf"), posf[:, t:t + 1], None, ALU.mult), a)
        a = dve.do(lambda: nc.vector.tensor_scalar(kk, ang, 1.0 / (2 * math.pi), MAGIC, ALU.mult, ALU.add), a2)
        a = dve.do(lambda: nc.vector.tensor_scalar(kk, kk, -MAGIC, None, ALU.add), a)
        parts, rest = [], 2 * math.pi
        for bits in (4, 12, 20):
            c = math.floor(rest * 2 ** bits) / 2 ** bits
            parts.append(c)
            rest -= c
        parts.append(rest)
        src_ = ang
        for c in parts:
            a = dve.do(lambda c=c, src_=src_: nc.vector.scalar_tensor_tensor(r, kk, -c, src_, ALU.mult, ALU.add), a)
            src_ = r
        a = dve.do(lambda: nc.vector.tensor_scalar(r, r, -3.1415925, 3.1415925, ALU.max, ALU.min), a)
        b_ = dve.do(lambda: nc.vector.tensor_scalar(ab, r, -1.0, None, ALU.mult), a)
        b_ = dve.do(lambda: nc.vector.tensor_tensor(ab, ab, r, ALU.max), b_)
        b_ = dve.do(lambda: nc.vector.tensor_scalar(ab, ab, -1.0, math.pi / 2, ALU.mult, ALU.add), b_)
        RC, RS = ropeb[:, 0], ropeb[:, 1]
        e1 = act.do(lambda: nc.scalar.activation(RS[:, :, 8:16], r, ACT.Sin), a)
        e2 = act.do(lambda: nc.scalar.activation(RC[:, :, 0:8], ab, ACT.Sin), b_)
        dve.do(lambda: nc.vector.tensor_scalar(RS[:, :, 0:8], RS[:, :, 8:16], -1.0, None, ALU.mult), e1)
        rope_ready = dve.do(lambda: nc.vector.tensor_copy(RC[:, :, 8:16], RC[:, :, 0:8]), e2)
        rope_done.append(rope_ready)

        x_ready = [xt_in]
        par_free = []
        x_ok = [x_in]

        def causal_heads(t, heads, q_of, k_of, v_of, vw, scale, ready, extra=None):
            d = scores(t, heads, q_of, k_of, ready)
            fill()
            e, rdy, rz = softmax_parts(t, heads, scale, d, extra)
            b, last = weighted(t, heads, lambda i: SC[:, pos_of(i), :], v_of, vw, [e])
            fill()
            o = O[:, t, :]
            for i in range(heads):
                p_ = pos_of(i)
                tok = dve.do(lambda i=i, p_=p_: nc.vector.tensor_scalar(
                    o[:, i * vw:(i + 1) * vw], bank[b][:, i * vw:(i + 1) * vw], rz[:, p_:p_ + 1], None, ALU.mult),
                    last, rdy, o_free[0])
            bank_free[b] = tok
            return tok

        def turn_o(n, ready):
            flat = OT[:, n].rearrange("p k s -> p (k s)")
            pieces = [O[:, t, k * P:(k + 1) * P] for k in range(4) for t in range(T)]
            done = transposes(lambda i0, m: flat[:, i0 * P:(i0 + m) * P], pieces, ready, ot_free[0])
            o_free[0] = pe_last()
            return done

        ot_free = [None]

        def turn_heads(dst, st, nblk, w, ready, free):
            pieces = [st[:, t, k * w:(k + 1) * w] for k in range(nblk) for t in range(T)]
            flat = dst.rearrange("p k s -> p (k s)")
            return transposes(lambda i0, m: flat[:, i0 * P:(i0 + m) * P], pieces, ready, free)

        def first_layer(l):
            lam_init = 0.8 - 0.6 * math.exp(-0.3 * l)
            src = par1[l * P1_N:(l + 1) * P1_N].partition_broadcast(P)
            par = load(pool, PAR[:, 0:P1_N], src, "l_par", par_free)
            xr = x_ready
            IST = STB[:, 0:T * 640].rearrange("p (t c) -> p t c", t=T)
            IW = sm[:, 104:104 + 16].rearrange("p (t h) -> p t h", t=T)
            done = []
            for c in range(2):
                done += projection("w_in", [(IST[:, :, c * 256:(c + 1) * 256], 0, 256)], xr, a_free[0])
            done += projection("w_in", [(IST[:, :, 512:576], 0, 64), (IST[:, :, 576:640], 0, 64), (IW, 64, 72)],
                               xr, a_free[0])
            iw = dve.do(lambda: nc.vector.tensor_scalar(IW, IW, 8 ** -0.5, None, ALU.mult), done)
            rot = rope(IST.rearrange("p t (h d) -> p t h d", d=64), 10, 0, 8, RC, RS, [*done, rope_ready])
            SST = STA.rearrange("p (t c) -> p t c", t=T)
            done = []
            for c in range(4):
                done += projection("w_in", [(SST[:, :, c * 256:(c + 1) * 256], 0, 256)], xr, a_free[0])
            IT = QKT[:, 0:5 * S].rearrange("p (k s) -> p k s", k=5)
            it = turn_heads(IT, IST, 5, P, rot, a_free[0])
            ist_free = pe_last()
            rot = rope(SST.rearrange("p t (h d) -> p t h d", d=64), 16, 0, 8, RC, RS, done)
            sel = []
            for t in range(T):
                kl = P * (t + 1)
                d = scores(t, 8, lambda i: IT[64 * (i % 2):64 * (i % 2) + 64, i // 2, :],
                           lambda i: IT[64 * (i % 2):64 * (i % 2) + 64, 4, :], it)
                if t == 0:
                    for c in range(2):
                        vt = projection("w_in", [(V[:, :, c * 256:(c + 1) * 256], 0, 256)], xr, v_free[0])
                else:
                    fillq = vt
                e = act.do(lambda t=t, kl=kl: nc.scalar.activation(SC[:, :, 0:kl], scp[:, :, 0:kl], ACT.Relu, scale=0.125),
                           d, p_free[0])
                sc_free[0] = e
                wk = work[:, t, 0:kl]
                a = e
                for i in range(8):
                    p_ = pos_of(i)
                    if i == 0:
                        a = dve.do(lambda wk=wk, p_=p_, t=t, kl=kl, i=i: nc.vector.tensor_scalar(
                            wk, SC[:, p_, 0:kl], IW[:, t, i:i + 1], None, ALU.mult), a, iw)
                    else:
                        a = dve.do(lambda wk=wk, p_=p_, t=t, kl=kl, i=i: nc.vector.scalar_tensor_tensor(
                            wk, SC[:, p_, 0:kl], IW[:, t, i:i + 1], wk, ALU.mult, ALU.add), a)
                p_free[0] = a
                dg = work[:, t, t * P:kl]
                a = dve.do(lambda dg=dg: nc.vector.tensor_tensor(dg, dg, const("caus"), ALU.add), a)
                m8 = sm[:, 80 + 8 * t:88 + 8 * t]
                for _ in range(TOPK // 8):
                    a = dve.do(lambda m8=m8, wk=wk: nc.vector.max(m8, wk), a)
                    a = dve.do(lambda m8=m8, wk=wk: nc.vector.match_replace(wk, m8, wk, GONE), a)
                bs = bias[:, t, 0:kl]
                a = dve.do(lambda bs=bs, wk=wk: nc.vector.tensor_scalar(bs, wk, -2e38, NEG, ALU.is_gt, ALU.mult), a)
                dg = bias[:, t, t * P:kl]
                sel.append(dve.do(lambda dg=dg: nc.vector.tensor_tensor(dg, dg, const("caus"), ALU.add), a))
            it_free = pe_last()
            DST = STB.rearrange("p (t c) -> p t c", t=T)[:, :, 0:1024]
            done = []
            for c in range(4):
                done += projection("w_in", [(STB[:, 0:2048].rearrange("p (t c) -> p t c", t=T)[:, :, c * 256:(c + 1) * 256], 0, 256)],
                                   xr, ist_free)
            DST = STB[:, 0:2048].rearrange("p (t c) -> p t c", t=T)
            dt_ = []
            for c in range(2):
                dt_ += projection("w_in", [(V[:, :, 512 + c * 256:512 + (c + 1) * 256], 0, 256)], xr, v_free[0])
            drot = rope(DST.rearrange("p t (h d) -> p t h d", d=64), 16, 0, 8, RC, RS, done)
            start_fill("w_in", 8, xr)
            ST = QKT[:, 0:8 * S].rearrange("p (k s) -> p k s", k=8)
            DT = QKT[:, 8 * S:16 * S].rearrange("p (k s) -> p k s", k=8)
            dtr = turn_heads(DT, DST, 8, P, drot, None)
            str_ = turn_heads(ST, SST, 8, P, rot, it_free)
            lp = par1_("diff_lambda").rearrange("p (a b d) -> p a b d", a=2, b=2)
            pr = sm[:, 256:384].rearrange("p (a d) -> p a d", a=2)
            sums, lam = sm[:, 116:118], sm[:, 118:119]
            a = dve.do(lambda: nc.vector.tensor_tensor(pr, lp[:, :, 0], lp[:, :, 1], ALU.mult), par)
            a = dve.do(lambda: nc.vector.tensor_reduce(sums, pr, AX.X, ALU.add), a)
            a = act.do(lambda: nc.scalar.activation(sums, sums, ACT.Exp), a)
            a = dve.do(lambda: nc.vector.tensor_tensor(lam, sums[:, 1:2], sums[:, 0:1], ALU.subtract), a)
            nlam = dve.do(lambda: nc.vector.tensor_scalar(lam, lam, -lam_init, None, ALU.add), a)
            for t in range(T):
                kl = P * (t + 1)
                d = scores(t, 8, lambda i: DT[64 * (i % 2):64 * (i % 2) + 64, i // 2, :],
                           lambda i: DT[64 * (i % 2):64 * (i % 2) + 64, 4 + i // 2, :], dtr)
                fill()
                e, rdy, rz = softmax_parts(t, 8, 0.125, d)
                w1 = sm[:, 56:64]
                a = dve.do(lambda rz=rz: nc.vector.tensor_scalar(w1, rz, lam, None, ALU.mult), rdy, nlam)
                for h in range(4):
                    p0, p1 = pos_of(2 * h), pos_of(2 * h + 1)
                    x1 = SC[:, p1, 0:kl]
                    x0_ = SC[:, p0, 0:kl]
                    b = dve.do(lambda x1=x1, p1=p1: nc.vector.tensor_scalar(x1, x1, w1[:, p1:p1 + 1], None, ALU.mult), a, e)
                    pr_ = dve.do(lambda x0_=x0_, x1=x1, p0=p0, rz=rz: nc.vector.scalar_tensor_tensor(
                        x0_, x0_, rz[:, p0:p0 + 1], x1, ALU.mult, ALU.add), b)
                b, last = weighted(t, 4, lambda i: SC[:, pos_of(2 * i), :],
                                   lambda i, k: V[:, k, 512 + i * P:512 + (i + 1) * P], P, [pr_])
                fill()
                ob = O[:, t, :].rearrange("p (h d) -> p h d", h=4)
                o = dve.do(lambda ob=ob, b=b: nc.vector.tensor_copy(ob, bank[b][:, :].rearrange("p (h d) -> p h d", h=4)),
                           last, o_free[0])
                bank_free[b] = o
                mean, var, ok = norm_stats(ob, 4, P, 64, LN_EPS, True, o)
                g = par1_("diff_subln_g")
                for h in range(4):
                    oh = ob[:, h, :]
                    a = dve.do(lambda oh=oh, var=var, h=h: nc.vector.tensor_scalar(
                        oh, oh, var[:, h:h + 1], 1.0 - lam_init, ALU.mult, ALU.mult), ok)
                o = dve.do(lambda ob=ob, g=g: nc.vector.tensor_tensor(
                    ob, ob, g.unsqueeze(1).broadcast_to([P, 4, P]), ALU.mult), a)
            ota = turn_o(0, o)
            for t in range(T):
                o = causal_heads(t, 8, lambda i: ST[64 * (i % 2):64 * (i % 2) + 64, i // 2, :],
                                 lambda i: ST[64 * (i % 2):64 * (i % 2) + 64, 4 + i // 2, :],
                                 lambda i, k: V[:, k, i * 64:(i + 1) * 64], 64, 0.125, str_, sel[t])
            v_free[0] = pe_last()
            fill(8)
            otb = turn_o(1, o)
            m = branches(("w_branch_diff", "w_branch_dsa"), (ota, otb))
            ot_free[0] = pe_last()
            x = mix_out("w_out", ALPHA, [*m, *x_ok])
            h_free[0] = pe_last()
            x = layer_norm(X, par1_("ln1_g"), par1_("ln1_b"), [*x, par])
            xt = turn_x(X, x)
            (wg, we), loaded = take("w_route_group", "w_route_expert")
            b = next_bank()
            lg = sm[:, 384:384 + T * 36].rearrange("p (t c) -> p t c", t=T)
            waits = [loaded, *xt, bank_free[b]]
            for t in range(T):
                for c0, w in ((0, wg), (4, we)):
                    n = w.shape[2]
                    for k in range(KD):
                        last = mm(bank[b][:, t * 64 + c0:t * 64 + c0 + n], XT[:, k, t * P:(t + 1) * P], w[:, k, :],
                                  k == 0, k == KD - 1, *waits)
                        waits = []
            release(last)
            rb = PAR[:, P1_AT["b_route_group"][0]:P1_AT["b_route_group"][0] + 36]
            for t in range(T):
                a = dve.do(lambda t=t, b=b: nc.vector.tensor_tensor(lg[:, t, :], bank[b][:, t * 64:t * 64 + 36], rb, ALU.add),
                           last)
            bank_free[b] = a
            val = rt[:, 0:4].rearrange("p (c t) -> p c t", c=2)
            for t in range(T):
                a = route(lg[:, t, :], [OH[:, c, t, :] for c in range(2)], [val[:, c, t:t + 1] for c in range(2)], a)
            chosen = a
            PTT = TMP2[:, 0:512].rearrange("p (k s) -> p k s", k=2)
            pt_in = load(pool, PTT, pT[l], "l_pt", rope_done[-1:])
            GP = A[:, 4608:6656].rearrange("p (t d) -> p t d", t=T)
            gp = []
            for c in range(4):
                b, v, last = tokens_major("w_ple_gate", XT, xt)
                g = GP[:, :, c * 256:(c + 1) * 256]
                bank_free[b] = act.do(lambda g=g, v=v: nc.scalar.activation(g, v, ACT.Tanh, scale=0.5), last)
                gp.append(bank_free[b])
            mk = dve.do(lambda: nc.vector.tensor_tensor(MK[:, :, :], OH[:, 0], OH[:, 1], ALU.add), chosen)
            b = next_bank()
            one = const("one")
            pp, cc = bank[b][:, 0:64], bank[b][:, 64:96]
            mm(pp[:, 0:32], const("before"), MK[:, 0, :], True, True, mk, bank_free[b])
            mm(pp[:, 32:64], one.broadcast_to([P, P]), MK[:, 0, :], True, False)
            mm(pp[:, 32:64], const("before"), MK[:, 1, :], False, True)
            for t in range(T):
                mm(cc, one.broadcast_to([P, P]), MK[:, t, :], t == 0, t == T - 1)
            for t in range(T):
                last = mm(bank[b][0:NE, 128:129], MK[:, t, :], one, t == 0, t == T - 1)
            cnt = rt[0:NE, 4:5]
            c1 = dve.do(lambda b=b: nc.vector.tensor_copy(cnt, bank[b][0:NE, 128:129]), last)
            cmx = rt[:, 5:6]
            a = dve.do(lambda cc=cc: nc.vector.tensor_reduce(cmx, cc, AX.X, ALU.max), last)
            a = dve.do(lambda: nc.vector.tensor_scalar(cmx, cmx, CAP + 0.5, None, ALU.is_gt), a)
            fl = dve.do(lambda: nc.vector.tensor_copy(flag[:, :], cmx), a)
            p_ok = dve.do(lambda pp=pp: nc.vector.tensor_copy(PS[:, :, :], pp.rearrange("p (t e) -> p t e", t=T)), last)
            last = mm(bank[b][:, 96:128], cnt.broadcast_to([NE, P]), const("before")[0:NE, 0:NE], True, True, c1, p_ok)
            o_ok = dve.do(lambda b=b: nc.vector.tensor_copy(OFF[:, :], bank[b][:, 96:128]), last)
            bank_free[b] = o_ok
            oi = dve.do(lambda: nc.vector.tensor_copy(offi[:, :], OFF[:, :]), o_ok)
            pos = rt[:, 8:12].rearrange("p (c t) -> p c t", c=2)
            slot = rt[:, 12:16].rearrange("p (c t) -> p c t", c=2)
            vm = rt[:, 16:20].rearrange("p (c t) -> p c t", c=2)
            vo = rt[:, 20:24].rearrange("p (c t) -> p c t", c=2)
            tm = sm[:, 256:320].rearrange("p (t e) -> p t e", t=T)
            tn = sm[:, 320:384].rearrange("p (t e) -> p t e", t=T)
            for c in range(2):
                a = dve.do(lambda c=c: nc.vector.tensor_tensor(tm, OH[:, c], PS[:, :, :], ALU.mult), p_ok, a)
                a = dve.do(lambda c=c: nc.vector.tensor_reduce(pos[:, c, :], tm, AX.X, ALU.add), a)
                a2 = dve.do(lambda c=c: nc.vector.tensor_tensor(
                    tn, OH[:, c], OFF[:, :].unsqueeze(1).broadcast_to([P, T, NE]), ALU.mult), o_ok, a)
                a2 = dve.do(lambda c=c: nc.vector.tensor_reduce(slot[:, c, :], tn, AX.X, ALU.add), a2)
                a = dve.do(lambda c=c: nc.vector.tensor_tensor(slot[:, c, :], slot[:, c, :], pos[:, c, :], ALU.add), a2)
                b_ = dve.do(lambda c=c: nc.vector.scalar_tensor_tensor(
                    vm[:, c, :], pos[:, c, :], CAP - 0.5, val[:, c, :], ALU.is_lt, ALU.mult), a)
                vok = dve.do(lambda c=c: nc.vector.tensor_tensor(vo[:, c, :], val[:, c, :], vm[:, c, :], ALU.subtract), b_)
            OTF = OT[:, :, :, :].rearrange("p n k s -> p (n k s)")
            G = OTF[:, 0:1024].rearrange("p (t s) -> p t s", t=T)
            C = OTF[:, 1024:2048].rearrange("p (t s) -> p t s", t=T)
            CT = OTF[:, 2048:3072].rearrange("p (j q) -> p j q", j=4)
            iota = const("iota")
            gk = []
            for t in range(T):
                a = dve.do(lambda t=t: nc.vector.tensor_scalar(G[:, t, :], iota, slot[:, 0, t:t + 1], None, ALU.is_equal), vok,
                           ot_free[0])
                gk.append(dve.do(lambda t=t: nc.vector.scalar_tensor_tensor(
                    G[:, t, :], iota, slot[:, 1, t:t + 1], G[:, t, :], ALU.is_equal, ALU.add), a))
            XG = GT[:, :, :, :].rearrange("p n k s -> p (n k s)")[:, 0:KD * (SLOTS + CAP)].rearrange("p (k s) -> p k s", k=KD)
            YC = A[:, 0:KD * (SLOTS + CAP)].rearrange("p (k s) -> p k s", k=KD)
            xg = [pool.do(lambda: nc.gpsimd.memset(XG[:, :, SLOTS:SLOTS + CAP], 0.0), merged_read[0])]
            yz = pool.do(lambda: nc.gpsimd.memset(YC, 0.0), v_free[0])
            for k in range(KD):
                b = next_bank()
                waits = [*gk, bank_free[b]]
                for t in range(T):
                    last = mm(bank[b][:, :], X[:, t, k * P:(k + 1) * P], G[:, t, :], t == 0, t == T - 1, *waits)
                    waits = []
                bank_free[b] = copy(either(), XG[:, k, 0:SLOTS], bank[b][:, :], last)
                xg.append(bank_free[b])
            x_read = last
            cw = TMP[:, 0:512]
            for t in range(T):
                a = dve.do(lambda t=t: nc.vector.tensor_scalar(
                    C[:, t, :], iota, slot[:, 0, t:t + 1], vm[:, 0, t:t + 1], ALU.is_equal, ALU.mult), vok, ot_free[0])
                a = dve.do(lambda t=t: nc.vector.tensor_scalar(
                    cw, iota, slot[:, 1, t:t + 1], vm[:, 1, t:t + 1], ALU.is_equal, ALU.mult), a)
                a = dve.do(lambda t=t: nc.vector.tensor_tensor(C[:, t, :], C[:, t, :], cw, ALU.add), a)
            CTF = CT.rearrange("p j q -> p (j q)")
            ct = transposes(lambda i0, n: CTF[:, i0 * P:(i0 + n) * P],
                            [C[:, t, j * P:(j + 1) * P] for j in range(4) for t in range(T)], a, ot_free[0])
            for t in range(T):
                xa = dve.do(lambda t=t: nc.vector.tensor_scalar(X[:, t, :], X[:, t, :], ALPHA, None, ALU.mult), xt, x_read)
            (w,), loaded = take("w_ple")
            for c in range(4):
                b = next_bank()
                v = bank[b][:, :].rearrange("p (t n) -> p t n", t=T)
                waits = [loaded, pt_in, bank_free[b]]
                for t in range(T):
                    for k in range(2):
                        last = mm(v[:, t, :], PTT[:, k, t * P:(t + 1) * P], w[:, k, c * 256:(c + 1) * 256],
                                  k == 0, k == 1, *waits)
                        waits = []
                g = GP[:, :, c * 256:(c + 1) * 256]
                xs = X[:, :, c * 256:(c + 1) * 256]
                a = dve.do(lambda g=g, v=v: nc.vector.scalar_tensor_tensor(g, g, 1.0, v, ALU.add, ALU.mult), last, gp)
                bank_free[b] = a
                ple = dve.do(lambda xs=xs, g=g: nc.vector.scalar_tensor_tensor(xs, g, 0.5, xs, ALU.mult, ALU.add), a, xa)
            release(last)
            yv = scp[:, :, :].rearrange("p a s -> p (a s)").rearrange("p (t n) -> p t n", t=T)
            SCF = SC[:, :, :].rearrange("p h s -> p (h s)")
            SG = [SCF[:, i * 256:i * 256 + P].rearrange("p (f s) -> p f s", f=2) for i in range(2)]
            HS = [SCF[:, i * 256 + P:i * 256 + 2 * P].rearrange("p (f s) -> p f s", f=2) for i in range(2)]
            hs_free = [p_free[0], p_free[0]]
            hs_ok = [None, None]
            first = {}

            def at(q, e, *waits):
                def go():
                    first[q, e] = q.eng.value_load(offi[0:1, e:e + 1], min_val=0, max_val=SLOTS)
                q.do(go, *waits)

            for e in range(NE + 1):
                if e < NE:
                    i = e % 2
                    b = next_bank()
                    v = bank[b][:, 0:4 * CAP].rearrange("p (g f s) -> p g f s", g=2, f=2)
                    at(pe, e, oi)
                    waits = [*xg, bank_free[b]]
                    for n, name in enumerate(("w_exp_gate", "w_exp_up")):
                        (w,), loaded = take(name)
                        waits.append(loaded)
                        for f in range(2):
                            for k in range(KD):
                                last = pe.do(lambda w=w, n=n, f=f, k=k, e=e, v=v: nc.tensor.matmul(
                                    v[:, n, f, :], w[:, k, f * P:(f + 1) * P], XG[:, k, bass.ds(first[pe, e], CAP)],
                                    start=(k == 0), stop=(k == KD - 1)), *waits)
                                waits = []
                        release(last)
                        if n == 0:
                            lg_ = last
                    a = act.do(lambda i=i, v=v: nc.scalar.activation(SG[i], v[:, 0], ACT.Tanh, scale=0.5), last, hs_free[i])
                    a = dve.do(lambda i=i, v=v: nc.vector.scalar_tensor_tensor(SG[i], SG[i], 1.0, v[:, 0], ALU.add, ALU.mult), a)
                    a = dve.do(lambda i=i, v=v: nc.vector.scalar_tensor_tensor(HS[i], SG[i], 0.5, v[:, 1], ALU.mult, ALU.mult), a)
                    bank_free[b] = a
                    hs_ok[i] = a
                if e:
                    i = (e - 1) % 2
                    (w,), loaded = take("w_exp_down")
                    b = next_bank()
                    v = bank[b][:, :].rearrange("p (k s) -> p k s", k=KD)
                    waits = [loaded, hs_ok[i], bank_free[b]]
                    for m in range(KD):
                        for f in range(2):
                            last = mm(v[:, m, :], w[:, f, m * P:(m + 1) * P], HS[i][:, f, :], f == 0, f == 1, *waits)
                            waits = []
                    release(last)
                    hs_free[i] = last
                    at(act, e - 1, oi)
                    yc = act.do(lambda v=v, e=e: nc.scalar.copy(YC[:, :, bass.ds(first[act, e - 1], CAP)], v), last, yz, yc_last)
                    yc_last[:] = [yc]
                    bank_free[b] = yc
            p_free[0] = last
            YS = V[:, :, :].rearrange("p t c -> p (t c)").rearrange("p (j d) -> p j d", j=4)
            YSF = YS.rearrange("p j d -> p (j d)")
            ys = transposes(lambda i0, n: YSF[:, i0 * P:(i0 + n) * P],
                            [YC[:, k, j * P:(j + 1) * P] for j in range(4) for k in range(KD)], yc, v_free[0])
            a_free[0] = pe_last()
            waits = [*ct, *ys, sc_free[0]]
            for t in range(T):
                for n in range(2):
                    for j in range(4):
                        last = mm(yv[:, t, n * 512:(n + 1) * 512], CT[:, j, t * P:(t + 1) * P], YS[:, j, n * 512:(n + 1) * 512],
                                  j == 0, j == 3, *waits)
                        waits = []
            ot_free[0] = v_free[0] = last
            for t in range(T):
                a = dve.do(lambda t=t: nc.vector.tensor_tensor(X[:, t, :], X[:, t, :], yv[:, t, :], ALU.add), last, ple)
            sc_free[0] = a
            overflow(l, a, fl, vok)
            x = layer_norm(X, par1_("ln2_g"), par1_("ln2_b"), a)
            par_free[:] = x
            x_ok[:] = x
            if l < DEPTH - 1:
                x_ready[:] = turn_x(X, x)

        a_free = [None]
        v_free = [None]
        yc_last = []

        def overflow(l, ready, flagged, vok):
            if not flags_on:
                return
            q = {e: Queue(e.eng, sem(f"over{l}_{i}")) for i, e in enumerate((pe, dve, act, pool))}
            qpe, qdve, qact, qpool = (q[e] for e in (pe, dve, act, pool))
            PTF = PT[:, :, :, :].rearrange("p h k q -> p (h k q)")
            HF = H[:, :, :].rearrange("p t d -> p (t d)")
            slots = [PTF, HF, A[:, 6656:8704]]
            sems = [sem(f"over{l}_ring{i}") for i in range(3)]
            freed_ = []
            SCF = SC[:, :, :].rearrange("p h s -> p (h s)")
            SG = [SCF[:, i * 512:(i + 1) * 512].rearrange("p (m s) -> p m s", m=2) for i in range(2)]
            HG = [SCF[:, 1024 + i * 512:1024 + (i + 1) * 512].rearrange("p (m s) -> p m s", m=2) for i in range(2)]
            CB = [O[:, i, 0:S] for i in range(2)]
            yv = scp[:, :, :].rearrange("p a s -> p (a s)").rearrange("p (t n) -> p t n", t=T)
            vo = rt[:, 20:24].rearrange("p (c t) -> p c t", c=2)
            names = ("w_exp_gate", "w_exp_up", "w_exp_down")
            for i in range(3 * NE):
                e = i // 3
                k = WHERE[names[i % 3], (l, e // EPG, e % EPG)]
                src = wts[AT[k]:AT[k + 1]].rearrange("(p n) -> p n", p=P)
                turn_ = i // 3 + 1
                slot_token = Token(None)
                freed_.append(slot_token)
                qpool.items.append((lambda i=i, src=src: nc.gpsimd.dma_start(slots[i % 3], src).then_inc(sems[i % 3], 16),
                                    [freed_[i - 3]] if i >= 3 else [ready], DmaDone(sems[i % 3], 16 * turn_)))

            def got(i):
                kt = 2 if i % 3 == 2 else KD
                return slots[i % 3].rearrange("p (k n) -> p k n", k=kt), DmaDone(sems[i % 3], 16 * (i // 3 + 1))

            def through(i, token):
                freed_[i].twin = token

            for t in range(T):
                a = qdve.do(lambda t=t: nc.vector.tensor_scalar(comb[:, t, :], OH[:, 0, t, :], vo[:, 0, t:t + 1], None, ALU.mult),
                            ready, vok)
                cm = qdve.do(lambda t=t: nc.vector.scalar_tensor_tensor(
                    comb[:, t, :], OH[:, 1, t, :], vo[:, 1, t:t + 1], comb[:, t, :], ALU.mult, ALU.add), a)
            free = [ready] * 4
            n = 0
            hg_free = [None, None]
            for e in range(NE):
                i = e % 2
                bs = [(n + j) % 4 for j in range(3)]
                n += 3
                prods = []
                for j in range(2):
                    w, loaded = got(3 * e + j)
                    v = bank[bs[j]][:, :].rearrange("p (m s) -> p m s", m=2)
                    waits = [loaded, free[bs[j]], bank_free[bs[j]]]
                    for m in range(2):
                        for k in range(KD):
                            last = qpe.do(lambda v=v, w=w, m=m, k=k: nc.tensor.matmul(
                                v[:, m, :], w[:, k, m * P:(m + 1) * P], XT[:, k, :], start=(k == 0), stop=(k == KD - 1)), *waits)
                            waits = []
                    through(3 * e + j, last)
                    prods.append((v, last))
                waits = [cm, free[bs[2]], bank_free[bs[2]]]
                for t in range(T):
                    l3 = qpe.do(lambda t=t, e=e, b=bs[2]: nc.tensor.matmul(
                        bank[b][:, t * P:(t + 1) * P], comb[:, t, e:e + 1].broadcast_to([P, P]), ident, start=True, stop=True), *waits)
                    waits = []
                (g, l1), (u, l2) = prods
                a = qact.do(lambda g=g, i=i: nc.scalar.activation(SG[i], g, ACT.Tanh, scale=0.5), l1, hg_free[i], ready)
                free[bs[2]] = cb = qact.do(lambda i=i, b=bs[2]: nc.scalar.copy(CB[i], bank[b][:, 0:S]), l3)
                free[bs[0]] = a = qdve.do(lambda g=g, i=i: nc.vector.scalar_tensor_tensor(SG[i], SG[i], 1.0, g, ALU.add, ALU.mult), a)
                free[bs[1]] = a = qdve.do(lambda u=u, i=i: nc.vector.scalar_tensor_tensor(SG[i], SG[i], 0.5, u, ALU.mult, ALU.mult), a, l2)
                a = qdve.do(lambda i=i: nc.vector.tensor_tensor(
                    HG[i], SG[i], CB[i].unsqueeze(1).broadcast_to([P, 2, S]), ALU.mult), a, cb)
                w, loaded = got(3 * e + 2)
                waits = [loaded, a]
                for k in range(2):
                    for t in range(T):
                        for h in range(2):
                            last = qpe.do(lambda k=k, t=t, h=h, e=e, i=i, w=w: nc.tensor.matmul(
                                yv[:, t, h * 512:(h + 1) * 512], HG[i][:, k, t * P:(t + 1) * P],
                                w[:, k, h * 512:(h + 1) * 512], start=(e == 0 and k == 0), stop=(e == NE - 1 and k == 1)), *waits)
                            waits = []
                through(3 * e + 2, last)
                hg_free[i] = last
            for t in range(T):
                end = qdve.do(lambda t=t: nc.vector.tensor_tensor(X[:, t, :], X[:, t, :], yv[:, t, :], ALU.add), last)
            for fn, waits, token in qpool.items:
                waits[:] = [w.twin if hasattr(w, "twin") else w for w in waits]
                for w in waits:
                    w.marked = True
            for x in (qpe, qdve, qact, qpool):
                x.do(lambda: None, end)
                x.number()
            for e in (pe, dve, act, pool):
                e.branch(flag[0:1, 0:1], q[e], flagged, ready)

        flags_on = True

        def one_hots(src, prob, which, out_, base, ready):
            m8 = sm[:, base:base + 8]
            fi = sm[:, base + 8:base + 16]
            a = dve.do(lambda: nc.vector.max(m8, src), ready)
            a = dve.do(lambda: nc.vector.max_index(idx8[:, :], m8, src), a)
            a = dve.do(lambda: nc.vector.tensor_copy(fi, idx8[:, :]), a)
            for i in range(which):
                last = dve.do(lambda i=i: nc.vector.tensor_scalar(out_[i], const("iota8"), fi[:, i:i + 1], None, ALU.is_equal), a)
            return m8, last

        def route(lg, hot, val, ready):
            b0 = 160
            gp = sm[:, b0:b0 + 8]
            gmx, gz, gv = (sm[:, b0 + 8 + i:b0 + 9 + i] for i in range(3))
            emx, es, ev = (sm[:, b0 + 12 + i:b0 + 13 + i] for i in range(3))
            oh = sm[:, b0 + 16:b0 + 24]
            e8 = sm[:, b0 + 24:b0 + 32]
            h1, h2 = sm[:, b0 + 32:b0 + 40], sm[:, b0 + 40:b0 + 48]
            sel = sm[:, 256:288].rearrange("p (g e) -> p g e", g=NG)
            d = [ready]

            def step(fn, *w):
                d[0] = dve.do(fn, d[0], *w)

            def astep(fn):
                d[0] = act.do(fn, d[0])

            step(lambda: nc.vector.memset(gp, -1.0))
            step(lambda: nc.vector.tensor_reduce(gmx, lg[:, 0:NG], AX.X, ALU.max))
            step(lambda: nc.vector.tensor_scalar(gmx, gmx, -1.0, None, ALU.mult))
            astep(lambda: nc.scalar.activation(gp[:, 0:NG], lg[:, 0:NG], ACT.Exp, bias=gmx, accum_out=gz))
            _, d[0] = one_hots(gp, None, 1, [oh], b0 + 48, d[0])
            m8 = sm[:, b0 + 48:b0 + 56]
            step(lambda: nc.vector.reciprocal(gz, gz))
            step(lambda: nc.vector.tensor_tensor(gv, m8[:, 0:1], gz, ALU.mult))
            le = lg[:, NG:NG + NE].rearrange("p (g e) -> p g e", g=NG)
            step(lambda: nc.vector.tensor_tensor(sel, le, oh[:, 0:NG].unsqueeze(2).broadcast_to([P, NG, EPG]), ALU.mult))
            step(lambda: nc.vector.tensor_reduce(e8, sel.rearrange("p g e -> p e g"), AX.X, ALU.add))
            step(lambda: nc.vector.tensor_reduce(emx, e8, AX.X, ALU.max))
            step(lambda: nc.vector.tensor_scalar(emx, emx, -1.0, None, ALU.mult))
            astep(lambda: nc.scalar.activation(e8, e8, ACT.Exp, bias=emx, accum_out=es))
            step(lambda: nc.vector.reciprocal(es, es))
            step(lambda: nc.vector.tensor_scalar(e8, e8, es, None, ALU.mult))
            _, d[0] = one_hots(e8, None, 2, [h1, h2], b0 + 48, d[0])
            step(lambda: nc.vector.tensor_tensor(es, m8[:, 0:1], m8[:, 1:2], ALU.add))
            step(lambda: nc.vector.reciprocal(es, es))
            step(lambda: nc.vector.tensor_tensor(es, es, gv, ALU.mult))
            for c, h in enumerate((h1, h2)):
                step(lambda c=c: nc.vector.tensor_tensor(val[c], m8[:, c:c + 1], es, ALU.mult))
                step(lambda c=c, h=h: nc.vector.tensor_tensor(
                    hot[c].rearrange("p (g e) -> p g e", g=NG), oh[:, 0:NG].unsqueeze(2).broadcast_to([P, NG, EPG]),
                    h.unsqueeze(1).broadcast_to([P, NG, EPG]), ALU.mult))
            return d[0]

        def second_layer(l):
            src = par2[l * P2_N:(l + 1) * P2_N].partition_broadcast(P)
            par = load(pool, PAR[:, 0:P2_N], src, "l_par", par_free)
            h = rms_norm(H, X, par2_("attn_norm_2"), NORM_EPS, D, [*x_ok, *c_in, par, *([h_free[0]] if h_free[0] else [])])
            xr = turn_x(H, h)
            h_free[0] = pe_last()
            CST_ = STA[:, 0:T * 416].rearrange("p (t c) -> p t c", t=T)
            done = projection("w_in_2", [(CST_[:, :, 0:256], 0, 256)], xr, a_free[0])
            done += projection("w_in_2", [(CST_[:, :, 256:416], 0, 160)], xr, a_free[0])
            a1 = rms_norm(CST_[:, :, 0:256], CST_[:, :, 0:256], par2_("mla_q_norm_2"), NORM_EPS, 256, done)
            a2 = rms_norm(CST_[:, :, 256:384], CST_[:, :, 256:384], par2_("mla_kv_norm_2"), NORM_EPS, 128, done)
            kr = rope(CST_[:, :, 384:416].unsqueeze(2), 1, 0, 16, *cs(32), done)
            CT = TMP2[:, 1024:1792].rearrange("p (k s) -> p k s", k=3)
            ct = turn_heads(CT, CST_[:, :, 0:384], 3, P, [*a1, *a2], None)
            QS = STB[:, 0:1536].rearrange("p (t c) -> p t c", t=T)
            KS = STB[:, 1536:3072].rearrange("p (t c) -> p t c", t=T)
            KS4 = KS.rearrange("p t (h d) -> p t h d", h=8)
            (w,), loaded = take("mla_w_q_up_2")
            qd = []
            for c in range(3):
                b = next_bank()
                v = bank[b][:, :].rearrange("p (t n) -> p t n", t=T)
                waits = [loaded, *ct, bank_free[b]]
                for t in range(T):
                    for k in range(2):
                        last = mm(v[:, t, :], CT[:, k, t * P:(t + 1) * P], w[:, k, c * 256:(c + 1) * 256], k == 0, k == 1, *waits)
                        waits = []
                bank_free[b] = copy(act, QS[:, :, c * 256:(c + 1) * 256], v, last, a_free[0])
                qd.append(bank_free[b])
            release(last)
            (w,), loaded = take("mla_w_kv_up_2")
            kd = []
            for c in range(4):
                b = next_bank()
                v = bank[b][:, :].rearrange("p (t n) -> p t n", t=T)
                waits = [loaded, bank_free[b]]
                for t in range(T):
                    last = mm(v[:, t, :], CT[:, 2, t * P:(t + 1) * P], w[:, 0, c * 256:(c + 1) * 256], True, True, *waits)
                    waits = []
                v4 = v.rearrange("p t (h d) -> p t h d", h=2)
                for t in range(T):
                    vd = V[:, t, c * P:(c + 1) * P].rearrange("p (h d) -> p h d", h=2)
                    copy(act, KS4[:, t, 2 * c:2 * c + 2, 0:64], v4[:, t, :, 0:64], last, a_free[0])
                    bank_free[b] = copy(act, vd, v4[:, t, :, 64:128], last, v_free[0])
                kd.append(bank_free[b])
            release(last)
            for t in range(T):
                kp = dve.do(lambda t=t: nc.vector.tensor_copy(
                    KS4[:, t, :, 64:96], CST_[:, t, 384:416].unsqueeze(1).broadcast_to([P, 8, 32])), kr, a_free[0])
            qr = rope(QS.rearrange("p t (h d) -> p t h d", h=8), 8, 64, 16, *cs(32), qd)
            MST = STA.rearrange("p (t c) -> p t c", t=T)
            mdone = []
            cst_free = kp
            for c in range(4):
                mdone += projection("w_in_2", [(MST[:, :, c * 256:(c + 1) * 256], 0, 256)], xr, cst_free, *ct)
            for c in range(2):
                mv = projection("w_in_2", [(V[:, :, 512 + c * 256:512 + (c + 1) * 256], 0, 256)], xr, v_free[0])
            QT = QKT[0:96, 0:8 * S].rearrange("p (k s) -> p k s", k=8)
            KT = QKT[0:96, 8 * S:16 * S].rearrange("p (k s) -> p k s", k=8)
            qt = turn_heads(QT, QS, 8, 96, qr, a_free[0])
            kt = turn_heads(KT, KS, 8, 96, [*kd, kp], a_free[0])
            stb_free = pe_last()
            mr = rope(MST.rearrange("p t (h d) -> p t h d", d=64), 16, 0, 8, *cs(16), mdone)
            RST = STB[:, 0:1024].rearrange("p (t c) -> p t c", t=T)
            rdone = []
            for c in range(2):
                rdone += projection("w_in_2", [(RST[:, :, c * 256:(c + 1) * 256], 0, 256)], xr, stb_free)
            rr = rope(RST.rearrange("p t (h d) -> p t h d", d=64), 8, 0, 32, *cs(64), rdone)
            rs = dve.do(lambda: nc.vector.tensor_scalar(RST[:, :, 256:512], RST[:, :, 256:512], 0.125, None, ALU.mult), rr)
            for c in range(4):
                rv = projection("w_in_2", [(V[:, :, 1024 + c * 256:1024 + (c + 1) * 256], 0, 256)], xr, v_free[0])
            start_fill("w_in_2", 12, xr)
            for t in range(T):
                o = causal_heads(t, 8, lambda i: QT[:, i, :], lambda i: KT[:, i, :],
                                 lambda i, k: V[:, k, i * 64:(i + 1) * 64], 64, 96 ** -0.5, [*qt, *kt])
            qk_free = pe_last()
            o0 = turn_o(0, o)
            MT = QKT[:, 0:8 * S].rearrange("p (k s) -> p k s", k=8)
            RT = QKT[:, 8 * S:12 * S].rearrange("p (k s) -> p k s", k=4)
            mt = turn_heads(MT, MST, 8, P, mr, qk_free)
            rt = turn_heads(RT, RST, 4, P, rs, qk_free)
            for t in range(T):
                o = causal_heads(t, 8, lambda i: MT[64 * (i % 2):64 * (i % 2) + 64, i // 2, :],
                                 lambda i: MT[64 * (i % 2):64 * (i % 2) + 64, 4 + i // 2, :],
                                 lambda i, k: V[:, k, 512 + i * 64:512 + (i + 1) * 64], 64, 0.125, mt)
            o1 = turn_o(1, o)
            dec = const("decay").rearrange("p (h k) -> p h k", h=4)
            for t in range(T):
                kl = P * (t + 1)
                d = scores(t, 4, lambda i: RT[64 * (i % 2):64 * (i % 2) + 64, i // 2, :],
                           lambda i: RT[64 * (i % 2):64 * (i % 2) + 64, 2 + i // 2, :], rt)
                fill()
                for i in range(4):
                    p_ = pos_of(i)
                    a = dve.do(lambda i=i, p_=p_, t=t, kl=kl: nc.vector.tensor_tensor(
                        SC[:, p_, 0:kl], scp[:, p_, 0:kl], dec[:, i, t * P:t * P + kl], ALU.mult), d, p_free[0])
                sc_free[0] = a
                b, last = weighted(t, 4, lambda i: SC[:, pos_of(i), :],
                                   lambda i, k: V[:, k, 1024 + i * P:1024 + (i + 1) * P], P, [a])
                fill()
                ob = O[:, t, :].rearrange("p (h d) -> p h d", h=4)
                o = dve.do(lambda ob=ob, b=b: nc.vector.tensor_copy(ob, bank[b][:, :].rearrange("p (h d) -> p h d", h=4)),
                           last, o_free[0])
                bank_free[b] = o
                mean, var, ok = norm_stats(ob, 4, P, 64, GN_EPS, False, o)
                for h in range(4):
                    oh = ob[:, h, :]
                    a = dve.do(lambda oh=oh, var=var, mean=mean, h=h: nc.vector.tensor_scalar(
                        oh, oh, mean[:, h:h + 1], var[:, h:h + 1], ALU.subtract, ALU.mult), ok)
                ot = O[:, t, :]
                a = dve.do(lambda ot=ot: nc.vector.tensor_tensor(ot, ot, par2_("ret_gn_w_2"), ALU.mult), a)
                a = dve.do(lambda ot=ot: nc.vector.tensor_tensor(ot, ot, par2_("ret_gn_b_2"), ALU.add), a)
                rg = V[:, t, 1536:2048]
                th = TMP2[:, 0:512]
                s_ = act.do(lambda rg=rg: nc.scalar.activation(th, rg, ACT.Tanh, scale=0.5), rv, rope_done[-1:], a)
                s_ = dve.do(lambda rg=rg: nc.vector.scalar_tensor_tensor(th, th, 1.0, rg, ALU.add, ALU.mult), s_)
                o = dve.do(lambda ot=ot: nc.vector.scalar_tensor_tensor(ot, th, 0.5, ot, ALU.mult, ALU.mult), s_, a)
            v_free[0] = pe_last()
            v_free2 = o
            fill(12)
            o2 = turn_o(2, o)
            m = branches(("w_branch_mla_2", "w_branch_moba_2", "w_branch_ret_2"), (o0, o1, o2))
            ot_free[0] = pe_last()
            x = mix_out("w_out_2", 1.0, [*m, *x_ok])
            h_free[0] = pe_last()
            h = rms_norm(H, X, par2_("mlp_norm_2"), NORM_EPS, D, [*x, h_free[0]])
            xt = turn_x(H, h)
            h_free[0] = pe_last()
            UT = A[:, 0:32 * S].rearrange("p (k s) -> p k s", k=32)
            ud = []
            for j in range(16):
                (w,), loaded = take("w_mlp_up_2")
                b, v, last = features_major(w, 0, XT, [loaded, *xt])
                release(last)
                u = UT[:, 2 * j:2 * j + 2, :]
                bank_free[b] = act.do(lambda u=u, v=v: nc.scalar.activation(u, v, ACT.Relu), last)
                ud.append(dve.do(lambda u=u: nc.vector.tensor_tensor(u, u, u, ALU.mult), bank_free[b]))
            yv = scp[:, :, :].rearrange("p a s -> p (a s)").rearrange("p (t n) -> p t n", t=T)
            for j in range(16):
                (w,), loaded = take("w_mlp_down_2")
                waits = [loaded, ud[j], sc_free[0]]
                for k in range(2):
                    for t in range(T):
                        for n in range(2):
                            last = mm(yv[:, t, n * 512:(n + 1) * 512], UT[:, 2 * j + k, t * P:(t + 1) * P],
                                      w[:, k, n * 512:(n + 1) * 512], j == 0 and k == 0, j == 15 and k == 1, *waits)
                            waits = []
                release(last)
            x = []
            for t in range(T):
                x.append(dve.do(lambda t=t: nc.vector.tensor_tensor(X[:, t, :], X[:, t, :], yv[:, t, :], ALU.add), last))
            sc_free[0] = x[-1]
            a_free[0] = last
            x_ok[:] = x
            par_free[:] = [*h, x[-1]]
            if l == DEPTH - 1:
                y = rms_norm(H, X, par2_("final_norm_2"), NORM_EPS, D, [*x, h_free[0]])
                for t in range(T):
                    o = load(sp, out[t], H[:, t, :], "l_out", y)
                sp.items.append((lambda: nc.sync.nop(), [o], Token(None)))

        for l in range(DEPTH):
            first_layer(l)
        c_in[:] = [load(pool, CST[:, C_N:C_N + C2_N], consts[P * (C_N + C1_N):].rearrange("(p n) -> p n", p=P), "l_cst2", x_ok)]
        for l in range(DEPTH):
            second_layer(l)
        assert taken[0] == len(STREAM)
        for q in (pe, dve, act, pool, sp):
            q.number()
        block = ctx.enter_context(nc.Block())

        @block.sync
        def _(e):
            sp.emit()

        @block.tensor
        def _(e):
            pe.emit()

        @block.vector
        def _(e):
            dve.emit()

        @block.scalar
        def _(e):
            act.emit()

        @block.gpsimd
        def _(e):
            pool.emit()


def constants():
    c = {}
    c["ident"] = np.eye(P)
    q = np.arange(P)
    c["caus"] = np.where(q[None, :] <= q[:, None], 0.0, NEG)
    lg = np.log(np.float32(1.0) - np.float32(2.0) ** (-5.0 - np.arange(4, dtype=np.float32))).astype(np.float64)
    s = np.arange(S)
    diff = s[:, None] - s[None, :]
    dec = np.where(diff[None] >= 0, np.exp(lg[:, None, None] * np.maximum(diff, 0)[None]), 0.0)
    dec = dec.reshape(4, T, P, S)
    c["decay"] = np.concatenate([dec[:, 0, :, 0:P], dec[:, 1]], 2).transpose(1, 0, 2).reshape(P, -1)

    def inv(dim, theta):
        return (np.float32(1.0) / (np.float32(theta) ** (np.arange(0, dim, 2, dtype=np.float32) / np.float32(dim)))).astype(np.float32)

    c["invf"] = np.broadcast_to(inv(16, 500000.0), (P, 8))
    for dim, theta in ((16, 500000.0), (32, 500000.0), (64, 10000.0)):
        ang = (np.arange(S, dtype=np.float32)[:, None] * inv(dim, theta)[None, :]).astype(np.float32).astype(np.float64)
        co, si = np.cos(ang), np.sin(ang)
        c[f"c{dim}"] = np.concatenate([co, co], 1).reshape(T, P, dim).transpose(1, 0, 2).reshape(P, -1)
        c[f"s{dim}"] = np.concatenate([-si, si], 1).reshape(T, P, dim).transpose(1, 0, 2).reshape(P, -1)
    c["iota8"] = np.broadcast_to(np.arange(8), (P, 8))
    c["nhalf"] = np.full((P, 8), -0.5)
    c["before"] = q[:, None] < q[None, :]
    c["iota"] = np.broadcast_to(np.arange(SLOTS), (P, SLOTS))
    c["one"] = np.ones((P, 1))
    return np.concatenate([np.concatenate([np.asarray(c[n], np.float32).reshape(P, m) for n, m in table], 1).reshape(-1)
                           for table in (C_TABLE, C1_TABLE, C2_TABLE)])


def kernel(**inputs):
    import numpy as _np
    import concourse.bacc as _bacc
    from concourse import mybir as _mybir
    from concourse.bass_utils import run_bass_kernel_spmd as _run

    a = {k: _np.asarray(v) for k, v in inputs.items()}
    arrays = {}
    stream = _np.empty(AT[-1], _np.float32)
    for i, block in enumerate(STREAM):
        at = 0
        dst = stream[AT[i]:AT[i + 1]].reshape(P, -1)
        for name, idx, k0, kt, c0, c1 in block:
            w = a[name][idx].reshape(-1, P, a[name].shape[-1])[k0:k0 + kt, :, c0:c1]
            n = kt * (c1 - c0)
            dst[:, at:at + n].reshape(P, kt, c1 - c0)[:] = w.transpose(1, 0, 2)
            at += n
    arrays["wts"] = stream
    flat = lambda name, l: a[name].reshape(-1) if name == "final_norm_2" else a[name][l].reshape(-1)
    arrays["par1"] = _np.concatenate([flat(n, l) for l in range(DEPTH) for n, _ in P1])
    arrays["par2"] = _np.concatenate([flat(n, l) for l in range(DEPTH) for n, _ in P2])
    arrays["consts"] = constants()
    arrays["pos"] = _np.ascontiguousarray(a["positions"].reshape(T, P).T)
    x = a["x"].reshape(S, D)
    arrays["x0"] = _np.ascontiguousarray(x.reshape(T, P, D).transpose(1, 0, 2))
    arrays["x0T"] = _np.ascontiguousarray(x.T.reshape(KD, P, S).transpose(1, 0, 2))
    p = a["p"].reshape(DEPTH, S, 256)
    arrays["pT"] = _np.ascontiguousarray(p.transpose(0, 2, 1).reshape(DEPTH, 2, P, S).transpose(0, 2, 1, 3))

    nc = _bacc.Bacc("TRN2", target_bir_lowering=False, num_devices=1)
    args = {n: nc.dram_tensor(n, v.shape, _mybir.dt.from_np(v.dtype), kind="ExternalInput").ap() for n, v in arrays.items()}
    out = nc.dram_tensor("out", (T, P, D), _mybir.dt.float32, kind="ExternalOutput").ap()
    build(nc, out=out, **args)
    r = _run(nc, [arrays], core_ids=[0])
    return r.results[0]["out"].reshape(1, S, D)
```

```python
import math
from contextlib import ExitStack

import numpy as np
import concourse.bass as bass
from concourse import mybir

F32 = mybir.dt.float32
F32R = mybir.dt.float32r
I32 = mybir.dt.int32
U32 = mybir.dt.uint32
ALU = mybir.AluOpType
ACT = mybir.ActivationFunctionType
AX = mybir.AxisListType

P = 128
S = 256
T = S // P
D = 1024
KD = D // P
DEPTH = 2
NG, EPG, NE, DE = 4, 8, 32, 256
TOPK = 64
ALPHA = (2 * DEPTH) ** 0.25
LN_EPS = 1e-5
NORM_EPS = 1e-6
GN_EPS = 1e-5
NEG = -1e30
GONE = -3e38
MAGIC = 12582912.0
DFF = 4096

W1 = dict(zip(("dq", "dk", "dv", "sq", "sk", "sv", "iq", "ik", "iw", "ga", "gb"),
              np.cumsum([0, 512, 512, 512, 512, 512, 512, 512, 64, 8, 1024]).tolist()))
W2 = dict(zip(("cq", "ckv", "kr", "mq", "mk", "mv", "rq", "rk", "rv", "rg", "g0", "g1", "g2"),
              np.cumsum([0, 256, 128, 32, 512, 512, 512, 256, 256, 512, 512, 1024, 1024]).tolist()))

BLK = 2048
RING = 3
CAP = 64
SLOTS = 2 * S
WORDS = DEPTH * (D * (W1["gb"] + D) + 2 * 512 * D + D * D + D * (NG + NE) + 256 * D + D * D + NE * 3 * D * DE
                 + D * (W2["g2"] + D) + 256 * 768 + P * 1024 + 3 * 512 * D + D * D + 2 * D * DFF)


def offsets(table):
    at, out = 0, {}
    for name, n in table:
        out[name] = (at, n)
        at += n
    return out, at


COLS = [(n, l, m) for l in range(DEPTH) for n, m in
        (("ln1_g", 8), ("ln1_b", 8), ("ln2_g", 8), ("ln2_b", 8), ("diff_subln_g", 1),
         ("attn_norm_2", 8), ("mlp_norm_2", 8), ("mla_q_norm_2", 2), ("mla_kv_norm_2", 1),
         ("ret_gn_w_2", 4), ("ret_gn_b_2", 4))]
COL_AT, COL_N = offsets([((n, l), m) for n, l, m in COLS])
ROWS = [(n, l) for l in range(DEPTH) for n in ("ln1_g", "ln1_b", "ln2_g", "ln2_b", "small")] + [("final_norm_2", None)]
SMALL = ["b_route_group", "b_route_expert", "diff_lambda"]

C_TABLE = [("ident", 128), ("caus", 128), ("invf", 8), ("iota8", 8), ("nhalf", 8)]
C1_TABLE = [("before", 128), ("iota", SLOTS), ("one", 1)]
C2_TABLE = [("ret", T * 8), ("c16", 2 * 16), ("s16", 2 * 16), ("c32", 2 * 32), ("s32", 2 * 32),
            ("c64", 2 * 64), ("s64", 2 * 64)]
C_AT, C_N = offsets(C_TABLE)
C1_AT, C1_N = offsets(C1_TABLE)
C2_AT, C2_N = offsets(C2_TABLE)
CX_AT = {n: (C_N + a, m) for at in (C1_AT, C2_AT) for n, (a, m) in at.items()} | C_AT


def width(block):
    return sum(kt * (c1 - c0) for _, _, _, kt, c0, c1 in block)


class Token:

    def __init__(self, sem):
        self.sem, self.value, self.marked = sem, None, False


class Queue:

    def __init__(self, eng, sem):
        self.eng, self.sem, self.items = eng, sem, []

    def do(self, fn, *waits):
        token = Token(self.sem)
        flat = [x for w in waits for x in ([] if w is None else w if isinstance(w, list) else [w])]
        for w in flat:
            w.marked = True
        self.items.append((fn, flat, token))
        return token

    def dma(self, fn, done, *waits):
        self.do(fn, *waits)
        self.items[-1] = (fn, self.items[-1][1], done)
        return done

    def number(self):
        n = 0
        for _, _, token in self.items:
            if isinstance(token, Token) and token.value is None and token.marked:
                n += 1
                token.value = n

    def branch(self, flag, other, *waits):
        self.do(None, *waits)
        fn, flat, token = self.items.pop()
        self.items.append(((flag, other), flat, token))

    def emit(self, seen=None):
        seen = dict(seen or {})
        for fn, waits, token in self.items:
            for w in waits:
                if seen.get(id(w.sem), 0) < w.value:
                    self.eng.wait_ge(w.sem, w.value)
                    seen[id(w.sem)] = w.value
            if isinstance(fn, tuple):
                assert not token.marked
                flag = self.eng.value_load(fn[0], min_val=0, max_val=1)
                with self.eng.If(flag > 0):
                    fn[1].emit(seen)
                continue
            ins = fn()
            if token.marked and token.sem is self.sem:
                ins.then_inc(self.sem, 1)


class Pairs(list):
    pass


class DmaDone:

    def __init__(self, sem, value):
        self.sem, self.value, self.marked = sem, value, True


def build(nc, wts, rows, cols, consts, pos, x0, x0T, pT, out, order):
    taken, at = [], []
    ctx = ExitStack()
    with ctx:
        def sb(name, *shape, dt=F32):
            return ctx.enter_context(nc.sbuf_tensor(name, [P, *shape], dt))

        def sem(name):
            return ctx.enter_context(nc.semaphore(name))

        pe = Queue(nc.tensor, sem("pe"))
        dve = Queue(nc.vector, sem("dve"))
        act = Queue(nc.scalar, sem("act"))
        pool = Queue(nc.gpsimd, sem("pool"))
        sp = Queue(nc.sync, sem("sp"))

        X = sb("X", T, D)
        XT = [sb(f"XT{i}", KD, S, dt=F32R) for i in "hl"]
        FA = sb("FA", 4096, dt=F32R)
        WS = [[sb(f"WS{i}{j}", BLK, dt=F32R) for i in "hl"] for j in range(2)]
        A = sb("A", 36 * 256)
        STA = A[:, 0:2048]
        STB = A[:, 2048:5120]
        QKT = A[:, 5120:9216]
        V = sb("V", 4096)
        SC = sb("SC", 8, S)
        PT = sb("PT", 8, 2, P)
        O = sb("O", T, 512)
        GT = sb("GT", KD, S)
        H = sb("H", T, D)
        TMP = sb("TMP", 1024)
        TMP2 = sb("TMP2", 1536)
        ring = [sb(f"ring{i}", BLK) for i in range(RING)]
        PR = sb("PR", D)
        PC = sb("PC", COL_N)
        CST = sb("CST", C_N + max(C1_N, C2_N))
        sm = sb("sm", 512)
        comb = sb("comb", T, NE)
        OH = sb("OH", 2, T, NE)
        MK = sb("MK", T, NE)
        PS = sb("PS", T, NE)
        OFF = sb("OFF", NE)
        offi = sb("offi", NE, dt=I32)
        flag = sb("flag", 1, dt=I32)
        rt = sb("rt", 32)
        posi = sb("posi", T, dt=I32)
        idx8 = sb("idx8", T, 8, dt=U32)
        ropeb = sb("ropeb", 2, T, 16)
        work = TMP2[:, 1024:1536].rearrange("p (t s) -> p t s", t=T)
        prm = TMP[:, 512:512 + 292]
        VT = V[:, 0:3072].rearrange("p (t c) -> p t c", t=T)
        SRG = V[:, 3072:4096].rearrange("p (k s) -> p k s", k=4)
        SCF = SC[:, :, :].rearrange("p h s -> p (h s)")
        MG = H[:, :, :].rearrange("p t d -> p (t d)").rearrange("p (k s) -> p k s", k=KD)
        MGS = [FA[:, i * 2048:(i + 1) * 2048].rearrange("p (k s) -> p k s", k=KD) for i in range(2)]
        OTS = [FA[:, i * 1024:(i + 1) * 1024].rearrange("p (k s) -> p k s", k=4) for i in range(2)]
        CTS = [FA[:, 2048 + i * 768:2048 + (i + 1) * 768].rearrange("p (k s) -> p k s", k=3) for i in range(2)]
        PTS = [FA[:, i * 512:(i + 1) * 512].rearrange("p (k s) -> p k s", k=2) for i in range(2)]

        def const(name):
            a, n = CX_AT[name]
            return CST[:, a:a + n]

        def col(name, l, c):
            a, n = COL_AT[name, l]
            return PC[:, a + c:a + c + 1]

        ident = const("ident")
        scp = ctx.enter_context(nc.psum_tensor("scp", [P, 8, S], F32))
        bank = [ctx.enter_context(nc.psum_tensor(f"bank{i}", [P, 512], F32)) for i in range(4)]
        yv = scp[:, :, :].rearrange("p a s -> p (a s)").rearrange("p (t n) -> p t n", t=T)

        def flat(waits):
            out_ = []
            for w in waits:
                out_ += flat(w) if isinstance(w, (list, tuple)) else [w] if w is not None else []
            return out_

        dma_n = {}

        def load(q, dst, src, name, *waits):
            if name not in dma_n:
                dma_n[name] = [sem(name), 0]
            s = dma_n[name]
            s[1] += 16
            return q.dma(lambda: q.eng.dma_start(dst, src).then_inc(s[0], 16), DmaDone(s[0], s[1]), *flat(waits))

        free_bufs = []
        uses, lent = {}, set()
        fetched = []
        split_at = {}
        split_free = [[None], [None]]
        n_split = [0]

        def lend(name, buf, *tokens):
            if name not in uses:
                uses[name] = [sem(f"w_{name}"), 0]
            lent.add(name)
            free_bufs.insert(0, (name, buf, flat(tokens)))

        def give_back(name, buf, token):
            if name in lent:
                free_bufs.append((name, buf, [token]))

        def recall(*names):
            lent.difference_update(names)
            free_bufs[:] = [b for b in free_bufs if b[0] in lent]

        for i in range(RING):
            lend(f"ring{i}", ring[i])

        def fetch(i, spec):
            assert len(fetched) == i
            name, buf, tokens = free_bufs.pop(0)
            uses[name][1] += 16
            s, n = uses[name][0], width(spec)
            start = at[-1][0] + at[-1][1] if at else 0
            at.append((start, P * n))
            src = wts[start:start + P * n].rearrange("(p n) -> p n", p=P)
            landed = sp.dma(lambda: nc.sync.dma_start(buf[:, 0:n], src).then_inc(s, 16), DmaDone(s, uses[name][1]), *tokens)
            fetched.append((name, buf, landed, spec))

        def is_raw(spec):
            return spec[0][0] == "w_exp_down"

        def split(i):
            name, buf, landed, spec = fetched[i]
            n = width(spec)
            hi, lo = WS[n_split[0] % 2]
            free = split_free[n_split[0] % 2]
            done = []
            half = n // 2
            for c0, c1 in ((0, half), (half, n)):
                h_ = act.do(lambda c0=c0, c1=c1: nc.scalar.copy(hi[:, c0:c1], buf[:, c0:c1]), landed, *free)
                done.append(dve.do(lambda c0=c0, c1=c1: nc.vector.tensor_tensor(
                    lo[:, c0:c1], buf[:, c0:c1], hi[:, c0:c1].bitcast(F32), ALU.subtract), h_, *free))
            give_back(name, buf, done[-1])
            split_at[i] = (hi, lo, done[-1], n_split[0] % 2)
            n_split[0] += 1

        def views(buf, spec):
            a, out_ = 0, []
            for _, _, _, kt, c0, c1 in spec:
                n = kt * (c1 - c0)
                out_.append(buf[:, a:a + n].rearrange("p (k n) -> p k n", k=kt))
                a += n
            return out_

        current = [None]
        spare, pace = [], [1]

        def spread_out(n):
            for _ in range(min(n, len(spare))):
                spare.pop(0)()

        def no_more_than(n):
            spread_out(max(len(spare) - n, 0))

        def take(*spec, whole=False):
            i = len(taken)
            spec = list(spec)
            taken.append(spec)
            assert order is None or order[i] == spec, (order[i], spec)
            raw = is_raw(spec)
            ahead = [] if order is None else [j for j in range(i + 1, min(i + 3, len(order))) if not is_raw(order[j])][:1 + raw]
            for j in [i] + ahead:
                while len(fetched) <= j:
                    fetch(len(fetched), order[len(fetched)] if order is not None else spec)
                if not is_raw(fetched[j][3]) and j not in split_at:
                    split(j)
            current[0] = i
            spread_out(pace[0])
            if raw:
                return views(fetched[i][1], spec), fetched[i][2]
            hi, lo, ok, _ = split_at[i]
            if whole:
                return [p_[:, 0:width(spec)] for p_ in (hi, lo)], ok
            return list(zip(views(hi, spec), views(lo, spec))), ok

        def release(token):
            i = current[0]
            if is_raw(taken[i]):
                name, buf, _, _ = fetched[i]
                give_back(name, buf, token)
            else:
                split_free[split_at[i][3]][:] = [token]

        bank_free = [None] * 4
        bank_at = [0]

        def next_bank():
            bank_at[0] += 1
            return (bank_at[0] - 1) % 4

        turn = [0]

        def copy(q, dst, src, *waits):
            if q is act:
                return act.do(lambda: nc.scalar.copy(dst, src), *waits)
            return dve.do(lambda: nc.vector.tensor_copy(dst, src), *waits)

        def either():
            turn[0] += 1
            return act if turn[0] % 2 else dve

        def mm(dst, lhsT, rhs, start, stop, *waits):
            return pe.do(lambda: nc.tensor.matmul(dst, lhsT, rhs, start=start, stop=stop), *waits)

        def mm3(dst, l, r, start, stop, *waits):
            mm(dst, l[0], r[0], start, False, *waits)
            mm(dst, l[0], r[1], False, False)
            return mm(dst, l[1], r[0], False, stop)

        def cut(pair, *ix):
            return [p_[(slice(None), *ix)] for p_ in pair]

        def pe_last():
            return pe.items[-1][2]

        def tokens_major(spec, src, ready, kt=KD):
            (w,), loaded = take(spec)
            n = w[0].shape[2]
            b = next_bank()
            v = bank[b][:, 0:T * n].rearrange("p (t n) -> p t n", t=T)
            waits = flat([loaded, bank_free[b], [] if isinstance(ready, Pairs) else ready])
            for t in range(T):
                for k in range(kt):
                    if isinstance(ready, Pairs):
                        waits += flat([ready[k // 2]])
                    last = mm3(v[:, t, :], cut(src, k, slice(t * P, (t + 1) * P)), cut(w, k), k == 0, k == kt - 1, *waits)
                    waits = []
            release(last)
            return b, v, last

        def features_major(w, m0, src, waits, kt=KD, ready=None):
            b = next_bank()
            v = bank[b][:, :].rearrange("p (m s) -> p m s", m=2)
            waits = flat([waits, bank_free[b]])
            for m in range(2):
                for k in range(kt):
                    if ready is not None:
                        waits += flat([ready[k // 2]])
                    c = (m0 + m) * P
                    last = mm3(v[:, m, :], cut(w, k, slice(c, c + P)), cut(src, k), k == 0, k == kt - 1, *waits)
                    waits = []
            return b, v, last

        def turned(pieces, ready):
            b = next_bank()
            waits = flat([ready, bank_free[b]])
            c = pieces[0].shape[1]
            for j, src in enumerate(pieces):
                last = pe.do(lambda j=j, src=src: nc.tensor.transpose(bank[b][0:c, j * P:(j + 1) * P], src, ident), *waits)
                waits = []
            return b, last

        def transposes(dst, pieces, ready, free):
            done = []
            for i0 in range(0, len(pieces), 4):
                part = pieces[i0:i0 + 4]
                b, last = turned(part, ready)
                c = part[0].shape[1]
                bank_free[b] = copy(either(), dst(i0, len(part)), bank[b][0:c, 0:len(part) * P], last, *flat([free]))
                done.append(bank_free[b])
            return done

        def turn_heads(dst, st, nblk, w, ready, free):
            pieces = [st[:, t, k * w:(k + 1) * w] for k in range(nblk) for t in range(T)]
            f = dst.rearrange("p k s -> p (k s)")
            return transposes(lambda i0, m: f[:, i0 * P:(i0 + m) * P], pieces, ready, free)

        tmp_free = [None, None]

        def turn_split(dst, chunks, ready, free, scale=None, bias=None, gate=None):
            done = Pairs()
            hi, lo = dst
            for c0 in range(0, len(chunks), 2):
                pair = chunks[c0:c0 + 2]
                b, last = turned([f(t) for f in pair for t in range(T)], ready[c0 // 2] if isinstance(ready, Pairs) else ready)
                n = len(pair)
                if scale is None:
                    v = bank[b][:, 0:n * S].rearrange("p (c s) -> p c s", c=n)
                    h_, l_ = hi[:, c0:c0 + n, :], lo[:, c0:c0 + n, :]
                    a = act.do(lambda h_=h_, v=v: nc.scalar.copy(h_, v), last, *flat([free]))
                    a = dve.do(lambda h_=h_, l_=l_, v=v: nc.vector.tensor_tensor(l_, v, h_.bitcast(F32), ALU.subtract), a, *flat([free]))
                    bank_free[b] = a
                    done.append(a)
                    continue
                if bias is None:
                    for i in range(n):
                        a = act.do(lambda h_=hi[:, c0 + i, :], v=bank[b][:, i * S:(i + 1) * S], c=c0 + i: nc.scalar.activation(
                            h_, v, ACT.Copy, scale=scale(c)), last, *flat([free]))
                    for i in range(n):
                        bank_free[b] = dve.do(
                            lambda h_=hi[:, c0 + i, :], l_=lo[:, c0 + i, :], v=bank[b][:, i * S:(i + 1) * S], c=c0 + i:
                            nc.vector.scalar_tensor_tensor(l_, v, scale(c), h_.bitcast(F32), ALU.mult, ALU.subtract), a, *flat([free]))
                    done.append(bank_free[b])
                    continue
                j = (c0 // 2) % 2
                Y = (TMP, TMP2)[j][:, 0:n * S]
                waits = [last, tmp_free[j], *rope_done[-1:]]
                for i in range(n):
                    c = c0 + i
                    v = bank[b][:, i * S:(i + 1) * S]
                    y = Y[:, i * S:(i + 1) * S]
                    if j == 0:
                        a = act.do(lambda y=y, v=v, c=c: nc.scalar.activation(y, v, ACT.Identity, scale=scale(c), bias=bias(c)), *waits)
                    else:
                        a = dve.do(lambda y=y, v=v, c=c: nc.vector.tensor_scalar(y, v, scale(c), bias(c), ALU.mult, ALU.add), *waits)
                bank_free[b] = a
                if gate is not None:
                    for i in range(n):
                        y = Y[:, i * S:(i + 1) * S]
                        a2 = dve.do(lambda y=y, c=c0 + i: nc.vector.scalar_tensor_tensor(y, y, 0.5, gate(c), ALU.mult, ALU.mult), a)
                    a = a2
                y = Y.rearrange("p (c s) -> p c s", c=n)
                h_, l_ = hi[:, c0:c0 + n, :], lo[:, c0:c0 + n, :]
                h1 = act.do(lambda h_=h_, y=y: nc.scalar.copy(h_, y), a, *flat([free]))
                a = dve.do(lambda h_=h_, l_=l_, y=y: nc.vector.tensor_tensor(l_, y, h_.bitcast(F32), ALU.subtract), h1, *flat([free]))
                tmp_free[j] = a
                done.append(a)
            return done

        def turn_x(src, ready, scale, bias=None):
            chunks = [lambda t, c=c: src[:, t, c * P:(c + 1) * P] for c in range(KD)]
            return turn_split(XT, chunks, ready, xt_free[0], scale, bias)

        xt_free = [None]

        def rope(st, heads, lo, hw, cc, ss, ready):
            n = T * heads * 2 * hw
            a = TMP[:, 0:n].rearrange("p (t h d) -> p t h d", t=T, h=heads)
            b = TMP2[:, 0:n].rearrange("p (t h d) -> p t h d", t=T, h=heads)
            toks = []
            for t in range(T):
                def tab(v, d0, d1, t=t):
                    return v[:, t, d0:d1].unsqueeze(1).broadcast_to([P, heads, d1 - d0])
                x = st[:, t, :, lo:lo + 2 * hw]
                x1 = st[:, t, :, lo:lo + hw]
                x2 = st[:, t, :, lo + hw:lo + 2 * hw]
                o1 = dve.do(lambda t=t, x=x: nc.vector.tensor_tensor(a[:, t], x, tab(cc, 0, 2 * hw, t), ALU.mult),
                            *flat([ready, rope_done[-1:], tmp_free]))
                dve.do(lambda t=t, x2=x2: nc.vector.tensor_tensor(b[:, t, :, 0:hw], x2, tab(ss, 0, hw, t), ALU.mult))
                o3 = dve.do(lambda t=t, x1=x1: nc.vector.tensor_tensor(b[:, t, :, hw:2 * hw], x1, tab(ss, hw, 2 * hw, t), ALU.mult))
                toks.append((x, o1, o3))
            for t, (x, o1, o3) in enumerate(toks):
                last = dve.do(lambda t=t, x=x: nc.vector.tensor_tensor(x, a[:, t], b[:, t], ALU.add), o1, o3)
            rope_done.append(last)
            return last

        rope_done = []

        todo = []

        def fill(n=1):
            for _ in range(min(n, len(todo))):
                todo.pop(0)()

        def pos_of(i):
            return ((i % 2) + 2 * (i // 4)) * 2 + (i // 2) % 2

        sc_free, p_free, pt_free, o_free = [None], [None], [None], [None]
        a_free, v_free, ot_free, h_free, gt_free = [None], [None], [None], [None], [None]

        def scores(t, heads, q_of, k_of, ready):
            kl = P * (t + 1)
            waits = flat([ready, sc_free[0]])
            done = []
            for i in range(heads):
                last = mm(scp[:, pos_of(i), 0:kl], q_of(i)[:, t * P:(t + 1) * P], k_of(i)[:, 0:kl], True, True, *waits)
                waits = []
                if i % 4 == 3:
                    done.append(last)
            return done

        def softmax_parts(t, heads, scale, done, extra=None):
            kl = P * (t + 1)
            m0 = t * P if extra is None else 0
            mask = const("caus") if extra is None else work[:, t, 0:kl]
            mx = sm[:, 0:8]
            nb = sm[:, 8 + 8 * t:16 + 8 * t]
            z = sm[:, 24 + 8 * t:32 + 8 * t]
            rz = sm[:, 40 + 8 * t:48 + 8 * t]
            es = []
            for g in range(heads // 4):
                h = slice(4 * g, 4 * g + 4)
                v = scp[:, h, m0:kl]
                m = mask.unsqueeze(1).broadcast_to([P, 4, kl - m0])
                a = dve.do(lambda v=v, m=m: nc.vector.tensor_tensor(v, v, m, ALU.add), *flat([done[g], extra]))
                b = dve.do(lambda h=h: nc.vector.tensor_reduce(mx[:, h], scp[:, h, 0:kl], AX.X, ALU.max), a)
                c = dve.do(lambda h=h: nc.vector.tensor_scalar(nb[:, h], mx[:, h], -scale, None, ALU.mult), b)
                for i in range(4 * g, 4 * g + 4):
                    e = act.do(lambda i=i: nc.scalar.activation(SC[:, i, 0:kl], scp[:, i, 0:kl], ACT.Exp, bias=nb[:, i:i + 1],
                                                                scale=scale, accum_out=z[:, i:i + 1]), c, p_free[0])
                es.append(e)
            sc_free[0] = e
            return es, lambda: dve.do(lambda: nc.vector.reciprocal(rz, z), e), rz

        def turn_p(t, heads, p_of, p_ready):
            nk = t + 1
            f = PT[:, :, :, :].rearrange("p h k q -> p (h k q)")
            done = []
            n_ = heads // len(p_ready)
            for g, rdy in enumerate(p_ready):
                j = g * n_ * nk
                pieces = [p_of(i)[:, k * P:(k + 1) * P] for i in range(g * n_, (g + 1) * n_) for k in range(nk)]
                done += transposes(lambda i0, n, j=j: f[:, (j + i0) * P:(j + i0 + n) * P], pieces, rdy, pt_free[0])
            p_free[0] = pe_last()
            return done

        def weighted(t, heads, v_of, vw, turned_ok):
            nk = t + 1
            f = PT[:, :, :, :].rearrange("p h k q -> p (h k q)")
            b = next_bank()
            waits = flat([turned_ok, bank_free[b]])
            for i in range(heads):
                for k in range(nk):
                    j = i * nk + k
                    last = mm(bank[b][:, i * vw:(i + 1) * vw], f[:, j * P:(j + 1) * P], v_of(i, k), k == 0, k == nk - 1, *waits)
                    waits = []
            pt_free[0] = last
            return b, last

        def attend(heads, p_of, q_of, k_of, v_of, vw, ready, soft, finish, fills, between=None):
            s0 = soft(0, scores(0, 8, q_of, k_of, ready))
            if between is not None:
                between()
            fill(fills[0])
            d = scores(1, 8, q_of, k_of, ready)
            turned_ok = turn_p(0, heads, p_of, s0[0])
            s1 = soft(1, d)
            finish(0, *weighted(0, heads, v_of, vw, turned_ok), s0)
            fill(fills[1])
            turned_ok = turn_p(1, heads, p_of, s1[0])
            fill(fills[2])
            return finish(1, *weighted(1, heads, v_of, vw, turned_ok), s1)

        def causal_heads(q_of, k_of, v_of, scale, ready, fills, extra=(None, None), between=None):
            def finish(t, b, last, soft):
                _, inverse, rz = soft
                rdy = inverse()
                for i in range(8):
                    p_ = pos_of(i)
                    tok = dve.do(lambda i=i, p_=p_: nc.vector.tensor_scalar(
                        O[:, t, i * 64:(i + 1) * 64], bank[b][:, i * 64:(i + 1) * 64], rz[:, p_:p_ + 1], None, ALU.mult),
                        last, rdy, o_free[0])
                bank_free[b] = tok
                return tok
            return attend(8, lambda i: SC[:, pos_of(i), :], q_of, k_of, v_of, 64, ready,
                          lambda t, d: softmax_parts(t, 8, scale, d, extra[t]), finish, fills, between)

        def half(v, i):
            return v[64 * (i % 2):64 * (i % 2) + 64, i // 2, :]

        def turn_o(ready, scale=None, bias=None, gate=None):
            chunks = [lambda t, c=c: O[:, t, c * P:(c + 1) * P] for c in range(4)]
            done = turn_split(OTS, chunks, ready, ot_free[0], scale, bias, gate)
            o_free[0] = pe_last()
            return done

        stat_free = [None]
        MIX_STATS = sm[:, 464:512].rearrange("p (t c) -> p t c", t=T)

        def norm_stats(src, groups, n, base, eps, rms, ready, parts=None):
            chunk = min(n, 512)
            nch = n // chunk
            st = sm[:, 128:128 + 6 * nch * groups]
            last = ready
            if parts is not None:
                st, nch = parts
            for g in range(groups if parts is None else 0):
                for c in range(nch):
                    o = st[:, (g * nch + c) * 6:(g * nch + c) * 6 + 6]
                    s_ = src[:, g, c * chunk:(c + 1) * chunk]
                    last = dve.do(lambda o=o, s_=s_: nc.vector.bn_stats(o, s_), *(flat([ready, stat_free[0]]) if g + c == 0 else []))
            mv = sm[:, base:base + 2 * groups]
            for g in range(groups):
                i_ = st[:, g * nch * 6:(g + 1) * nch * 6]
                last2 = dve.do(lambda g=g, i_=i_: nc.vector.bn_aggr(mv[:, 2 * g:2 * g + 2], i_), *flat([last]))
            stat_free[0] = last2
            mean = mv.rearrange("p (g c) -> p g c", c=2)[:, :, 0]
            var = mv.rearrange("p (g c) -> p g c", c=2)[:, :, 1]
            if rms:
                sq = sm[:, 120:120 + groups]
                a = dve.do(lambda: nc.vector.tensor_tensor(sq, mean, mean, ALU.mult), last2)
                last2 = dve.do(lambda: nc.vector.tensor_tensor(var, var, sq, ALU.add), a)
            e_ = dve.do(lambda: nc.vector.tensor_scalar(var, var, eps, None, ALU.add), last2)
            return mean, var, pool.do(lambda: nc.gpsimd.tensor_tensor(var, var, const("nhalf")[:, 0:groups], ALU.pow), e_)

        def add_y(t, n, *waits):
            x_ = X[:, t, n * 512:(n + 1) * 512]
            a = dve.do(lambda: nc.vector.tensor_tensor(x_, x_, yv[:, t, n * 512:(n + 1) * 512], ALU.add), *flat(waits))
            return dve.do(lambda: nc.vector.bn_stats(MIX_STATS[:, t, n * 6:n * 6 + 6], x_), a, stat_free[0])

        def normed(dst, src, eps, n, ready, rms, base=64, parts=None):
            stats = [norm_stats(src[:, t:t + 1, :], 1, n, base + 2 * t, eps, rms, ready, None if parts is None else (parts[0][:, t, :], parts[1]))
                     for t in range(T)]
            mean, var, ok = stats[1]
            shift = sm[:, 120 + base % 2:121 + base % 2]
            if not rms:
                ok = dve.do(lambda mean=mean, var=var: nc.vector.scalar_tensor_tensor(
                    shift, mean, -1.0, var, ALU.mult, ALU.mult), ok)
            last = Pairs()
            step = min(n, 512)
            for c in range(0, n, step):
                (d0, x0_), (d1, x1) = ((dst[:, t, c:c + step], src[:, t, c:c + step]) for t in range(T))
                mean, var, ok0 = stats[0]
                if rms:
                    toks = [dve.do(lambda d=d0, x_=x0_, var=var: nc.vector.tensor_scalar(d, x_, var, None, ALU.mult), ok0)]
                    var = stats[1][1]
                    toks.append(act.do(lambda d=d1, x_=x1, var=var: nc.scalar.activation(d, x_, ACT.Copy, scale=var), ok, *flat([ready])))
                else:
                    toks = [dve.do(lambda d=d0, x_=x0_, mean=mean, var=var: nc.vector.tensor_scalar(
                        d, x_, mean, var, ALU.subtract, ALU.mult), ok0)]
                    var = stats[1][1]
                    toks.append(act.do(lambda d=d1, x_=x1, var=var: nc.scalar.activation(
                        d, x_, ACT.Identity, scale=var, bias=shift), ok, *flat([ready])))
                last += [toks] * (step // 256 or 1)
            return last

        def spread(dst, name, l, c0, n, *waits):
            r = ROWS.index((name, l))
            m = len(ROWS)
            return mm(dst, ident[0:m, r:r + 1].broadcast_to([m, P]), PR[0:m, c0:c0 + n], True, True, *flat([waits, p_in]))

        def affine(name, l, ready):
            g, b = yv[:, 0, :], yv[:, 1, :]
            for c in range(2):
                s1 = spread(g[:, c * 512:(c + 1) * 512], name + "_g", l, c * 512, 512, sc_free[0])
            for c in range(2):
                s2 = spread(b[:, c * 512:(c + 1) * 512], name + "_b", l, c * 512, 512)
            done = []
            for t in range(T):
                a = dve.do(lambda t=t: nc.vector.tensor_tensor(X[:, t, :], H[:, t, :], g, ALU.mult), *flat([s1, ready]))
                done.append(dve.do(lambda t=t: nc.vector.tensor_tensor(X[:, t, :], X[:, t, :], b, ALU.add), a, s2))
            sc_free[0] = done[-1]
            return done

        def gates(name, l, c0, src_ready):
            done = []

            def block(j):
                (w,), loaded = take((name, (l,), 0, KD, c0 + 256 * j, c0 + 256 * (j + 1)))
                b, v, last = features_major(w, 0, XT, [loaded], ready=src_ready)
                release(last)
                dst = GT[:, 2 * j:2 * j + 2, :]
                bank_free[b] = act.do(lambda: nc.scalar.activation(dst, v, ACT.Tanh, scale=0.5), last, *flat([gt_free[0]]))
                done.append(bank_free[b])
            return [lambda j=j: block(j) for j in range(4)], done

        def branch(name, l, first, ot, g_done, m_done):
            def block(h):
                (w,), loaded = take((name, (l,), 0, 4, 512 * h, 512 * (h + 1)))
                for m in range(2):
                    b, v, last = features_major(w, 2 * m, OTS, [loaded], kt=4, ready=ot)
                    c = 4 * h + 2 * m
                    g = GT[:, c:c + 2, :]
                    M = MG[:, c:c + 2, :]
                    dst = M if first else g
                    a = dve.do(lambda g=g, v=v, dst=dst: nc.vector.scalar_tensor_tensor(
                        dst, g, 1.0, v, ALU.add, ALU.mult), *flat([last, g_done, h_free[0] if first else None]))
                    bank_free[b] = a
                    if not first:
                        a = dve.do(lambda M=M, g=g: nc.vector.tensor_tensor(M, M, g, ALU.add), a, m_done[2 * h + m])
                    m_done[2 * h + m] = a
                release(last)
                if h:
                    ot_free[0] = last
                    gt_free[0] = m_done[-1]
            return [lambda h=h: block(h) for h in range(2)]

        def merged(m_done):
            done = Pairs()
            for j in range(4):
                M = MG[:, 2 * j:2 * j + 2, :]
                h_, l_ = MGS[0][:, 2 * j:2 * j + 2, :], MGS[1][:, 2 * j:2 * j + 2, :]
                a = act.do(lambda M=M, h_=h_: nc.scalar.copy(h_, M), m_done[j], ot_free[0])
                done.append(dve.do(lambda M=M, h_=h_, l_=l_: nc.vector.tensor_tensor(l_, M, h_.bitcast(F32), ALU.subtract),
                                   a, ot_free[0]))
            h_free[0] = done[-1]
            return done

        def mix_out(name, l, ready, x_ready):
            done = []
            for c in range(4):
                b, v, last = tokens_major((name, (l,), 0, KD, c * 256, (c + 1) * 256), MGS, ready)
                xs = X[:, :, c * 256:(c + 1) * 256]
                bank_free[b] = dve.do(lambda xs=xs, v=v: nc.vector.scalar_tensor_tensor(
                    xs, v, 0.5, xs, ALU.mult, ALU.add), *flat([last, x_ready]))
                for t in range(T):
                    done.append(dve.do(lambda c=c, t=t: nc.vector.bn_stats(
                        MIX_STATS[:, t, c * 6:c * 6 + 6], X[:, t, c * 256:(c + 1) * 256]), bank_free[b], stat_free[0]))
            ot_free[0] = last
            return done

        def projection(spec, dsts, src_ready, *free):
            b, v, last = tokens_major(spec, XT, src_ready)
            done = [act.do(lambda dst=dst, c0=c0, c1=c1: nc.scalar.copy(dst, v[:, :, c0:c1]), *flat([last, free]))
                    for dst, c0, c1 in dsts]
            bank_free[b] = done[-1]
            return done

        def columns(name, l, c0, n, dst, src_ready, *free):
            done = []
            for c in range(0, n, 256):
                done += projection((name, (l,), 0, KD, c0 + c, c0 + c + 256), [(dst[:, :, c:c + 256], 0, 256)], src_ready, *free)
            return done

        def cs(n):
            return (const(f"c{n}").rearrange("p (t d) -> p t d", t=T), const(f"s{n}").rearrange("p (t d) -> p t d", t=T))

        XR = A[:, 5120:7168].rearrange("p (k s) -> p k s", k=KD)
        xt_in = [load(q, XR[:, h:h + 4, :], x0T[:, h:h + 4, :], f"l_xt{h}") for q, h in ((act, 0), (sp, 4))]
        c_in = [load(act, CST[:, 0:C_N], consts[0:P * C_N].rearrange("(p n) -> p n", p=P), "l_cst"),
                load(act, posi[:, :], pos, "l_pos")]
        x_ready = [Pairs()]
        for h in range(2):
            hi, lo = cut(XT, slice(4 * h, 4 * h + 4))
            xh = act.do(lambda h=h, hi=hi: nc.scalar.copy(hi, XR[:, 4 * h:4 * h + 4, :]), xt_in[h])
            xl = dve.do(lambda h=h, hi=hi, lo=lo: nc.vector.tensor_tensor(
                lo, XR[:, 4 * h:4 * h + 4, :], hi.bitcast(F32), ALU.subtract), xh)
            x_ready[0] += [xl, xl]

        RC, RS = ropeb[:, 0], ropeb[:, 1]

        def tables():
            posf = sm[:, 100:102]
            ang, kk, r, ab = (TMP[:, 16 * i:16 * i + 16].rearrange("p (t d) -> p t d", t=T) for i in range(4))
            a = dve.do(lambda: nc.vector.tensor_copy(posf, posi[:, :]), *c_in)
            for t in range(T):
                a2 = dve.do(lambda t=t: nc.vector.tensor_scalar(ang[:, t, :], const("invf"), posf[:, t:t + 1], None, ALU.mult), a)
            a = dve.do(lambda: nc.vector.tensor_scalar(kk, ang, 1.0 / (2 * math.pi), MAGIC, ALU.mult, ALU.add), a2)
            a = dve.do(lambda: nc.vector.tensor_scalar(kk, kk, -MAGIC, None, ALU.add), a)
            parts, rest = [], 2 * math.pi
            for bits in (4, 12, 20):
                c = math.floor(rest * 2 ** bits) / 2 ** bits
                parts.append(c)
                rest -= c
            src_ = ang
            for c in (*parts, rest):
                a = dve.do(lambda c=c, src_=src_: nc.vector.scalar_tensor_tensor(r, kk, -c, src_, ALU.mult, ALU.add), a)
                src_ = r
            a = dve.do(lambda: nc.vector.tensor_scalar(r, r, -3.1415925, 3.1415925, ALU.max, ALU.min), a)
            b_ = dve.do(lambda: nc.vector.tensor_scalar(ab, r, -1.0, None, ALU.mult), a)
            b_ = dve.do(lambda: nc.vector.tensor_tensor(ab, ab, r, ALU.max), b_)
            b_ = dve.do(lambda: nc.vector.tensor_scalar(ab, ab, -1.0, math.pi / 2, ALU.mult, ALU.add), b_)
            e1 = act.do(lambda: nc.scalar.activation(RS[:, :, 8:16], r, ACT.Sin), a)
            e2 = act.do(lambda: nc.scalar.activation(RC[:, :, 0:8], ab, ACT.Sin), b_)
            dve.do(lambda: nc.vector.tensor_scalar(RS[:, :, 0:8], RS[:, :, 8:16], -1.0, None, ALU.mult), e1)
            rope_done.append(dve.do(lambda: nc.vector.tensor_copy(RC[:, :, 8:16], RC[:, :, 0:8]), e2))

        x_ok = [None]
        loaded_late = {}

        def late_loads(after):
            loaded_late["c1"] = load(pool, CST[:, C_N:C_N + C1_N],
                                     consts[P * C_N:P * (C_N + C1_N)].rearrange("(p n) -> p n", p=P), "l_cst1", after)
            p_in.extend([load(pool, PR[0:len(ROWS), :], rows, "l_rows", after), load(pool, PC[:, :], cols, "l_cols", after)])
            x_ok[0] = [load(pool, X[:, :, :], x0, "l_x", after)]

        p_in = []
        yc_last = []

        def first_layer(l):
            lam_init = 0.8 - 0.6 * math.exp(-0.3 * l)
            xr = x_ready[0]
            IST = STB[:, 0:T * 640].rearrange("p (t c) -> p t c", t=T)
            IW = sm[:, 104:104 + 16].rearrange("p (t h) -> p t h", t=T)
            done = columns("w_in", l, W1["iq"], 512, IST, xr, a_free[0])
            if l == 0:
                late_loads(done)
                tables()
            done += projection(("w_in", (l,), 0, KD, W1["ik"], W1["ga"]),
                               [(IST[:, :, 512:576], 0, 64), (IST[:, :, 576:640], 0, 64), (IW, 64, 72)], xr, a_free[0])
            xs_ok = [pool.do(lambda: nc.gpsimd.tensor_scalar(X[:, :, :], X[:, :, :], ALPHA, None, ALU.mult), *flat(x_ok))]
            iw = dve.do(lambda: nc.vector.tensor_scalar(IW, IW, 8 ** -0.5, None, ALU.mult), *done)
            rot = rope(IST.rearrange("p t (h d) -> p t h d", d=64), 10, 0, 8, RC, RS, [done, rope_done[0]])
            SST = STA.rearrange("p (t c) -> p t c", t=T)
            sdone = columns("w_in", l, W1["sq"], 1024, SST, xr, a_free[0])
            b = next_bank()
            last = spread(bank[b][:, 0:292], "small", l, 0, 292, bank_free[b])
            par = bank_free[b] = dve.do(lambda b=b: nc.vector.tensor_copy(prm, bank[b][:, 0:292]), *flat([last, rope_done[-1:], tmp_free]))
            lp = prm[:, 36:292].rearrange("p (a b d) -> p a b d", a=2, b=2)
            pr = sm[:, 256:384].rearrange("p (a d) -> p a d", a=2)
            sums, lam = sm[:, 460:462], sm[:, 462:463]
            a = dve.do(lambda: nc.vector.tensor_tensor(pr, lp[:, :, 0], lp[:, :, 1], ALU.mult), par)
            a = dve.do(lambda: nc.vector.tensor_reduce(sums, pr, AX.X, ALU.add), a)
            a = act.do(lambda: nc.scalar.activation(sums, sums, ACT.Exp), a)
            a = dve.do(lambda: nc.vector.tensor_tensor(lam, sums[:, 1:2], sums[:, 0:1], ALU.subtract), a)
            nlam = dve.do(lambda: nc.vector.tensor_scalar(lam, lam, -lam_init, None, ALU.add), a)
            IT = QKT[:, 0:5 * S].rearrange("p (k s) -> p k s", k=5)
            it = turn_heads(IT, IST, 5, P, rot, [a_free[0], xl])
            ist_free = pe_last()
            srot = rope(SST.rearrange("p t (h d) -> p t h d", d=64), 16, 0, 8, RC, RS, sdone)
            DST = STB[:, 0:2048].rearrange("p (t c) -> p t c", t=T)
            sel, ddone, vdone = [None, None], [], []
            RL = [PT[:, :, :, :].rearrange("p h k q -> p (h k q)")[:, 0:8 * P].rearrange("p (h s) -> p h s", h=8), SC]
            rl_free = [pt_free, p_free]

            def index_steps(t, e):
                kl = P * (t + 1)
                wk, dg = work[:, t, 0:kl], work[:, t, t * P:kl]
                m8 = sm[:, 80 + 8 * t:88 + 8 * t]
                at_ = [e]

                def step(fn, *waits):
                    def go():
                        at_[0] = sel[t] = dve.do(fn, at_[0], *waits)
                    return go

                def summed(i):
                    p_, w = pos_of(i), IW[:, t, i:i + 1]
                    go = step(lambda: nc.vector.tensor_scalar(wk, RL[t][:, p_, 0:kl], w, None, ALU.mult) if i == 0 else
                              nc.vector.scalar_tensor_tensor(wk, RL[t][:, p_, 0:kl], w, wk, ALU.mult, ALU.add), iw)
                    if i < 7:
                        return go

                    def end():
                        go()
                        rl_free[t][0] = at_[0]
                    return end
                steps = [summed(i) for i in range(8)]
                steps.append(step(lambda: nc.vector.tensor_tensor(dg, dg, const("caus"), ALU.add)))
                for _ in range(TOPK // 8):
                    steps.append(step(lambda: nc.vector.max(m8, wk)))
                    steps.append(step(lambda: nc.vector.match_replace(wk, m8, wk, GONE)))
                steps.append(step(lambda: nc.vector.tensor_scalar(wk, wk, -2e38, NEG, ALU.is_gt, ALU.mult)))
                steps.append(step(lambda: nc.vector.tensor_tensor(dg, dg, const("caus"), ALU.add)))
                return steps

            both = []
            for t in range(T):
                kl = P * (t + 1)
                d = scores(t, 8, lambda i: half(IT, i), lambda i: IT[64 * (i % 2):64 * (i % 2) + 64, 4, :], it)
                e = act.do(lambda kl=kl, t=t: nc.scalar.activation(RL[t][:, :, 0:kl], scp[:, :, 0:kl], ACT.Relu, scale=0.125),
                           *flat([d, rl_free[t][0]]))
                sc_free[0] = e
                both.append(index_steps(t, e))
                if t == 0:
                    ddone += columns("w_in", l, W1["dq"], 512, DST[:, :, 0:512], xr, ist_free)
            spare.extend(f for pair in zip(*both) for f in pair)
            pace[0] = 9
            ddone += columns("w_in", l, W1["dk"], 512, DST[:, :, 512:1024], xr, ist_free)
            drot = rope(DST.rearrange("p t (h d) -> p t h d", d=64), 16, 0, 8, RC, RS, ddone)
            vdone += columns("w_in", l, W1["dv"], 512, VT[:, :, 512:1024], xr, v_free[0])
            vdone += columns("w_in", l, W1["sv"], 512, VT[:, :, 0:512], xr, v_free[0])
            no_more_than(0)
            pace[0] = 1
            it_free = pe_last()
            work_g, g_done = gates("w_in", l, W1["ga"], xr)
            todo.extend(work_g)
            ST = QKT[:, 0:8 * S].rearrange("p (k s) -> p k s", k=8)
            DT = QKT[:, 8 * S:16 * S].rearrange("p (k s) -> p k s", k=8)
            str_ = turn_heads(ST, SST, 8, P, srot, it_free)
            fill()
            dtr = turn_heads(DT, DST, 8, P, drot, [it_free, xl])
            def diff_soft(t, d):
                kl = P * (t + 1)
                es, inverse, rz = softmax_parts(t, 8, 0.125, d)
                w1 = sm[:, 56:64]
                a = dve.do(lambda: nc.vector.tensor_scalar(w1, rz, lam, None, ALU.mult), inverse(), nlam)
                done = []
                for h in range(4):
                    p0, p1 = pos_of(2 * h), pos_of(2 * h + 1)
                    x1, x0_ = SC[:, p1, 0:kl], SC[:, p0, 0:kl]
                    b = dve.do(lambda x1=x1, p1=p1: nc.vector.tensor_scalar(x1, x1, w1[:, p1:p1 + 1], None, ALU.mult), a, es)
                    done.append(dve.do(lambda x0_=x0_, x1=x1, p0=p0: nc.vector.scalar_tensor_tensor(
                        x0_, x0_, rz[:, p0:p0 + 1], x1, ALU.mult, ALU.add), b))
                return ([[done[1]], [done[3]]] if t else [[done[3]]],)

            def diff_finish(t, b, last, _):
                ob = O[:, t, :].rearrange("p (h d) -> p h d", h=4)
                o = dve.do(lambda: nc.vector.tensor_copy(ob, bank[b][:, :].rearrange("p (h d) -> p h d", h=4)), last, o_free[0])
                bank_free[b] = o
                mean, var, ok = norm_stats(ob, 4, P, 64, LN_EPS, True, o)
                for h in range(4):
                    oh = ob[:, h, :]
                    o = dve.do(lambda oh=oh, h=h: nc.vector.tensor_scalar(
                        oh, oh, var[:, h:h + 1], 1.0 - lam_init, ALU.mult, ALU.mult), ok)
                return o

            o = attend(4, lambda i: SC[:, pos_of(2 * i), :], lambda i: half(DT, i), lambda i: half(DT, 8 + i),
                       lambda i, k: VT[:, k, 512 + i * P:512 + (i + 1) * P], P, [dtr, vdone], diff_soft, diff_finish, (1, 1, 1))
            m_done = [None] * 4

            def diff_out():
                ota = turn_o([o, p_in], scale=lambda c: col("diff_subln_g", l, 0))
                todo.extend(branch("w_branch_diff", l, True, ota, g_done, m_done))
                work_g, more = gates("w_in", l, W1["gb"], xr)
                todo.extend(work_g)
                return more

            g_done2 = []
            o2 = causal_heads(lambda i: half(ST, i), lambda i: half(ST, 8 + i), lambda i, k: VT[:, k, i * 64:(i + 1) * 64], 0.125,
                              [str_, vdone], (1, 2, 1), sel, lambda: g_done2.append(diff_out()))
            v_free[0] = pe_last()
            fill(9)
            otb = turn_o(o2)
            for f in branch("w_branch_dsa", l, False, otb, g_done2[0], m_done):
                f()
            xt_free[0] = pe_last()
            m = merged(m_done)
            x = mix_out("w_out", l, m, xs_ok)
            PR_ = TMP2[:, 0:512].rearrange("p (k s) -> p k s", k=2)
            pt_in = load(sp, PR_, pT[l], "l_pt", rope_done[-1:])
            ph = act.do(lambda: nc.scalar.copy(PTS[0], PR_), pt_in, ot_free[0])
            pl = dve.do(lambda: nc.vector.tensor_tensor(PTS[1], PR_, PTS[0].bitcast(F32), ALU.subtract), ph, ot_free[0])
            z = normed(H, X, LN_EPS, D, [*x, h_free[0]], False, parts=(MIX_STATS, 4))
            PW = GT[:, :, :].rearrange("p k s -> p (k s)").rearrange("p (t d) -> p t d", t=T)
            pw = []
            (w,), loaded = take(("w_ple", (l,), 0, 2, 0, D))

            def ple_part(c):
                b = next_bank()
                v = bank[b][:, :].rearrange("p (t n) -> p t n", t=T)
                waits = flat([loaded, pl, bank_free[b]])
                for t in range(T):
                    for k in range(2):
                        last = mm3(v[:, t, :], cut(PTS, k, slice(t * P, (t + 1) * P)), cut(w, k, slice(c * 256, (c + 1) * 256)),
                                   k == 0, k == 1, *waits)
                        waits = []
                bank_free[b] = act.do(lambda: nc.scalar.copy(PW[:, :, c * 256:(c + 1) * 256], v), *flat([last, gt_free[0]]))
                pw.append(bank_free[b])
                return last

            ple_part(0)
            ple_part(1)
            xt = turn_x(H, z, lambda c: col("ln1_g", l, c), lambda c: col("ln1_b", l, c))
            ple_part(2)
            last = ple_part(3)
            release(last)
            ot_free[0] = last
            x = affine("ln1", l, z)
            NR = NG + NE
            ws, loaded = take(*((name, (l,), k, 1, 0, n) for k in range(KD) for name, n in (("w_route_group", NG), ("w_route_expert", NE))),
                              whole=True)
            w = [p_.rearrange("p (k n) -> p k n", k=KD) for p_ in ws]
            b = next_bank()
            lg = sm[:, 384:384 + T * NR].rearrange("p (t c) -> p t c", t=T)
            waits = flat([loaded, xt, bank_free[b]])
            for t in range(T):
                for k in range(KD):
                    last = mm3(bank[b][:, t * 64:t * 64 + NR], cut(XT, k, slice(t * P, (t + 1) * P)), cut(w, k),
                               k == 0, k == KD - 1, *waits)
                    waits = []
            release(last)
            for t in range(T):
                a = dve.do(lambda t=t, b=b: nc.vector.tensor_tensor(lg[:, t, :], bank[b][:, t * 64:t * 64 + 36], prm[:, 0:36], ALU.add),
                           last, par)
            bank_free[b] = a
            val = rt[:, 0:4].rearrange("p (c t) -> p c t", c=2)
            chains = [route(t, lg[:, t, :], [OH[:, c, t, :] for c in range(2)], [val[:, c, t:t + 1] for c in range(2)], a) for t in range(T)]
            spare.extend(f for pair in zip(chains[0][0], chains[1][0]) for f in pair)
            gp = []
            tg = [TMP[:, 0:512], TMP2[:, 512:1024]]
            tg_free = [flat([tmp_free]), rope_done[-1:]]

            def ple_gate(c):
                b, v, last = tokens_major(("w_ple_gate", (l,), 0, KD, c * 256, (c + 1) * 256), XT, xt)
                g = tg[c % 2].rearrange("p (t n) -> p t n", t=T)
                xs = PW[:, :, c * 256:(c + 1) * 256]
                bank_free[b] = act.do(lambda: nc.scalar.activation(g, v, ACT.Tanh, scale=0.5), last, *tg_free[c % 2])
                a = dve.do(lambda: nc.vector.scalar_tensor_tensor(xs, g, 1.0, xs, ALU.add, ALU.mult), bank_free[b], *pw)
                tg_free[c % 2] = [a]
                gp.append(a)

            pace[0] = 20
            for c in range(3):
                ple_gate(c)
            no_more_than(0)
            pace[0] = 1
            chosen = [d[0] for _, d in chains]
            mk = dve.do(lambda: nc.vector.tensor_tensor(MK[:, :, :], OH[:, 0], OH[:, 1], ALU.add), chosen)
            b = next_bank()
            one = const("one")
            pp, cc = bank[b][:, 0:64], bank[b][:, 64:96]
            mm(pp[:, 0:32], const("before"), MK[:, 0, :], True, True, *flat([mk, bank_free[b], loaded_late["c1"]]))
            mm(pp[:, 32:64], one.broadcast_to([P, P]), MK[:, 0, :], True, False)
            mm(pp[:, 32:64], const("before"), MK[:, 1, :], False, True)
            for t in range(T):
                mm(cc, one.broadcast_to([P, P]), MK[:, t, :], t == 0, t == T - 1)
            for t in range(T):
                last = mm(bank[b][0:NE, 128:129], MK[:, t, :], one, t == 0, t == T - 1)
            cnt = rt[0:NE, 4:5]
            c1 = dve.do(lambda b=b: nc.vector.tensor_copy(cnt, bank[b][0:NE, 128:129]), last)
            cmx = rt[:, 5:6]
            p_ok = dve.do(lambda pp=pp: nc.vector.tensor_copy(PS[:, :, :], pp.rearrange("p (t e) -> p t e", t=T)), last)
            a = dve.do(lambda cc=cc: nc.vector.tensor_reduce(cmx, cc, AX.X, ALU.max), last)
            last = mm(bank[b][:, 96:128], cnt.broadcast_to([NE, P]), const("before")[0:NE, 0:NE], True, True, c1, p_ok, a)
            a = dve.do(lambda: nc.vector.tensor_scalar(cmx, cmx, CAP + 0.5, None, ALU.is_gt), a)
            fl = dve.do(lambda: nc.vector.tensor_copy(flag[:, :], cmx), a)
            o_ok = dve.do(lambda b=b: nc.vector.tensor_copy(OFF[:, :], bank[b][:, 96:128]), last)
            bank_free[b] = o_ok
            oi = dve.do(lambda: nc.vector.tensor_copy(offi[:, :], OFF[:, :]), o_ok)
            ple_gate(3)
            pos_, slot, vm, vo = (rt[:, 8 + 4 * i:12 + 4 * i].rearrange("p (c t) -> p c t", c=2) for i in range(4))
            tm = sm[:, 256:384].rearrange("p (c t e) -> p c t e", c=2, t=T)
            a = dve.do(lambda: nc.vector.tensor_tensor(PS[:, :, :], PS[:, :, :], OFF[:, :].unsqueeze(1).broadcast_to([P, T, NE]), ALU.add),
                       o_ok, p_ok)
            for c in range(2):
                a2 = dve.do(lambda c=c: nc.vector.tensor_tensor(tm[:, c], OH[:, c], PS[:, :, :], ALU.mult), a)
            a = dve.do(lambda: nc.vector.tensor_reduce(slot, tm, AX.X, ALU.add), a2)
            for c in range(2):
                a2 = dve.do(lambda c=c: nc.vector.tensor_tensor(
                    tm[:, c], OH[:, c], OFF[:, :].unsqueeze(1).broadcast_to([P, T, NE]), ALU.mult), a)
            a2 = dve.do(lambda: nc.vector.tensor_reduce(pos_, tm, AX.X, ALU.add), a2)
            a2 = dve.do(lambda: nc.vector.tensor_tensor(pos_, slot, pos_, ALU.subtract), a2)
            a2 = dve.do(lambda: nc.vector.scalar_tensor_tensor(vm, pos_, CAP - 0.5, val, ALU.is_lt, ALU.mult), a2)
            vok = dve.do(lambda: nc.vector.tensor_tensor(vo, val, vm, ALU.subtract), a2)
            s_ok = a
            G = SCF[:, 0:1024].rearrange("p (t s) -> p t s", t=T)
            CT = SCF[:, 0:1024].rearrange("p (j q) -> p j q", j=4)
            C = O
            iota = const("iota")
            gk = []
            for t in range(T):
                a = dve.do(lambda t=t: nc.vector.tensor_scalar(G[:, t, :], iota, slot[:, 0, t:t + 1], None, ALU.is_equal), s_ok,
                           p_free[0])
                gk.append(dve.do(lambda t=t: nc.vector.scalar_tensor_tensor(
                    G[:, t, :], iota, slot[:, 1, t:t + 1], G[:, t, :], ALU.is_equal, ALU.add), a))
            XG = A[:, 0:KD * (SLOTS + CAP)].rearrange("p (k s) -> p k s", k=KD)
            YC = A[:, KD * (SLOTS + CAP):2 * KD * (SLOTS + CAP)].rearrange("p (k s) -> p k s", k=KD)
            xg = [pool.do(lambda: nc.gpsimd.memset(XG[:, :, SLOTS:SLOTS + CAP], 0.0), v_free[0])]
            yz = pool.do(lambda: nc.gpsimd.memset(YC, 0.0), v_free[0])
            for k in range(KD):
                b = next_bank()
                waits = flat([gk, x, bank_free[b]])
                for t in range(T):
                    last = mm(bank[b][:, :], X[:, t, k * P:(k + 1) * P], G[:, t, :], t == 0, t == T - 1, *waits)
                    waits = []
                bank_free[b] = copy(either(), XG[:, k, 0:SLOTS], bank[b][:, :], last)
                xg.append(bank_free[b])
            x_read = last
            lend("PT", PT[:, :, :, :].rearrange("p h k q -> p (h k q)"), pt_free[0])
            lend("H", H[:, :, :].rearrange("p t d -> p (t d)"), x, xt)
            HE = [SCF[0:CAP, 1024 + i * 256:1280 + i * 256] for i in range(2)]
            HT = [SCF[:, 1536 + i * P:1536 + (i + 1) * P].rearrange("p (f s) -> p f s", f=2) for i in range(2)]
            XE = [[FA[:, (2 * i + j) * 512:(2 * i + j + 1) * 512].rearrange("p (k s) -> p k s", k=KD) for j in range(2)] for i in range(2)]
            he_free, xe_free = [p_free[0], p_free[0]], [ot_free[0], ot_free[0]]
            ht_ok, xe_ok, ht_free = [None, None], [None, None], [p_free[0], p_free[0]]
            first = {}

            def at_(q, e, *waits):
                def go():
                    first[q, e] = q.eng.value_load(offi[0:1, e:e + 1], min_val=0, max_val=SLOTS)
                q.do(go, *waits)

            def tokens_of(e):
                i = e % 2
                at_(act, e, oi)
                at_(dve, e, oi)
                hi, lo = XE[i]
                a = act.do(lambda: nc.scalar.copy(hi, XG[:, :, bass.ds(first[act, e], CAP)]), *flat([xg, xe_free[i]]))
                xe_ok[i] = dve.do(lambda: nc.vector.tensor_tensor(
                    lo, XG[:, :, bass.ds(first[dve, e], CAP)], hi.bitcast(F32), ALU.subtract), a)

            def down(e):
                i = e % 2
                (w,), loaded = take(("w_exp_down", (l, e // EPG, e % EPG), 0, 2, 0, D))
                b = next_bank()
                v = bank[b][:, :].rearrange("p (k s) -> p k s", k=KD)
                waits = flat([loaded, ht_ok[i], bank_free[b]])
                for m in range(KD):
                    for f in range(2):
                        last = mm(v[:, m, :], w[:, f, m * P:(m + 1) * P], HT[i][:, f, :], f == 0, f == 1, *waits)
                        waits = []
                release(last)
                ht_free[i] = last
                yc = act.do(lambda: nc.scalar.copy(YC[:, :, bass.ds(first[act, e], CAP)], v), last, yz, *yc_last)
                yc_last[:] = [yc]
                bank_free[b] = yc
                return last, yc

            cw = TMP2[:, 0:512]
            CTF = CT.rearrange("p j q -> p (j q)")
            c_ok, ple = [], []

            def weight(t, c):
                dst = cw if c else C[:, t, :]
                return lambda: c_ok.append(dve.do(lambda: nc.vector.tensor_scalar(
                    dst, iota, slot[:, c, t:t + 1], vm[:, c, t:t + 1], ALU.is_equal, ALU.mult), *flat([vok, o_free[0], ph, pl, c_ok[-1:]])))

            def both_weights(t):
                return lambda: c_ok.append(dve.do(lambda: nc.vector.tensor_tensor(C[:, t, :], C[:, t, :], cw, ALU.add), c_ok[-1]))

            def embedded(t):
                def go():
                    a = pool.do(lambda: nc.gpsimd.tensor_scalar(X[:, t, :], X[:, t, :], ALPHA, None, ALU.mult), *flat([x, x_read]))
                    ple.append(dve.do(lambda: nc.vector.scalar_tensor_tensor(
                        X[:, t, :], PW[:, t, :], 0.5, X[:, t, :], ALU.mult, ALU.add), *flat([a, gp])))
                return go
            weights_back = [f for t in range(T) for f in (weight(t, 0), weight(t, 1), both_weights(t))] + [embedded(t) for t in range(T)]
            tokens_of(0)
            for e in range(NE):
                if e == NE - 2:
                    recall("PT", "H", "GT")
                if e == 8:
                    lend("GT", GT[:, :, :].rearrange("p k s -> p (k s)"), ple)
                i = e % 2
                b = next_bank()
                v = bank[b][0:CAP, :].rearrange("p (g n) -> p g n", g=2)
                waits = flat([xe_ok[i], bank_free[b]])
                for n, name in enumerate(("w_exp_gate", "w_exp_up")):
                    (w,), loaded = take((name, (l, e // EPG, e % EPG), 0, KD, 0, DE))
                    waits.append(loaded)
                    for k in range(KD):
                        last = mm3(v[:, n, :], cut(XE[i], k), cut(w, k), k == 0, k == KD - 1, *waits)
                        waits = []
                    release(last)
                xe_free[i] = last
                if e + 1 < NE:
                    tokens_of(e + 1)
                g = HE[i]
                a = act.do(lambda g=g, v=v: nc.scalar.activation(g, v[:, 0], ACT.Tanh, scale=0.5), last, he_free[i])
                a = dve.do(lambda g=g, v=v: nc.vector.scalar_tensor_tensor(g, g, 1.0, v[:, 0], ALU.add, ALU.mult), a)
                h_ok = bank_free[b] = dve.do(lambda g=g, v=v: nc.vector.scalar_tensor_tensor(g, g, 0.5, v[:, 1], ALU.mult, ALU.mult), a)
                if e:
                    down(e - 1)
                if e == 2:
                    spare.extend(weights_back)
                if e == 7:
                    no_more_than(0)
                    ct = transposes(lambda i0, n: CTF[:, i0 * P:(i0 + n) * P],
                                    [C[:, t, j * P:(j + 1) * P] for j in range(4) for t in range(T)], c_ok, x_read)
                    o_free[0] = pe_last()
                b = next_bank()
                waits = flat([h_ok, bank_free[b]])
                for f in range(2):
                    last = pe.do(lambda b=b, f=f, g=g: nc.tensor.transpose(
                        bank[b][:, f * CAP:(f + 1) * CAP], g[:, f * P:(f + 1) * P], ident[0:CAP, 0:CAP]), *waits)
                    waits = []
                he_free[i] = last
                ht_ok[i] = bank_free[b] = dve.do(lambda b=b, i=i: nc.vector.tensor_copy(
                    HT[i], bank[b][:, 0:2 * CAP].rearrange("p (f s) -> p f s", f=2)), last, ht_free[i])
            last, yc = down(NE - 1)
            ot_free[0] = xe_free
            pt_free[0] = gt_free[0] = h_free[0] = last
            YS = V[:, :].rearrange("p (j d) -> p j d", j=4)
            ys = transposes(lambda i0, n: V[:, i0 * P:(i0 + n) * P],
                            [YC[:, k, j * P:(j + 1) * P] for j in range(4) for k in range(KD)], yc, v_free[0])
            a_free[0] = pe_last()
            waits = flat([ct, ys, sc_free[0]])
            for n in range(2):
                for t in range(T):
                    for j in range(4):
                        last = mm(yv[:, t, n * 512:(n + 1) * 512], CT[:, j, t * P:(t + 1) * P], YS[:, j, n * 512:(n + 1) * 512],
                                  j == 0, j == 3, *waits)
                        waits = []
                    a = add_y(t, n, last, ple)
            p_free[0] = v_free[0] = last
            sc_free[0] = a
            xt_free[0] = last
            overflow(l, a, fl, vok)
            z = normed(H, X, LN_EPS, D, [a, h_free[0]], False, parts=(MIX_STATS, 2))
            if l < DEPTH - 1:
                x_ready[0] = turn_x(H, z, lambda c: col("ln2_g", l, c), lambda c: col("ln2_b", l, c))
            x_ok[0] = affine("ln2", l, z)
            h_free[0] = [x_ok[0], pe_last()]

        def overflow(l, ready, flagged, vok):
            q = {e: Queue(e.eng, sem(f"over{l}_{i}")) for i, e in enumerate((pe, dve, act, pool))}
            qpe, qdve, qact, qpool = (q[e] for e in (pe, dve, act, pool))
            slots = [PT[:, :, :, :].rearrange("p h k q -> p (h k q)"), H[:, :, :].rearrange("p t d -> p (t d)"),
                     GT[:, :, :].rearrange("p k s -> p (k s)")]
            XA = V[:, 0:KD * S].rearrange("p (k s) -> p k s", k=KD)
            sems = [sem(f"over{l}_ring{i}") for i in range(3)]
            freed_ = []
            SG = [SCF[:, i * 512:(i + 1) * 512].rearrange("p (m s) -> p m s", m=2) for i in range(2)]
            HG = [SCF[:, 1024 + i * 512:1024 + (i + 1) * 512].rearrange("p (m s) -> p m s", m=2) for i in range(2)]
            CB = [O[:, i, 0:S] for i in range(2)]
            vo = rt[:, 20:24].rearrange("p (c t) -> p c t", c=2)
            names = ("w_exp_gate", "w_exp_up", "w_exp_down")
            for i in range(3 * NE):
                e = i // 3
                start, n = at[[b[0][:2] for b in taken].index((names[i % 3], (l, e // EPG, e % EPG)))]
                src = wts[start:start + n].rearrange("(p n) -> p n", p=P)
                turn_ = i // 3 + 1
                slot_token = Token(None)
                freed_.append(slot_token)
                qpool.items.append((lambda i=i, src=src: nc.gpsimd.dma_start(slots[i % 3], src).then_inc(sems[i % 3], 16),
                                    [freed_[i - 3]] if i >= 3 else [ready], DmaDone(sems[i % 3], 16 * turn_)))

            def got(i):
                kt = 2 if i % 3 == 2 else KD
                return slots[i % 3].rearrange("p (k n) -> p k n", k=kt), DmaDone(sems[i % 3], 16 * (i // 3 + 1))

            def through(i, token):
                freed_[i].twin = token

            xa = qdve.do(lambda: nc.vector.tensor_tensor(XA, XT[0][:, :, :].bitcast(F32), XT[1][:, :, :].bitcast(F32), ALU.add), ready)
            for t in range(T):
                a = qdve.do(lambda t=t: nc.vector.tensor_scalar(comb[:, t, :], OH[:, 0, t, :], vo[:, 0, t:t + 1], None, ALU.mult),
                            ready, vok)
                cm = qdve.do(lambda t=t: nc.vector.scalar_tensor_tensor(
                    comb[:, t, :], OH[:, 1, t, :], vo[:, 1, t:t + 1], comb[:, t, :], ALU.mult, ALU.add), a)
            free = [ready] * 4
            n = 0
            hg_free = [None, None]
            for e in range(NE):
                i = e % 2
                bs = [(n + j) % 4 for j in range(3)]
                n += 3
                prods = []
                for j in range(2):
                    w, loaded = got(3 * e + j)
                    v = bank[bs[j]][:, :].rearrange("p (m s) -> p m s", m=2)
                    waits = flat([loaded, xa, free[bs[j]], bank_free[bs[j]]])
                    for m in range(2):
                        for k in range(KD):
                            last = qpe.do(lambda v=v, w=w, m=m, k=k: nc.tensor.matmul(
                                v[:, m, :], w[:, k, m * P:(m + 1) * P], XA[:, k, :], start=(k == 0), stop=(k == KD - 1)), *waits)
                            waits = []
                    through(3 * e + j, last)
                    prods.append((v, last))
                waits = flat([cm, free[bs[2]], bank_free[bs[2]]])
                for t in range(T):
                    l3 = qpe.do(lambda t=t, e=e, b=bs[2]: nc.tensor.matmul(
                        bank[b][:, t * P:(t + 1) * P], comb[:, t, e:e + 1].broadcast_to([P, P]), ident, start=True, stop=True), *waits)
                    waits = []
                (g, l1), (u, l2) = prods
                a = qact.do(lambda g=g, i=i: nc.scalar.activation(SG[i], g, ACT.Tanh, scale=0.5), l1, hg_free[i], ready)
                free[bs[2]] = cb = qact.do(lambda i=i, b=bs[2]: nc.scalar.copy(CB[i], bank[b][:, 0:S]), l3)
                free[bs[0]] = a = qdve.do(lambda g=g, i=i: nc.vector.scalar_tensor_tensor(SG[i], SG[i], 1.0, g, ALU.add, ALU.mult), a)
                free[bs[1]] = a = qdve.do(lambda u=u, i=i: nc.vector.scalar_tensor_tensor(SG[i], SG[i], 0.5, u, ALU.mult, ALU.mult), a, l2)
                a = qdve.do(lambda i=i: nc.vector.tensor_tensor(
                    HG[i], SG[i], CB[i].unsqueeze(1).broadcast_to([P, 2, S]), ALU.mult), a, cb)
                w, loaded = got(3 * e + 2)
                waits = [loaded, a]
                for k in range(2):
                    for t in range(T):
                        for h in range(2):
                            last = qpe.do(lambda k=k, t=t, h=h, e=e, i=i, w=w: nc.tensor.matmul(
                                yv[:, t, h * 512:(h + 1) * 512], HG[i][:, k, t * P:(t + 1) * P],
                                w[:, k, h * 512:(h + 1) * 512], start=(e == 0 and k == 0), stop=(e == NE - 1 and k == 1)), *waits)
                            waits = []
                through(3 * e + 2, last)
                hg_free[i] = last
            for t in range(T):
                end = qdve.do(lambda t=t: nc.vector.tensor_tensor(X[:, t, :], X[:, t, :], yv[:, t, :], ALU.add), last)
                for h in range(2):
                    st_ok = qdve.do(lambda t=t, h=h: nc.vector.bn_stats(
                        MIX_STATS[:, t, 6 * h:6 * h + 6], X[:, t, 512 * h:512 * (h + 1)]), end)
            end = st_ok
            for fn, waits, token in qpool.items:
                waits[:] = [w.twin if hasattr(w, "twin") else w for w in waits]
                for w in waits:
                    w.marked = True
            for x in (qpe, qdve, qact, qpool):
                x.do(lambda: None, end)
                x.number()
            for e in (pe, dve, act, pool):
                e.branch(flag[0:1, 0:1], q[e], flagged, ready)

        def route(t, lg, hot, val, ready):
            b0 = 160 + 56 * t
            gp = sm[:, b0:b0 + 8]
            gmx, gz, gv = (sm[:, b0 + 8 + i:b0 + 9 + i] for i in range(3))
            emx, es = (sm[:, b0 + 12 + i:b0 + 13 + i] for i in range(2))
            oh = sm[:, b0 + 16:b0 + 24]
            e8 = sm[:, b0 + 24:b0 + 32]
            h1, h2 = sm[:, b0 + 32:b0 + 40], sm[:, b0 + 40:b0 + 48]
            m8 = sm[:, b0 + 48:b0 + 56]
            fi = sm[:, 336 + 8 * t:344 + 8 * t]
            sel = sm[:, 272 + 32 * t:304 + 32 * t].rearrange("p (g e) -> p g e", g=NG)
            le = lg[:, NG:NG + NE].rearrange("p (g e) -> p g e", g=NG)
            d = [ready]
            steps = []

            def step(fn, q=dve):
                def go():
                    d[0] = q.do(fn, d[0])
                steps.append(go)

            def one_hots(src, out_):
                step(lambda: nc.vector.max(m8, src))
                step(lambda: nc.vector.max_index(idx8[:, t, :], m8, src))
                step(lambda: nc.vector.tensor_copy(fi, idx8[:, t, :]))
                for i, o in enumerate(out_):
                    step(lambda i=i, o=o: nc.vector.tensor_scalar(o, const("iota8"), fi[:, i:i + 1], None, ALU.is_equal))

            step(lambda: nc.vector.memset(gp, -1.0))
            step(lambda: nc.vector.tensor_reduce(gmx, lg[:, 0:NG], AX.X, ALU.max))
            step(lambda: nc.vector.tensor_scalar(gmx, gmx, -1.0, None, ALU.mult))
            step(lambda: nc.scalar.activation(gp[:, 0:NG], lg[:, 0:NG], ACT.Exp, bias=gmx, accum_out=gz), act)
            one_hots(gp, [oh])
            step(lambda: nc.vector.reciprocal(gz, gz))
            step(lambda: nc.vector.tensor_tensor(gv, m8[:, 0:1], gz, ALU.mult))
            step(lambda: nc.vector.tensor_tensor(sel, le, oh[:, 0:NG].unsqueeze(2).broadcast_to([P, NG, EPG]), ALU.mult))
            step(lambda: nc.vector.tensor_reduce(e8, sel.rearrange("p g e -> p e g"), AX.X, ALU.add))
            step(lambda: nc.vector.tensor_reduce(emx, e8, AX.X, ALU.max))
            step(lambda: nc.vector.tensor_scalar(emx, emx, -1.0, None, ALU.mult))
            step(lambda: nc.scalar.activation(e8, e8, ACT.Exp, bias=emx, accum_out=es), act)
            step(lambda: nc.vector.reciprocal(es, es))
            step(lambda: nc.vector.tensor_scalar(e8, e8, es, None, ALU.mult))
            one_hots(e8, [h1, h2])
            step(lambda: nc.vector.tensor_tensor(es, m8[:, 0:1], m8[:, 1:2], ALU.add))
            step(lambda: nc.vector.reciprocal(es, es))
            step(lambda: nc.vector.tensor_tensor(es, es, gv, ALU.mult))
            for c, h in enumerate((h1, h2)):
                step(lambda c=c: nc.vector.tensor_tensor(val[c], m8[:, c:c + 1], es, ALU.mult))
                step(lambda c=c, h=h: nc.vector.tensor_tensor(
                    hot[c].rearrange("p (g e) -> p g e", g=NG), oh[:, 0:NG].unsqueeze(2).broadcast_to([P, NG, EPG]),
                    h.unsqueeze(1).broadcast_to([P, NG, EPG]), ALU.mult))
            return steps, d

        def second_layer(l):
            h = normed(H, X, NORM_EPS, D, flat([x_ok, c2_in, h_free[0]]), True, parts=(MIX_STATS, 2) if l else None)
            xr = turn_x(H, h, lambda c: col("attn_norm_2", l, c))
            h_free[0] = pe_last()
            W = "w_in_2"
            CS = QKT[:, 0:T * 416].rearrange("p (t c) -> p t c", t=T)
            cdone = projection((W, (l,), 0, KD, W2["cq"], W2["ckv"]), [(CS[:, :, 0:256], 0, 256)], xr, a_free[0])
            cdone += projection((W, (l,), 0, KD, W2["ckv"], W2["mq"]), [(CS[:, :, 256:416], 0, 160)], xr, a_free[0])
            MST = STA.rearrange("p (t c) -> p t c", t=T)
            a1 = normed(CS[:, :, 0:256], CS[:, :, 0:256], NORM_EPS, 256, cdone, True)
            a2 = normed(CS[:, :, 256:384], CS[:, :, 256:384], NORM_EPS, 128, cdone, True, base=72)
            kr = rope(CS[:, :, 384:416].unsqueeze(2), 1, 0, 16, *cs(32), cdone)
            mdone = columns(W, l, W2["mq"], 512, MST[:, :, 0:512], xr, a_free[0])
            chunks = [lambda t, c=c: CS[:, t, c * P:(c + 1) * P] for c in range(3)]
            ct = turn_split(CTS, chunks, [a1, a2], ot_free[0],
                            lambda c: col("mla_q_norm_2", l, c) if c < 2 else col("mla_kv_norm_2", l, 0))
            mdone += columns(W, l, W2["mk"], 512, MST[:, :, 512:1024], xr, a_free[0])
            QS = STB[:, 0:1536].rearrange("p (t c) -> p t c", t=T)
            KS = STB[:, 1536:3072].rearrange("p (t c) -> p t c", t=T)
            KS4 = KS.rearrange("p t (h d) -> p t h d", h=8)
            (w,), loaded = take(("mla_w_q_up_2", (l,), 0, 2, 0, 768))
            qd = []
            for c in range(3):
                b = next_bank()
                v = bank[b][:, :].rearrange("p (t n) -> p t n", t=T)
                waits = flat([loaded, ct, bank_free[b]])
                for t in range(T):
                    for k in range(2):
                        last = mm3(v[:, t, :], cut(CTS, k, slice(t * P, (t + 1) * P)), cut(w, k, slice(c * 256, (c + 1) * 256)),
                                   k == 0, k == 1, *waits)
                        waits = []
                bank_free[b] = act.do(lambda c=c, v=v: nc.scalar.copy(QS[:, :, c * 256:(c + 1) * 256], v), *flat([last, a_free[0]]))
                qd.append(bank_free[b])
            release(last)
            qr = rope(QS.rearrange("p t (h d) -> p t h d", h=8), 8, 64, 16, *cs(32), qd)
            (w,), loaded = take(("mla_w_kv_up_2", (l,), 0, 1, 0, 1024))
            kd = []
            for c in range(4):
                b = next_bank()
                v = bank[b][:, :].rearrange("p (t n) -> p t n", t=T)
                waits = flat([loaded, bank_free[b]])
                for t in range(T):
                    last = mm3(v[:, t, :], cut(CTS, 2, slice(t * P, (t + 1) * P)), cut(w, 0, slice(c * 256, (c + 1) * 256)),
                               True, True, *waits)
                    waits = []
                v4 = v.rearrange("p t (h d) -> p t h d", h=2)
                for t in range(T):
                    vd = VT[:, t, c * P:(c + 1) * P].rearrange("p (h d) -> p h d", h=2)
                    ks = KS4[:, t, 2 * c:2 * c + 2, 0:64]
                    act.do(lambda ks=ks, v4=v4, t=t: nc.scalar.copy(ks, v4[:, t, :, 0:64]), *flat([last, a_free[0]]))
                    bank_free[b] = act.do(lambda vd=vd, v4=v4, t=t: nc.scalar.copy(vd, v4[:, t, :, 64:128]), *flat([last, v_free[0]]))
                kd.append(bank_free[b])
            release(last)
            for t in range(T):
                kp = dve.do(lambda t=t: nc.vector.tensor_copy(
                    KS4[:, t, :, 64:96], CS[:, t, 384:416].unsqueeze(1).broadcast_to([P, 8, 32])), *flat([kr, a_free[0]]))
            mv = columns(W, l, W2["mv"], 512, VT[:, :, 512:1024], xr, v_free[0])
            QT = QKT[0:96, 0:8 * S].rearrange("p (k s) -> p k s", k=8)
            KT = QKT[0:96, 8 * S:16 * S].rearrange("p (k s) -> p k s", k=8)
            qt = turn_heads(QT, QS, 8, 96, qr, [a_free[0], kp, ct])
            rv = columns(W, l, W2["rv"], 512, VT[:, :, 1024:1536], xr, v_free[0])
            kt = turn_heads(KT, KS, 8, 96, [kd, kp], a_free[0])
            stb_free = pe_last()
            mr = rope(MST.rearrange("p t (h d) -> p t h d", d=64), 16, 0, 8, *cs(16), mdone)
            RST = STB[:, 0:1024].rearrange("p (t c) -> p t c", t=T)
            rdone = columns(W, l, W2["rq"], 512, RST, xr, stb_free)
            rr = rope(RST.rearrange("p t (h d) -> p t h d", d=64), 8, 0, 32, *cs(64), rdone)
            R3 = RST.rearrange("p t (h d) -> p (t h) d", d=64)
            rs = dve.do(lambda: nc.vector.tensor_tensor(R3, R3, const("ret").unsqueeze(2).broadcast_to([P, T * 8, 64]), ALU.mult), rr)
            srg = []

            def ret_gate(j):
                (w,), loaded = take((W, (l,), 0, KD, W2["rg"] + 256 * j, W2["rg"] + 256 * (j + 1)))
                b, v, last = features_major(w, 0, XT, [loaded], ready=xr)
                release(last)
                g = SRG[:, 2 * j:2 * j + 2, :]
                a = act.do(lambda: nc.scalar.activation(g, v, ACT.Tanh, scale=0.5), *flat([last, v_free[0]]))
                bank_free[b] = dve.do(lambda: nc.vector.scalar_tensor_tensor(g, g, 1.0, v, ALU.add, ALU.mult), a)
                srg.append(bank_free[b])

            g0, g0_done = gates(W, l, W2["g0"], xr)
            g1, g1_done = gates(W, l, W2["g1"], xr)
            g2, g2_done = gates(W, l, W2["g2"], xr)
            m_done = [None] * 4
            todo.extend(g0)
            todo.extend([lambda: ret_gate(0), lambda: ret_gate(1)])
            o = causal_heads(lambda i: QT[:, i, :], lambda i: KT[:, i, :], lambda i, k: VT[:, k, i * 64:(i + 1) * 64], 96 ** -0.5,
                             [qt, kt], (1, 2, 1))
            qk_free = pe_last()
            MT = QKT[:, 0:8 * S].rearrange("p (k s) -> p k s", k=8)
            RT = QKT[:, 8 * S:12 * S].rearrange("p (k s) -> p k s", k=4)
            mt = turn_heads(MT, MST, 8, P, mr, qk_free)
            fill(9)
            rtt = turn_heads(RT, RST, 4, P, rs, qk_free)
            o0 = o

            def mla_out():
                todo.extend(branch("w_branch_mla_2", l, True, turn_o(o0), g0_done, m_done))
                todo.extend(g1)

            o = causal_heads(lambda i: half(MT, i), lambda i: half(MT, 8 + i), lambda i, k: VT[:, k, 512 + i * 64:512 + (i + 1) * 64],
                             0.125, [mt, mv], (1, 2, 1), between=mla_out)
            fill(9)
            o1 = o
            for t in range(T):
                kl = P * (t + 1)
                d = scores(t, 4, lambda i: half(RT, i), lambda i: half(RT, 4 + i), rtt)
                w_ = flat([d, p_free[0]])
                if t:
                    dve.do(lambda: nc.vector.tensor_copy(SC[:, 0:4, 0:P], scp[:, 0:4, 0:P]), *w_)
                m = const("caus").unsqueeze(1).broadcast_to([P, 4, P])
                a = dve.do(lambda t=t, kl=kl, m=m: nc.vector.scalar_tensor_tensor(
                    SC[:, 0:4, t * P:kl], m, -1.0, scp[:, 0:4, t * P:kl], ALU.is_ge, ALU.mult), *w_)
                sc_free[0] = a
                if t == 0:
                    todo.extend(branch("w_branch_moba_2", l, False, turn_o(o1), g1_done, m_done))
                    todo.extend(g2)
                fill(1)
                turned_ok = turn_p(t, 4, lambda i: SC[:, pos_of(i), :], [[a, rv]])
                fill(1)
                b, last = weighted(t, 4, lambda i, k: VT[:, k, 1024 + i * P:1024 + (i + 1) * P], P, turned_ok)
                ob = O[:, t, :].rearrange("p (h d) -> p h d", h=4)
                o = dve.do(lambda ob=ob, b=b: nc.vector.tensor_copy(ob, bank[b][:, :].rearrange("p (h d) -> p h d", h=4)),
                           last, o_free[0])
                bank_free[b] = o
                mean, var, ok = norm_stats(ob, 4, P, 64, GN_EPS, False, o)
                for h in range(4):
                    oh = ob[:, h, :]
                    o = dve.do(lambda oh=oh, var=var, mean=mean, h=h: nc.vector.tensor_scalar(
                        oh, oh, mean[:, h:h + 1], var[:, h:h + 1], ALU.subtract, ALU.mult), ok)
            fill(9)
            o2 = turn_o([o, srg], lambda c: col("ret_gn_w_2", l, c), lambda c: col("ret_gn_b_2", l, c), lambda c: SRG[:, c, :])
            v_free[0] = [pe_last(), o2]
            for f in branch("w_branch_ret_2", l, False, o2, g2_done, m_done):
                f()
            xt_free[0] = pe_last()
            m = merged(m_done)
            x = mix_out("w_out_2", l, m, x_ok[0])
            h = normed(H, X, NORM_EPS, D, [*x, h_free[0]], True, parts=(MIX_STATS, 4))
            xt = turn_x(H, h, lambda c: col("mlp_norm_2", l, c))
            h_free[0] = pe_last()
            UT = [FA[:, i * 2048:(i + 1) * 2048].rearrange("p (k s) -> p k s", k=8) for i in range(2)]
            ru = [TMP[:, j * 512:(j + 1) * 512].rearrange("p (m s) -> p m s", m=2) for j in range(2)]
            rq = [TMP2[:, j * 512:(j + 1) * 512].rearrange("p (m s) -> p m s", m=2) for j in range(2)]
            r_free = [flat([rope_done[-1:], tmp_free])] * 2
            u_free = ot_free[0]
            for q in range(4):
                ud = []
                for j in range(4):
                    c = q * 1024 + j * 256
                    (w,), loaded = take(("w_mlp_up_2", (l,), 0, KD, c, c + 256))
                    b, v, last = features_major(w, 0, XT, [loaded], ready=xt)
                    release(last)
                    r_, s_ = ru[j % 2], rq[j % 2]
                    h_, l_ = (u[:, 2 * j:2 * j + 2, :] for u in UT)
                    a = bank_free[b] = act.do(lambda r_=r_, v=v: nc.scalar.activation(r_, v, ACT.Relu), last, *r_free[j % 2])
                    hh = act.do(lambda h_=h_, r_=r_: nc.scalar.activation(h_, r_, ACT.Square), a, u_free)
                    sq = pool.do(lambda r_=r_, s_=s_: nc.gpsimd.tensor_tensor(s_, r_, r_, ALU.mult), a, *r_free[j % 2])
                    ud.append(dve.do(lambda h_=h_, l_=l_, s_=s_: nc.vector.tensor_tensor(l_, s_, h_.bitcast(F32), ALU.subtract),
                                     sq, hh, u_free))
                    r_free[j % 2] = [ud[-1], hh]
                for j in range(4):
                    (w,), loaded = take(("w_mlp_down_2", (l,), q * 8 + 2 * j, 2, 0, D))
                    waits = flat([loaded, ud[j], sc_free[0]])
                    ends = q == 3 and j == 3
                    x = []
                    for n in range(2):
                        for t in range(T):
                            for k in range(2):
                                last = mm3(yv[:, t, n * 512:(n + 1) * 512], cut(UT, 2 * j + k, slice(t * P, (t + 1) * P)),
                                           cut(w, k, slice(n * 512, (n + 1) * 512)), q + j + k == 0, ends and k == 1, *waits)
                                waits = []
                            if ends:
                                x.append(add_y(t, n, last))
                    release(last)
                u_free = last
            xt_free[0] = ot_free[0] = last
            tmp_free[:] = [r_free[0], r_free[1]]
            rope_done.append(ud[-1])
            sc_free[0] = x[-1]
            a_free[0] = last
            x_ok[0] = x
            if l == DEPTH - 1:
                z = normed(H, X, NORM_EPS, D, [*x, h_free[0]], True, parts=(MIX_STATS, 2))
                for c in range(2):
                    s1 = spread(yv[:, 0, c * 512:(c + 1) * 512], "final_norm_2", None, c * 512, 512, sc_free[0])
                for t in range(T):
                    y = dve.do(lambda t=t: nc.vector.tensor_tensor(H[:, t, :], H[:, t, :], yv[:, 0, :], ALU.mult), *flat([s1, z]))
                    o = load((sp, act)[t], out[t], H[:, t, :], f"l_out{t}", y)
                    (sp, act)[t].do(lambda: None, o)

        for l in range(DEPTH):
            first_layer(l)
        c2_in = [load(pool, CST[:, C_N:C_N + C2_N], consts[P * (C_N + C1_N):].rearrange("(p n) -> p n", p=P), "l_cst2", x_ok)]
        for l in range(DEPTH):
            second_layer(l)
        assert not todo and at[-1][0] + at[-1][1] == WORDS, (at[-1], WORDS)
        if order is None:
            return taken
        for q in (pe, dve, act, pool, sp):
            q.number()
        block = ctx.enter_context(nc.Block())

        @block.sync
        def _(e):
            sp.emit()

        @block.tensor
        def _(e):
            pe.emit()

        @block.vector
        def _(e):
            dve.emit()

        @block.scalar
        def _(e):
            act.emit()

        @block.gpsimd
        def _(e):
            pool.emit()

def constants():
    c = {}
    c["ident"] = np.eye(P)
    q = np.arange(P)
    c["caus"] = np.where(q[None, :] <= q[:, None], 0.0, NEG)
    gamma = 1.0 - 2.0 ** (-5.0 - np.arange(4))
    at = np.arange(S, dtype=np.float64)[:, None]
    ret = np.concatenate([gamma ** at, gamma ** -at * 0.125], 1)
    c["ret"] = ret.reshape(T, P, 8).transpose(1, 0, 2).reshape(P, -1)

    def inv(dim, theta):
        return (np.float32(1.0) / (np.float32(theta) ** (np.arange(0, dim, 2, dtype=np.float32) / np.float32(dim)))).astype(np.float32)

    c["invf"] = np.broadcast_to(inv(16, 500000.0), (P, 8))
    for dim, theta in ((16, 500000.0), (32, 500000.0), (64, 10000.0)):
        ang = (np.arange(S, dtype=np.float32)[:, None] * inv(dim, theta)[None, :]).astype(np.float32).astype(np.float64)
        co, si = np.cos(ang), np.sin(ang)
        c[f"c{dim}"] = np.concatenate([co, co], 1).reshape(T, P, dim).transpose(1, 0, 2).reshape(P, -1)
        c[f"s{dim}"] = np.concatenate([-si, si], 1).reshape(T, P, dim).transpose(1, 0, 2).reshape(P, -1)
    c["iota8"] = np.broadcast_to(np.arange(8), (P, 8))
    c["nhalf"] = np.full((P, 8), -0.5)
    c["before"] = q[:, None] < q[None, :]
    c["iota"] = np.broadcast_to(np.arange(SLOTS), (P, SLOTS))
    c["one"] = np.ones((P, 1))
    return np.concatenate([np.concatenate([np.asarray(c[n], np.float32).reshape(P, m) for n, m in table], 1).reshape(-1)
                           for table in (C_TABLE, C1_TABLE, C2_TABLE)])


def kernel(**inputs):
    import numpy as _np
    import concourse.bacc as _bacc
    from concourse import mybir as _mybir
    from concourse.bass_utils import run_bass_kernel_spmd as _run

    a = {k: _np.asarray(v) for k, v in inputs.items()}
    arrays = {}
    arrays["consts"] = constants()
    arrays["pos"] = _np.ascontiguousarray(a["positions"].reshape(T, P).T)
    x = a["x"].reshape(S, D)
    arrays["x0"] = _np.ascontiguousarray(x.reshape(T, P, D).transpose(1, 0, 2))
    arrays["x0T"] = _np.ascontiguousarray(x.T.reshape(KD, P, S).transpose(1, 0, 2))
    p = a["p"].reshape(DEPTH, S, 256)
    arrays["pT"] = _np.ascontiguousarray(p.transpose(0, 2, 1).reshape(DEPTH, 2, P, S).transpose(0, 2, 1, 3))

    arrays["cols"] = _np.ascontiguousarray(_np.concatenate([a[n][l].reshape(m, P).T for n, l, m in COLS], 1))
    small = [_np.concatenate([a[n][l].reshape(-1) for n in SMALL] + [_np.zeros(D - 292, _np.float32)]) for l in range(DEPTH)]
    arrays["rows"] = _np.stack([small[l] if n == "small" else a[n] if l is None else a[n][l] for n, l in ROWS])
    arrays["wts"] = stream = _np.empty(WORDS, _np.float32)

    def program(order):
        nc = _bacc.Bacc("TRN2", target_bir_lowering=False, num_devices=1)
        args = {n: nc.dram_tensor(n, v.shape, _mybir.dt.from_np(v.dtype), kind="ExternalInput").ap() for n, v in arrays.items()}
        out = nc.dram_tensor("out", (T, P, D), _mybir.dt.float32, kind="ExternalOutput").ap()
        return nc, build(nc, out=out, order=order, **args)

    order = program(None)[1]
    nc = program(order)[0]
    at = 0
    for block in order:
        dst = stream[at:at + P * width(block)].reshape(P, -1)
        at += dst.size
        c = 0
        for name, idx, k0, kt, c0, c1 in block:
            w = a[name][idx].reshape(-1, P, a[name].shape[-1])[k0:k0 + kt, :, c0:c1]
            n = kt * (c1 - c0)
            dst[:, c:c + n].reshape(P, kt, c1 - c0)[:] = w.transpose(1, 0, 2)
            c += n
    r = _run(nc, [arrays], core_ids=[0])
    return r.results[0]["out"].reshape(1, S, D)
```
